# Optimizing a Trainium2 kernel written in Bass

```python
import math
import jax
import jax.numpy as jnp
from jax import lax
import numpy as np

D_MODEL = 1024
BATCH = 1
SEQ = 1024
DEPTH = 2
DEC_BATCH = 8
DEC_SEQ = 8
PAST_LEN = 1024
PAGE_SIZE = 128

RWKV_HEADS = 12
RWKV_HS = 64
W_RWKV = RWKV_HEADS * RWKV_HS
LORA_W = 64
LORA_A = 64
LORA_V = 32
LNX_EPS = 64e-5
SHIFT_FIRST = 3 * W_RWKV + LORA_W + LORA_A
SHIFT_REST = SHIFT_FIRST + LORA_V
DIFF_HEADS = 6
DIFF_HD = 64
W_DIFF = DIFF_HEADS * 2 * DIFF_HD
MEM_TOKENS = 256
MEM_HEADS = 4
MEM_HD = 64
W_MEM = MEM_HEADS * MEM_HD
MIX = W_RWKV + W_MEM
ROPE_THETA = 10000.0
Q_BLOCK = 128
NORM_EPS = 1e-6
NEG_INF = -1e30

kernel_name = "yoco_rwkv7_diffattn_mem_decoder_step"

def rms_norm(x, g, eps=NORM_EPS):
    xf = x.astype(jnp.float32)
    y = xf * lax.rsqrt(jnp.mean(xf * xf, axis=-1, keepdims=True) + eps)
    return (y * g.astype(jnp.float32)).astype(x.dtype)

def rope(x, pos):
    half = x.shape[-1] // 2
    inv = ROPE_THETA ** (-jnp.arange(half, dtype=jnp.float32) / half)
    ang = pos.astype(jnp.float32)[:, None] * inv[None, :]
    shape = (1, pos.shape[0]) + (1,) * (x.ndim - 3) + (half,)
    cos, sin = jnp.cos(ang).reshape(shape), jnp.sin(ang).reshape(shape)
    xf = x.astype(jnp.float32)
    x1, x2 = xf[..., :half], xf[..., half:]
    return jnp.concatenate([x1 * cos - x2 * sin, x2 * cos + x1 * sin], axis=-1).astype(x.dtype)

def wkv_scan(s0, r, decay, k, v, kk, a):
    def step(s, inp):
        r_t, w_t, k_t, v_t, kk_t, a_t = inp
        sa = jnp.einsum("bhij,bhj->bhi", s, -kk_t)
        s = (s * w_t[:, :, None, :] + sa[..., None] * (kk_t * a_t)[:, :, None, :]
             + v_t[..., None] * k_t[:, :, None, :])
        return s, jnp.einsum("bhij,bhj->bhi", s, r_t)
    xs = tuple(jnp.moveaxis(z, 1, 0) for z in (r, decay, k, v, kk, a))
    s, o = lax.scan(step, s0, xs)
    return s, jnp.moveaxis(o, 0, 1)

def mem_kv(mem, g, w_kv, k_g):
    bsz, m, _ = mem.shape
    k, v = jnp.split(rms_norm(mem, g) @ w_kv, [W_MEM], axis=-1)
    return (rms_norm(k.reshape(bsz, m, MEM_HEADS, MEM_HD), k_g),
            v.reshape(bsz, m, MEM_HEADS, MEM_HD))

def mem_attend(q, mem_k, mem_v, q_g):
    bsz, t, _ = q.shape
    qh = rms_norm(q.reshape(bsz, t, MEM_HEADS, MEM_HD), q_g)
    s = jnp.einsum("btnd,bmnd->bntm", qh, mem_k).astype(jnp.float32) * MEM_HD ** -0.5
    p = jax.nn.softmax(s, axis=-1)
    o = jnp.einsum("bntm,bmnd->btnd", p.astype(mem_v.dtype), mem_v)
    return o.reshape(bsz, t, W_MEM)

def diff_scores(q, k):
    return jnp.einsum("bqhcd,bkhcd->bhcqk", q, k).astype(jnp.float32) * DIFF_HD ** -0.5

def diff_weights(s, lam):
    p = jax.nn.softmax(s, axis=-1)
    return p[:, :, 0] - lam * p[:, :, 1]

def diff_attn_prompt(q, k, v, lam):
    bsz, t = q.shape[0], q.shape[1]
    kpos = jnp.arange(t)
    def block(i):
        q_b = lax.dynamic_slice_in_dim(q, i * Q_BLOCK, Q_BLOCK, axis=1)
        qpos = i * Q_BLOCK + jnp.arange(Q_BLOCK)
        s = jnp.where(qpos[:, None] >= kpos[None, :], diff_scores(q_b, k), NEG_INF)
        w = diff_weights(s, lam)
        return jnp.einsum("bhqk,bkhe->bqhe", w.astype(v.dtype), v)
    o = lax.map(block, jnp.arange(t // Q_BLOCK))
    return jnp.moveaxis(o, 0, 1).reshape(bsz, t, DIFF_HEADS, 2 * DIFF_HD)

def diff_attn_sample(q, k, v, lam, past_k, past_v):
    t = q.shape[1]
    n_past = past_k.shape[1]
    causal = jnp.arange(t)[:, None] >= jnp.arange(t)[None, :]
    s = jnp.concatenate([diff_scores(q, past_k),
                         jnp.where(causal, diff_scores(q, k), NEG_INF)], axis=-1)
    w = diff_weights(s, lam)
    return (jnp.einsum("bhqk,bkhe->bqhe", w[..., :n_past].astype(v.dtype), past_v)
            + jnp.einsum("bhqk,bkhe->bqhe", w[..., n_past:].astype(v.dtype), v))

def gather_pages(pool, page_table):
    rows = jnp.take(pool, page_table, axis=0)
    return rows.reshape((page_table.shape[0], page_table.shape[1] * pool.shape[1]) + pool.shape[2:])

def a_layer(h, prev_xn, s0, v_first, mem_k, mem_v, norm_g, w_in, mu, w0, w_up, a0, a_up,
            k_k, k_a, r_k, lnx_g, lnx_b, mq_g, w_out, v0=None, v_up=None):
    bsz, t, _ = h.shape
    f32 = jnp.float32
    xn = rms_norm(h, norm_g)
    proj = jnp.concatenate([prev_xn[:, None, :].astype(xn.dtype), xn], axis=1) @ w_in
    n_sh = mu.shape[0]
    cur = proj[:, 1:, :n_sh]
    mixed = cur + (proj[:, :-1, :n_sh] - cur) * mu
    mem_q, gate = jnp.split(proj[:, 1:, n_sh:], [W_MEM], axis=-1)
    r, k, v, wd, ad, vd = jnp.split(
        mixed, [W_RWKV, 2 * W_RWKV, 3 * W_RWKV, 3 * W_RWKV + LORA_W, SHIFT_FIRST], axis=-1)
    log_w = -jax.nn.softplus(-(w0 + jnp.tanh(wd) @ w_up).astype(f32)) - 0.5
    decay = jnp.exp(-jnp.exp(log_w))
    a = jax.nn.sigmoid((a0 + ad @ a_up).astype(f32))
    if v0 is None:
        v_first = v
    else:
        v = v + (v_first - v) * jax.nn.sigmoid(v0 + vd @ v_up)
    hd = lambda z: z.reshape(bsz, t, RWKV_HEADS, RWKV_HS).astype(f32)
    hp = lambda z: z.reshape(RWKV_HEADS, RWKV_HS).astype(f32)
    r, k, v, decay, a = hd(r), hd(k), hd(v), hd(decay), hd(a)
    kk = k * hp(k_k)
    kk = kk / jnp.maximum(jnp.sqrt(jnp.sum(kk * kk, axis=-1, keepdims=True)), 1e-12)
    k = k * (1.0 + (a - 1.0) * hp(k_a))
    s, o = wkv_scan(s0.astype(f32), r, decay, k, v, kk, a)
    mu_o = jnp.mean(o, axis=-1, keepdims=True)
    var_o = jnp.mean(jnp.square(o - mu_o), axis=-1, keepdims=True)
    o = (o - mu_o) * lax.rsqrt(var_o + LNX_EPS) * hp(lnx_g) + hp(lnx_b)
    o = o + jnp.sum(r * k * hp(r_k), axis=-1, keepdims=True) * v
    o = o.reshape(bsz, t, W_RWKV).astype(h.dtype)
    mo = mem_attend(mem_q, mem_k, mem_v, mq_g).astype(h.dtype)
    y = jnp.concatenate([o, mo], axis=-1) * jax.nn.silu(gate)
    return h + (y @ w_out).astype(h.dtype), xn[:, -1], s.astype(s0.dtype), v_first

def shared_kv(h, pos, g, w_kv, k_g):
    bsz, t, _ = h.shape
    k, v = jnp.split(rms_norm(h, g) @ w_kv, [W_DIFF], axis=-1)
    k = rope(rms_norm(k.reshape(bsz, t, DIFF_HEADS, 2, DIFF_HD), k_g), pos)
    return k, v.reshape(bsz, t, DIFF_HEADS, 2 * DIFF_HD)

def b_layer(h, pos, attend, mem_k, mem_v, norm_g, w_in, q_g, lam_v, lam_init, subln_g, mq_g, w_out):
    bsz, t, _ = h.shape
    xn = rms_norm(h, norm_g)
    q, mem_q, gate = jnp.split(xn @ w_in, [W_DIFF, W_DIFF + W_MEM], axis=-1)
    q = rope(rms_norm(q.reshape(bsz, t, DIFF_HEADS, 2, DIFF_HD), q_g), pos)
    lv = lam_v.astype(jnp.float32)
    lam = jnp.exp(jnp.sum(lv[0] * lv[1])) - jnp.exp(jnp.sum(lv[2] * lv[3])) + lam_init
    o = attend(q, lam)
    o = (rms_norm(o, subln_g) * (1.0 - lam_init)).reshape(bsz, t, W_DIFF).astype(h.dtype)
    mo = mem_attend(mem_q, mem_k, mem_v, mq_g).astype(h.dtype)
    y = jnp.concatenate([o, mo], axis=-1) * jax.nn.silu(gate)
    return h + (y @ w_out).astype(h.dtype)

def trunk(h, pos, mem_layers, shift0, wkv0, attend_fn, p):
    n_a = DEPTH // 2
    shifts, states = [], []
    v_first = None
    k_new = v_new = attend = None
    for l in range(DEPTH):
        mk, mv = mem_layers[l]
        if l < n_a:
            if l == 0:
                w_in, mu, v0, v_up = p["a_w_in_first"], p["a_mu_first"], None, None
            else:
                w_in, mu = p["a_w_in_rest"][l - 1], p["a_mu_rest"][l - 1]
                v0, v_up = p["a_v0"][l - 1], p["a_v_up"][l - 1]
            h, sh, st, v_first = a_layer(
                h, shift0[l], wkv0[l], v_first, mk, mv, p["norm_g"][l], w_in, mu,
                p["a_w0"][l], p["a_w_up"][l], p["a_a0"][l], p["a_a_up"][l], p["a_k_k"][l],
                p["a_k_a"][l], p["a_r_k"][l], p["a_lnx_g"][l], p["a_lnx_b"][l],
                p["mem_q_g"][l], p["w_out"][l], v0, v_up)
            shifts.append(sh)
            states.append(st)
            if l == n_a - 1:
                k_new, v_new = shared_kv(h, pos, p["kv_norm_g"], p["kv_w"], p["kv_k_g"])
                attend = lambda q, lam: attend_fn(q, k_new, v_new, lam)
        else:
            j = l - n_a
            lam_init = 0.8 - 0.6 * math.exp(-0.3 * l)
            h = b_layer(h, pos, attend, mk, mv, p["norm_g"][l], p["b_w_in"][j], p["b_q_g"][j],
                        p["b_lam"][j], lam_init, p["b_subln_g"][j], p["mem_q_g"][l], p["w_out"][l])
    return h, jnp.stack(shifts), jnp.stack(states), k_new, v_new

def setup_inputs(seed: int = 0) -> dict:
    key = jax.random.key(seed)
    ks = iter(jax.random.split(key, 64))
    f32 = jnp.float32
    def nrm(shape, scale):
        return jax.random.normal(next(ks), shape, f32) * scale
    def unif(shape, lo, hi):
        return jax.random.uniform(next(ks), shape, f32, lo, hi)
    def gain(shape):
        return 1.0 + nrm(shape, 0.02)
    n_a = DEPTH // 2
    n_b = DEPTH - n_a
    n_pages = PAST_LEN // PAGE_SIZE
    n_used = DEC_BATCH * n_pages
    n_pool = n_used + max(1, n_used // 4)
    c_first = SHIFT_FIRST + W_MEM + MIX
    c_rest = SHIFT_REST + W_MEM + MIX
    d_inv = D_MODEL ** -0.5
    return {
        "x_prompt": nrm((BATCH, SEQ, D_MODEL), 1.0),
        "x_sample": nrm((DEC_BATCH, DEC_SEQ, D_MODEL), 1.0),
        "mem_prompt": nrm((BATCH, MEM_TOKENS, D_MODEL), 1.0),
        "state_wkv": nrm((n_a, DEC_BATCH, RWKV_HEADS, RWKV_HS, RWKV_HS), 0.3),
        "state_shift": nrm((n_a, DEC_BATCH, D_MODEL), 1.0),
        "cache_k": nrm((n_pool, PAGE_SIZE, DIFF_HEADS, 2, DIFF_HD), 1.0),
        "cache_v": nrm((n_pool, PAGE_SIZE, DIFF_HEADS, 2 * DIFF_HD), 1.0),
        "cache_mem_k": nrm((DEPTH, DEC_BATCH, MEM_TOKENS, MEM_HEADS, MEM_HD), 1.0),
        "cache_mem_v": nrm((DEPTH, DEC_BATCH, MEM_TOKENS, MEM_HEADS, MEM_HD), 1.0),
        "page_table": jax.random.permutation(next(ks), n_pool)[:n_used].reshape(DEC_BATCH, n_pages).astype(jnp.int32),
        "norm_g": gain((DEPTH, D_MODEL)),
        "a_w_in_first": nrm((D_MODEL, c_first), d_inv),
        "a_mu_first": unif((SHIFT_FIRST,), 0.1, 0.9),
        "a_w_in_rest": nrm((n_a - 1, D_MODEL, c_rest), d_inv),
        "a_mu_rest": unif((n_a - 1, SHIFT_REST), 0.1, 0.9),
        "a_w0": unif((n_a, W_RWKV), -4.0, 0.0),
        "a_w_up": nrm((n_a, LORA_W, W_RWKV), 0.1),
        "a_a0": nrm((n_a, W_RWKV), 0.5),
        "a_a_up": nrm((n_a, LORA_A, W_RWKV), 0.5 * LORA_A ** -0.5),
        "a_v0": nrm((n_a - 1, W_RWKV), 0.5),
        "a_v_up": nrm((n_a - 1, LORA_V, W_RWKV), 0.5 * LORA_V ** -0.5),
        "a_k_k": 1.0 + nrm((n_a, W_RWKV), 0.1),
        "a_k_a": 1.0 + nrm((n_a, W_RWKV), 0.1),
        "a_r_k": nrm((n_a, W_RWKV), 0.1),
        "a_lnx_g": gain((n_a, W_RWKV)),
        "a_lnx_b": nrm((n_a, W_RWKV), 0.01),
        "kv_norm_g": gain((D_MODEL,)),
        "kv_w": nrm((D_MODEL, 2 * W_DIFF), d_inv),
        "kv_k_g": gain((DIFF_HD,)),
        "b_w_in": nrm((n_b, D_MODEL, W_DIFF + W_MEM + MIX), d_inv),
        "b_q_g": gain((n_b, DIFF_HD)),
        "b_lam": nrm((n_b, 4, DIFF_HD), 0.1),
        "b_subln_g": gain((n_b, 2 * DIFF_HD)),
        "mem_norm_g": gain((DEPTH, D_MODEL)),
        "mem_w_kv": nrm((DEPTH, D_MODEL, 2 * W_MEM), d_inv),
        "mem_k_g": gain((DEPTH, MEM_HD)),
        "mem_q_g": gain((DEPTH, MEM_HD)),
        "w_out": nrm((DEPTH, MIX, D_MODEL), MIX ** -0.5),
    }

def reference(x_prompt, x_sample, mem_prompt, state_wkv, state_shift, cache_k, cache_v,
              cache_mem_k, cache_mem_v, page_table, norm_g, a_w_in_first, a_mu_first,
              a_w_in_rest, a_mu_rest, a_w0, a_w_up, a_a0, a_a_up, a_v0, a_v_up, a_k_k, a_k_a,
              a_r_k, a_lnx_g, a_lnx_b, kv_norm_g, kv_w, kv_k_g, b_w_in, b_q_g, b_lam, b_subln_g,
              mem_norm_g, mem_w_kv, mem_k_g, mem_q_g, w_out):
    p = dict(norm_g=norm_g, a_w_in_first=a_w_in_first, a_mu_first=a_mu_first,
             a_w_in_rest=a_w_in_rest, a_mu_rest=a_mu_rest, a_w0=a_w0, a_w_up=a_w_up, a_a0=a_a0,
             a_a_up=a_a_up, a_v0=a_v0, a_v_up=a_v_up, a_k_k=a_k_k, a_k_a=a_k_a, a_r_k=a_r_k,
             a_lnx_g=a_lnx_g, a_lnx_b=a_lnx_b, kv_norm_g=kv_norm_g, kv_w=kv_w, kv_k_g=kv_k_g,
             b_w_in=b_w_in, b_q_g=b_q_g, b_lam=b_lam, b_subln_g=b_subln_g, mem_q_g=mem_q_g,
             w_out=w_out)
    n_a = DEPTH // 2
    bsz, seq, _ = x_prompt.shape
    dec_seq = x_sample.shape[1]
    past_len = page_table.shape[1] * cache_k.shape[1]

    mem_p = [mem_kv(mem_prompt, mem_norm_g[l], mem_w_kv[l], mem_k_g[l]) for l in range(DEPTH)]
    shift0_p = jnp.zeros((n_a, bsz, D_MODEL), x_prompt.dtype)
    wkv0_p = jnp.zeros((n_a, bsz, RWKV_HEADS, RWKV_HS, RWKV_HS), x_prompt.dtype)
    y_prompt, shift_p, wkv_p, k_p, v_p = trunk(
        x_prompt, jnp.arange(seq), mem_p, shift0_p, wkv0_p, diff_attn_prompt, p)
    mem_k_p = jnp.stack([m[0] for m in mem_p])
    mem_v_p = jnp.stack([m[1] for m in mem_p])

    past_k = gather_pages(cache_k, page_table)
    past_v = gather_pages(cache_v, page_table)
    mem_s = [(cache_mem_k[l], cache_mem_v[l]) for l in range(DEPTH)]
    attend_s = lambda q, k, v, lam: diff_attn_sample(q, k, v, lam, past_k, past_v)
    y_sample, shift_s, wkv_s, k_s, v_s = trunk(
        x_sample, past_len + jnp.arange(dec_seq), mem_s, state_shift, state_wkv, attend_s, p)

    return (y_prompt, y_sample, wkv_p, shift_p, k_p, v_p, mem_k_p, mem_v_p,
            wkv_s, shift_s, k_s, v_s)


_drawn_inputs = setup_inputs


def setup_inputs(seed=0):
    import zlib

    import numpy as np

    out = dict(_drawn_inputs(seed))
    spreads = {}
    factors = {'a_lnx_g': 5.555,
     'a_lnx_b': 8.0,
     'kv_norm_g': 2.732,
     'kv_k_g': 2.69,
     'b_q_g': 7.133,
     'b_subln_g': 8.0,
     'mem_norm_g': 2.815,
     'mem_k_g': 2.975,
     'mem_q_g': 8.0}
    for name, (base, spread) in spreads.items():
        noise = np.random.default_rng([zlib.crc32(name.encode()), seed]).standard_normal(out[name].shape)
        drawn = base * np.exp(spread * noise) if base else spread * noise
        out[name] = jnp.asarray(drawn.astype(out[name].dtype))
    for name, factor in factors.items():
        out[name] = (out[name] * factor).astype(out[name].dtype)
    return out
```

```python
import math
from contextlib import ExitStack

import numpy as np

import concourse.bass as bass
from concourse import mybir

F32 = mybir.dt.float32
I32 = mybir.dt.int32
ALU = mybir.AluOpType
ACT = mybir.ActivationFunctionType
X = mybir.AxisListType.X

P = 128
D = 1024
KC = D // P
SEQ = 1024
NT = SEQ // P
B = 8
TS = 8
NS = B * TS
TT = SEQ + NS
TX = TT + B
NTILE = NT + 1
HEADS = 12
HS = 64
PAIRS = HEADS // 2
NCH = 29
DH = 6
PAGES = 8
MEMT = 256
W_GATE = math.exp(-0.5)
EPS = 1e-6
LNX_EPS = 64e-5
NEG = -1e30
LAM_INIT = 0.8 - 0.6 * math.exp(-0.3)
LEVELS = [2, 4, 8, 16, 32, 64]
COLS = [(0, 512), (512, 1024), (1024, TX)]


def rows_of(n):
    return P if n < NT else NS


def make_constants():
    t = np.arange(P)
    parts, at = {}, 0
    out = []

    def put(name, a):
        nonlocal at
        a = np.asarray(a, np.float32).reshape(a.shape[0], -1)
        full = np.zeros((P, a.shape[1]), np.float32)
        full[:a.shape[0]] = a
        parts[name] = (at, a.shape[1])
        at += a.shape[1]
        out.append(full)

    s_, t_ = t[:, None], t[None, :]
    put("ident", np.eye(P))
    strict, incl = (s_ < t_), (s_ <= t_)
    put("headsum", s_ // HS == t_ // HS)
    early = at
    put("mask4", np.stack([strict, incl, strict, incl], 1))
    own = (s_[:NS] // TS == t_[:, :NS] // TS)
    put("mask4s", np.stack([strict[:NS, :NS] & own, incl[:NS, :NS] & own] * 2, 1))
    put("pair1", (s_ // 2 == t_ // 2) & (s_ < t_))
    for b in LEVELS:
        put(f"pair{b}", (s_ // b % 2 == 1) & (t_ // b == s_ // b - 1))
    put("headsel", s_ // HS == np.arange(2)[None, :])
    keep = np.ones(TT)
    keep[0:SEQ:P] = 0
    keep[SEQ::TS] = 0
    put("keep", np.broadcast_to(keep, (P, TT)))
    put("ownseq", (np.arange(NS)[:, None] // TS == np.arange(B)[None, :]))
    own_cols = (np.arange(B)[:, None] == (np.arange(NS) // TS)[None, :])
    put("owncols", np.broadcast_to(own_cols[None], (P, B, NS)))
    late = at
    put("causal", np.where(s_ >= t_, 0.0, NEG))
    j, i = np.arange(NS)[:, None, None], np.arange(TS)[None, None, :]
    b = np.arange(B)[None, :, None]
    put("newmask", np.where((j // TS == b) & (j % TS <= i), 0.0, NEG))
    half = 32
    inv = 10000.0 ** (-np.arange(half, dtype=np.float32) / half)
    pos = np.zeros((NTILE, P), np.float32)
    pos[:NT] = np.arange(SEQ).reshape(NT, P)
    pos[NT, :NS] = SEQ + np.arange(NS) % TS
    ang = (pos.T[:, :, None] * inv).astype(np.float32)
    put("cos", np.cos(ang))
    put("sin", np.sin(ang))
    every = np.concatenate(out, 1)
    cuts = [0, early, late, at]
    where = {}
    for name, (a, w) in parts.items():
        part = max(i for i in range(3) if cuts[i] <= a)
        where[name] = (part, a - cuts[part], w)
    return [every[:, cuts[i]:cuts[i + 1]] for i in range(3)], where


_CONST, _AT = make_constants()

_VEC = {}
_n = 0
for _name, _w in (("mu", 19), ("w0", 6), ("a0", 6), ("k_k", 6), ("k_a", 6), ("r_k", 6), ("mq0", 1), ("mq1", 1),
                  ("memg0", 8), ("memg1", 8), ("kvg", 8), ("bg", 8), ("subc", 1)):
    _VEC[_name] = (_n, _w)
    _n += _w
NVEC = _n
_ROW = {}
_n = 0
for _name, _w in (("lnx_g", 768), ("lnx_b", 768), ("k_g", 64), ("q_g", 64), ("subln", 128), ("lam", 256),
                  ("memk0", 64), ("memk1", 64)):
    _ROW[_name] = (_n if _n < 1536 else _n - 1536, _w)
    _n += _w
NROW = 1536
NROW2 = _n - NROW


class Chain:

    def __init__(self, eng, sem):
        self.eng, self.sem, self.n = eng, sem, 0

    def __call__(self, ins):
        self.n += 1
        ins.then_inc(self.sem, 1)
        self.eng.wait_ge(self.sem, self.n)


STORE_SIGNALS = {}
STORES = ("norm0_shift_stored rwkv_stored rwkv_y_stored memkv_stored out0_stored kvq_k_stored kvq_v_stored "
          "out1_stored").split()


class Stage:

    def __init__(self, nc, name):
        self.nc, self.name = nc, name

    def __enter__(self):
        self.ctx = ExitStack()
        self.signals = []
        return self

    def __exit__(self, *a):
        self.ctx.__exit__(*a)
        if a[0] is None:
            self.nc.clear_and_free_semaphores(self.signals)
            self.nc.all_engine_barrier()

    def sb(self, name, shape, dt=F32):
        return self.ctx.enter_context(self.nc.sbuf_tensor(f"{self.name}_{name}", shape, dt))

    def sem(self, name):
        if "stored" in name:
            return STORE_SIGNALS[f"{self.name}_{name}"]
        self.signals.append(self.nc.alloc_semaphore(f"{self.name}_{name}"))
        return self.signals[-1]

    def sems(self, names):
        return [self.sem(x) for x in names.split()]

    def block(self):
        return self.ctx.enter_context(self.nc.Block())


def bcast(ap, shape):
    return ap.broadcast_to(shape)


def load_tensors(nc, name, pairs, fills=()):
    with Stage(nc, name) as st:
        loaded, filled = st.sems("loaded filled")
        block = st.block()

        @block.sync
        def _(sp):
            for dst, src in pairs:
                sp.dma_start(dst, src).then_inc(loaded, 16)
            sp.wait_ge(loaded, 16 * len(pairs))

        if fills:
            @block.vector
            def _(dve):
                for dst, value in fills:
                    nc.vector.memset(dst, value).then_inc(filled, 1)


def norm_and_turn(nc, name, x_sb, xT, bank, ident, gain, state_shift=None, shifts=None, source=None):
    with Stage(nc, name) as st:
        sq = st.sb("sq", [P, 2, D])
        scaled = st.sb("scaled", [P, 2, D]) if gain is None else None
        ss = st.sb("ss", [P, NTILE])
        rstd = st.sb("rstd", [P, NTILE])
        grow = st.sb("grow", [P, D]) if gain is not None else None
        x_loaded = [st.sem(f"x_loaded{n}") for n in range(NTILE)]
        (ss_clear, rstd_ready, xn_ready, turned, act_out, dve_out, act_chain, g_loaded) = st.sems(
            "ss_clear rstd_ready xn_ready turned act_out dve_out act_chain g_loaded")
        shift_stored = st.sem("shift_stored") if shifts is not None else None
        block = st.block()
        last = NS + (B if state_shift is not None else 0)

        @block.sync
        def _(sp):
            if source is not None:
                x_prompt, x_sample = source
                for n in range(NT):
                    sp.dma_start(x_sb[:, n, :], x_prompt[n * P:(n + 1) * P, :]).then_inc(x_loaded[n], 16)
                sp.dma_start(x_sb[0:NS, NT, :], x_sample).then_inc(x_loaded[NT], 16)
                sp.dma_start(x_sb[NS:last, NT, :], state_shift).then_inc(x_loaded[NT], 16)
                sp.dma_start(grow[:, :], gain.partition_broadcast(P)).then_inc(g_loaded, 16)
                shift_p, shift_s = shifts
                sp.wait_ge(xn_ready, NTILE)
                sp.dma_start(shift_p, x_sb[P - 1:P, NT - 1, :]).then_inc(shift_stored, 16)
                for b in range(B):
                    sp.dma_start(shift_s[b:b + 1, :], x_sb[b * TS + TS - 1:b * TS + TS, NT, :]).then_inc(shift_stored, 16)
                sp.wait_ge(shift_stored, 16 * (B + 1))

        @block.scalar
        def _(act):
            link = Chain(act, act_chain)
            act.wait_ge(ss_clear, 1)
            for n in range(NTILE):
                r = rows_of(n)
                if source is not None:
                    act.wait_ge(x_loaded[n], 16 if n < NT else 32)
                link(nc.scalar.activation(sq[0:r, n % 2, :], x_sb[0:r, n, :], ACT.Square, accum_out=ss[0:r, n:n + 1]))
            link(nc.scalar.activation(ss[:, :], ss[:, :], ACT.Ln, scale=1.0 / D, bias=eps_tile(nc)[:, 0:1]))
            nc.scalar.activation(rstd[:, :], ss[:, :], ACT.Exp, scale=-0.5).then_inc(rstd_ready, 1)
            for n in range(NTILE):
                act.wait_ge(turned, 2 * n + 1)
                c = last if n == NT else P
                nc.scalar.copy(xT[:, 0:4, n * P:n * P + c],
                               bank[:, (2 * n) % 8, :].rearrange("p (k t) -> p k t", k=4)[:, :, 0:c]).then_inc(act_out, 1)

        @block.vector
        def _(dve):
            def evac(n):
                dve.wait_ge(turned, 2 * n + 2)
                c = last if n == NT else P
                nc.vector.tensor_copy(xT[:, 4:8, n * P:n * P + c],
                                      bank[:, (2 * n + 1) % 8, :].rearrange("p (k t) -> p k t", k=4)[:, :, 0:c]
                                      ).then_inc(dve_out, 1)

            nc.vector.memset(ss[:, :], 1.0).then_inc(ss_clear, 1)
            dve.wait_ge(rstd_ready, 1)
            if gain is not None:
                dve.wait_ge(g_loaded, 16)
            for n in range(NTILE):
                r = rows_of(n)
                if gain is not None:
                    if source is not None:
                        dve.wait_ge(x_loaded[n], 16 if n < NT else 32)
                    nc.vector.scalar_tensor_tensor(out=x_sb[0:r, n, :], in0=x_sb[0:r, n, :], scalar=rstd[0:r, n:n + 1],
                                                   in1=grow[0:r, :], op0=ALU.mult, op1=ALU.mult).then_inc(xn_ready, 1)
                else:
                    if n >= 2:
                        dve.wait_ge(turned, 2 * n - 2)
                    nc.vector.tensor_scalar(scaled[0:r, n % 2, :], x_sb[0:r, n, :], rstd[0:r, n:n + 1], None,
                                            ALU.mult).then_inc(xn_ready, 1)
                if n >= 1:
                    evac(n - 1)
            evac(NTILE - 1)

        @block.tensor
        def _(pe):
            for n in range(NTILE):
                pe.wait_ge(xn_ready, n + 1)
                r = last if n == NT else P
                for half in range(2):
                    j = 2 * n + half
                    if n >= 4:
                        pe.wait_ge(dve_out if half else act_out, n - 3)
                    for k in range(4):
                        kk = 4 * half + k
                        src = x_sb[0:r, n, kk * P:(kk + 1) * P] if gain is not None else \
                            scaled[0:r, n % 2, kk * P:(kk + 1) * P]
                        mm = pe.transpose(bank[:, j % 8, k * P:k * P + r], src, ident[0:r, 0:r])
                    mm.then_inc(turned, 1)


_EPS = {}


def eps_tile(nc):
    return _EPS["tile"]


def memory_keys(nc, mem, w_kv, vecs, rows, ident, bank, mkT, mv, out_k, out_v):
    with Stage(nc, "memkv") as st:
        x = st.sb("x", [P, 2, D])
        sq = st.sb("sq", [P, D])
        ss = st.sb("ss", [P, 2])
        rstd = st.sb("rstd", [P, 2])
        xT = st.sb("xT", [P, KC, MEMT])
        xg = st.sb("xg", [P, 2, KC, MEMT])
        w = st.sb("w", [P, 2, KC, 512])
        kss = st.sb("kss", [P, 16])
        krstd = st.sb("krstd", [P, 16])
        kn = st.sb("kn", [P, 4, MEMT])
        x_loaded, = st.sems("x_loaded")
        w_loaded = [st.sem(f"w_loaded{layer}") for layer in range(2)]
        (rstd_ready, xh_ready, turned, xT_ready, xg_ready, kv_ready, sq_ready, kss_ready, krstd_ready, kn_ready,
         v_ready, kn_turned, act_chain, dve_chain, stored) = st.sems(
            "rstd_ready xh_ready turned xT_ready xg_ready kv_ready sq_ready kss_ready krstd_ready kn_ready v_ready "
            "kn_turned act_chain dve_chain stored")
        block = st.block()

        @block.sync
        def _(sp):
            for n in range(2):
                sp.dma_start(x[:, n, :], mem[n * P:(n + 1) * P, :]).then_inc(x_loaded, 16)
            for layer in range(2):
                sp.dma_start(w[:, layer, :, :].rearrange("p k c -> p (k c)"), w_kv[layer]).then_inc(w_loaded[layer], 16)
            for j in range(4):
                layer, n = j // 2, j % 2
                sp.wait_ge(v_ready, j + 1)
                sp.dma_start(out_v[layer, n * P:(n + 1) * P, :], mv[:, layer, n, :]).then_inc(stored, 16)
            for j in range(4):
                layer, n = j // 2, j % 2
                sp.wait_ge(kn_ready, j + 1)
                sp.dma_start(out_k[layer, n * P:(n + 1) * P, :], kn[:, j, :]).then_inc(stored, 16)
            sp.wait_ge(stored, 16 * 8)

        @block.scalar
        def _(act):
            link = Chain(act, act_chain)
            act.wait_ge(x_loaded, 32)
            for n in range(2):
                link(nc.scalar.activation(sq[:, :], x[:, n, :], ACT.Square, accum_out=ss[:, n:n + 1]))
            link(nc.scalar.activation(ss[:, :], ss[:, :], ACT.Ln, scale=1.0 / D, bias=eps_tile(nc)[:, 0:1]))
            nc.scalar.activation(rstd[:, :], ss[:, :], ACT.Exp, scale=-0.5).then_inc(rstd_ready, 1)
            for j in range(4):
                act.wait_ge(turned, j + 1)
                n, half = j // 2, j % 2
                nc.scalar.copy(xT[:, 4 * half:4 * half + 4, n * P:(n + 1) * P],
                               bank[:, j, :].rearrange("p (k t) -> p k t", k=4)).then_inc(xT_ready, 1)
            for j in range(4):
                act.wait_ge(kv_ready, j + 1)
                if j >= 1:
                    act.wait_ge(kss_ready, j)
                nc.scalar.activation(sq[:, 0:MEMT], bank[:, 4 + j, 0:MEMT], ACT.Square).then_inc(sq_ready, 1)
            act.wait_ge(kss_ready, 4)
            link(nc.scalar.activation(krstd[:, :], kss[:, :], ACT.Ln, scale=1.0 / HS, bias=eps_tile(nc)[:, 0:1]))
            nc.scalar.activation(krstd[:, :], krstd[:, :], ACT.Exp, scale=-0.5).then_inc(krstd_ready, 1)
            for j in range(4):
                act.wait_ge(kn_turned, j + 1)
                layer, n = j // 2, j % 2
                link(nc.scalar.copy(mkT[:, layer, :, n * P:(n + 1) * P],
                                    bank[:, j, 0:MEMT].rearrange("p (c t) -> p c t", c=2)))

        @block.vector
        def _(dve):
            link = Chain(dve, dve_chain)
            dve.wait_ge(rstd_ready, 1)
            for n in range(2):
                nc.vector.tensor_scalar(x[:, n, :], x[:, n, :], rstd[:, n:n + 1], None, ALU.mult).then_inc(xh_ready, 1)
            dve.wait_ge(xT_ready, 4)
            for layer in range(2):
                g = vec(vecs, f"memg{layer}")
                nc.vector.tensor_tensor(xg[:, layer, :, :], xT[:, :, :], bcast(g.unsqueeze(2), [P, KC, MEMT]),
                                        ALU.mult).then_inc(xg_ready, 1)
            for j in range(4):
                layer, n = j // 2, j % 2
                dve.wait_ge(sq_ready, j + 1)
                nc.vector.tensor_copy(mv[:, layer, n, :], bank[:, 4 + j, MEMT:2 * MEMT]).then_inc(v_ready, 1)
                nc.vector.tensor_reduce(kss[:, 4 * j:4 * j + 4], sq[:, 0:MEMT].rearrange("p (h d) -> p h d", h=4), X,
                                        ALU.add).then_inc(kss_ready, 1)
            dve.wait_ge(krstd_ready, 1)
            for j in range(4):
                kv = kn[:, j, :].rearrange("p (h d) -> p h d", h=4)
                link(nc.vector.tensor_tensor(kv, bank[:, 4 + j, 0:MEMT].rearrange("p (h d) -> p h d", h=4),
                                             bcast(krstd[:, 4 * j:4 * j + 4].unsqueeze(2), [P, 4, HS]), ALU.mult))
                nc.vector.tensor_tensor(kv, kv, bcast(row(rows, f"memk{j // 2}").unsqueeze(1), [P, 4, HS]),
                                        ALU.mult).then_inc(kn_ready, 1)

        @block.tensor
        def _(pe):
            for j in range(4):
                n, half = j // 2, j % 2
                pe.wait_ge(xh_ready, n + 1)
                for k in range(4):
                    kk = 4 * half + k
                    mm = pe.transpose(bank[:, j, k * P:(k + 1) * P], x[:, n, kk * P:(kk + 1) * P], ident[:, :])
                mm.then_inc(turned, 1)
            for j in range(4):
                layer, n = j // 2, j % 2
                pe.wait_ge(xg_ready, layer + 1)
                pe.wait_ge(w_loaded[layer], 16)
                for k in range(KC):
                    mm = pe.matmul(bank[:, 4 + j, :], xg[:, layer, k, n * P:(n + 1) * P], w[:, layer, k, :],
                                   start=(k == 0), stop=(k == KC - 1))
                mm.then_inc(kv_ready, 1)
            for j in range(4):
                pe.wait_ge(kn_ready, j + 1)
                for c in range(2):
                    mm = pe.transpose(bank[:, j, c * P:(c + 1) * P], kn[:, j, c * P:(c + 1) * P], ident[:, :])
                mm.then_inc(kn_turned, 1)


def vec(vecs, name, i=None):
    at, w = _VEC[name]
    return vecs[:, at:at + w] if i is None else vecs[:, at + i:at + i + 1]


def row(rows, name, a=0, b=None):
    at, w = _ROW[name]
    return rows[:, at + a:at + (w if b is None else b)]


def const_view(const, name):
    part, at, w = _AT[name]
    return const[part][:, at:at + w]


def project(pe, wide, base, w, xT, width=TX, k_outer=False):
    for a, b in COLS:
        b = min(b, width)
        for k in range(KC):
            mm = pe.matmul(wide[:, base + a:base + b], w[:, k, :], xT[:, k, a:b], start=(k == 0), stop=(k == KC - 1))
    return mm


def mix_scaled(nc, ps, mu, prev, prev_s):
    nc.scalar.activation(prev[:, 1:SEQ + 1], ps[:, 0:SEQ], ACT.Copy, scale=mu)
    nc.scalar.activation(prev_s[:, :, 1:TS + 1], ps[:, SEQ:TT].rearrange("p (b t) -> p b t", b=B), ACT.Copy, scale=mu)
    return nc.scalar.activation(prev_s[:, :, 0], ps[:, TT:TX], ACT.Copy, scale=mu)


def mix_rest(nc, out, ps, omu, prev, prev_s):
    nc.vector.scalar_tensor_tensor(out=out[:, 0:SEQ], in0=ps[:, 0:SEQ], scalar=omu, in1=prev[:, 0:SEQ],
                                   op0=ALU.mult, op1=ALU.add)
    return nc.vector.scalar_tensor_tensor(out=out[:, SEQ:TT].rearrange("p (b t) -> p b t", b=B),
                                          in0=ps[:, SEQ:TT].rearrange("p (b t) -> p b t", b=B), scalar=omu,
                                          in1=prev_s[:, :, 0:TS], op0=ALU.mult, op1=ALU.add)


def lora_inputs(nc, w_in, w_up_d, a_up_d, vecs, omu, xT, wide, lora, up):
    with Stage(nc, "lora") as st:
        w = st.sb("w", [P, KC, P])
        prev = st.sb("prev", [P, SEQ + 1])
        prev_s = st.sb("prev_s", [P, B, TS + 1])
        loaded, up_loaded, projected, scaled, mixed, dve_chain, act_chain = st.sems(
            "loaded up_loaded projected scaled mixed dve_chain act_chain")
        block = st.block()

        @block.sync
        def _(sp):
            sp.dma_start(w[:, :, :].rearrange("p k c -> p (k c)"), w_in[18]).then_inc(loaded, 16)
            sp.dma_start(up[0:HS, :], w_up_d).then_inc(up_loaded, 16)
            sp.dma_start(up[HS:P, :], a_up_d).then_inc(up_loaded, 16)
            sp.wait_ge(up_loaded, 32)

        @block.tensor
        def _(pe):
            pe.wait_ge(loaded, 16)
            project(pe, wide, 0, w, xT).then_inc(projected, 1)

        @block.scalar
        def _(act):
            act.wait_ge(projected, 1)
            mix_scaled(nc, wide, vec(vecs, "mu", 18), prev, prev_s).then_inc(scaled, 1)
            act.wait_ge(mixed, 1)
            Chain(act, act_chain)(nc.scalar.activation(lora[0:HS, :], lora[0:HS, :], ACT.Tanh))

        @block.vector
        def _(dve):
            link = Chain(dve, dve_chain)
            link(nc.vector.memset(prev[:, 0:1], 0.0))
            link(nc.vector.tensor_scalar(omu[:, :], vec(vecs, "mu"), -1.0, 1.0, ALU.mult, ALU.add))
            dve.wait_ge(scaled, 1)
            mix_rest(nc, lora, wide, omu[:, 18:19], prev, prev_s).then_inc(mixed, 1)


UNITS = 2 * NT
GROUPS = UNITS // 4
STEPS = [(lev, g) for lev in range(len(LEVELS)) for g in range(GROUPS + 1) if g < GROUPS or LEVELS[lev] < TS]


def rwkv_pairs(nc, w_in, state_d, new_state_p, new_state_s, const, vecs, rows, omu, xT, wide, bank, lora, up, y_d):
    ident = const_view(const, "ident")
    with Stage(nc, "rwkv") as st:
        w = st.sb("w", [P, 2, KC, P])
        prev_s = st.sb("prev_s", [P, B, TS + 1])
        turns = [[st.sb(f"turn{i}{j}", [P, NTILE * P if j < 2 else TT]) for j in range(3)] for i in range(2)]
        aT = st.sb("aT", [P, TT])
        gT = st.sb("gT", [P, TT])
        sig_pr = st.sb("sig_pr", [P, TT])
        dec_mm = st.sb("dec_mm", [P, 5, 4, P])
        be_dd = st.sb("be_dd", [P, 5, 4, P])
        arT = st.sb("arT", [P, NTILE, 2, P])
        tok = st.sb("tok", [P, 3, NTILE, P])
        am = st.sb("am", [P, UNITS, 4, P])
        ams = st.sb("ams", [NS, 2, 4, NS])
        ee = st.sb("ee", [P, GROUPS + 1, 4, P])
        stat = st.sb("stat", [P, 4, 2 * NTILE])
        xscale = st.sb("xscale", [P, NT])
        pm = st.sb("pm", [P, NT])
        hv = st.sb("hv", [P, 3, PAIRS])
        s0 = st.sb("s0", [P, 2, B, P])
        sig = prT = sig_pr

        def krv(p):
            return [t[:, 0:TT] for t in turns[p % 2]]

        def kk_cum_dec(p):
            return [t[:, 0:TT] for t in turns[1 - p % 2]]

        def tiled(t):
            return t[:, :].rearrange("p (n c) -> p n c", n=NTILE)

        def small(p):
            v = turns[p % 2][2]
            return [v[:, i * P:(i + 1) * P] for i in range(4)] + [v[:, 4 * P:6 * P].rearrange("p (a i) -> p a i", a=2)]

        flat_mm = dec_mm[:, :, :, :].rearrange("p a b c -> p (a b c)")
        flat_dd = be_dd[:, :, :, :].rearrange("p a b c -> p (a b c)")
        dprevT, dinvT = flat_mm[:, 0:TT], flat_mm[:, TT:2 * TT]
        mm_, dd = dec_mm, be_dd
        sq_o = flat_mm[:, 0:NTILE * P]
        masked = flat_mm[:, 0:2 * B * NS].rearrange("p (c b t) -> p c b t", c=2, b=B)
        out_s = flat_mm[:, NTILE * P:NTILE * P + B * P].rearrange("p (b c) -> p b c", b=B)
        beT, kaT = flat_dd[:, 0:TT], flat_dd[:, TT:2 * TT]
        prev = flat_dd[:, TT:TT + SEQ + 1]
        expd = flat_dd[0:NS, 0:2 * B * P].rearrange("p (c b i) -> p c b i", c=2, b=B)
        w_loaded = [st.sem(f"w_loaded{i}") for i in range(2)]
        (s0_loaded, s0_zeroed, hv_ready, wide_ready, prev_ready, prev_used, th_ready, th_used, sq_ready,
         kk_max, rn_ready, cc_ready, dec_ready, prep_ready, tok_turned, tok_ready, am_mm, am_ready, e0_ready,
         d0_turned, d0_ready, m_mm, m_ready, dm_mm, d_ready, e_turned, e_ready, x_ready, r_mm, r_ready, sa_mm,
         sa_ready, y_mm, o_mm, o_ready, s0_turned, s0_ready, masked_ready, sample_r_ready, sample_sa_ready, ys_mm, ys_ready, st_turned,
         st_ready, stored, var_ready, rs_ready, on_ready, y_turned, y_done, gate_read, bonus_done, y_stored, dve_chain,
         act_chain, pool_chain) = st.sems(
            "s0_loaded s0_zeroed hv_ready wide_ready prev_ready prev_used th_ready th_used sq_ready kk_max "
            "rn_ready cc_ready dec_ready prep_ready tok_turned tok_ready am_mm am_ready e0_ready d0_turned d0_ready "
            "m_mm m_ready dm_mm d_ready e_turned e_ready x_ready r_mm r_ready sa_mm sa_ready y_mm o_mm o_ready "
            "s0_turned s0_ready masked_ready sample_r_ready sample_sa_ready ys_mm ys_ready st_turned st_ready stored var_ready rs_ready "
            "on_ready y_turned y_done gate_read bonus_done y_stored dve_chain act_chain pool_chain")
        block = st.block()

        NG = GROUPS + 1
        NLEV = len(STEPS)
        G = 5 * 512
        LOADS = [(6, 0), (0, 2), (12, 4), (21, 6)]
        WJ = 8
        PARTS = 3 * KC
        FILL = {}
        for at, first, count in ((0, 0, PARTS), (10, PARTS, 3), (12, PARTS + 3, PARTS), (22, 2 * PARTS + 3, 3)):
            for i in range(0, count, 3):
                FILL[divmod(at + i // 3, 3)] = range(first + i, first + i + 3)

        def used(g):
            return (P, P, 4) if g < GROUPS else (NS, NS, 2)

        def amat(g, i, kind, hh=None):
            if g < GROUPS:
                return am[:, 4 * g + i, kind, :]
            return ams[:, i, kind, :]

        @block.sync
        def _(sp):
            for p in range(PAIRS):
                for i, (chunk, wide_job) in enumerate(LOADS):
                    if 4 * p + i >= 2:
                        q, j = divmod(4 * p + i - 2, 4)
                        sp.wait_ge(wide_ready, WJ * q + LOADS[j][1] + 1)
                    sp.dma_start(w[:, i % 2, :, :].rearrange("p k c -> p (k c)"), w_in[chunk + p]).then_inc(w_loaded[i % 2], 16)
                if p == 0:
                    sp.wait_ge(s0_zeroed, 1)
                else:
                    sp.wait_ge(s0_turned, p)
                for hh in range(2):
                    sp.dma_start(s0[hh * HS:(hh + 1) * HS, 0, :, hh * HS:(hh + 1) * HS],
                                 state_d[:, 2 * p + hh, :, :].rearrange("b i j -> i b j")).then_inc(s0_loaded, 16)

        @block.gpsimd
        def _(pool):
            for p in range(PAIRS):
                pool.wait_ge(st_ready, p + 1)
                out_p = small(p)[3]
                for hh in range(2):
                    d = slice(hh * HS, (hh + 1) * HS)
                    pool.dma_start(new_state_s[:, 2 * p + hh, :, :].rearrange("b i j -> i b j"), out_s[d, :, d]).then_inc(stored, 16)
                    pool.dma_start(new_state_p[2 * p + hh, :, :], out_p[d, d]).then_inc(stored, 16)
                pool.wait_ge(y_done, p + 1)
                pool.dma_start(y_d[:, p, :], gT[:, :]).then_inc(y_stored, 16)
            pool.wait_ge(stored, 16 * 4 * PAIRS)
            pool.wait_ge(y_stored, 16 * PAIRS)

        @block.tensor
        def _(pe):
            def product(q, load, i):
                if i == 0:
                    pe.wait_ge(w_loaded[load % 2], 16 * (2 * q + load // 2 + 1))
                (a, b), k = COLS[i // KC], i % KC
                mm = pe.matmul(wide[:, G + a:G + b], w[:, load % 2, k, :], xT[:, k, a:b], start=(k == 0), stop=(k == KC - 1))
                if i == PARTS - 1:
                    mm.then_inc(wide_ready, 1)

            def low_rank(q, lo, i):
                a, b = COLS[i][0], min(COLS[i][1], TT)
                mm = pe.matmul(wide[:, G + a:G + b], up[lo:lo + HS, q * P:(q + 1) * P], lora[lo:lo + HS, a:b],
                               start=True, stop=True)
                if i == 2:
                    mm.then_inc(wide_ready, 1)

            def projection_part(q, i):
                if i < PARTS:
                    if i == 0 and q >= 1:
                        pe.wait_ge(gate_read, q)
                    product(q, 0, i)
                elif i < PARTS + 3:
                    if i == PARTS:
                        pe.wait_ge(prev_used, 3 * q + 1)
                    low_rank(q, 0, i - PARTS)
                elif i < 2 * PARTS + 3:
                    if i == PARTS + 3:
                        pe.wait_ge(th_ready, 3 * q + 1)
                    product(q, 1, i - PARTS - 3)
                elif i < 2 * PARTS + 6:
                    if i == 2 * PARTS + 3:
                        pe.wait_ge(prev_used, 3 * q + 2)
                    low_rank(q, HS, i - 2 * PARTS - 3)
                else:
                    if i == 2 * PARTS + 6:
                        pe.wait_ge(th_ready, 3 * q + 2)
                        if q >= 1:
                            pe.wait_ge(st_ready, q)
                    product(q, 2, i - 2 * PARTS - 6)

            for p in range(PAIRS):
                if p == 0:
                    for i in range(3 * PARTS + 6):
                        projection_part(0, i)
                kT, rT, vT = krv(p)
                kkT = kk_cum_dec(p)[0]
                r_sb, sa_sb, _, _, xs = small(p)
                o_all = tiled(turns[p % 2][1])
                if p >= 1:
                    pe.wait_ge(y_done, p)
                pe.wait_ge(sq_ready, p + 1)
                for a, b in COLS:
                    b = min(b, TT)
                    mm = pe.matmul(wide[:, a:b], const_view(const, "headsum"), kkT[:, a:b], start=True, stop=True)
                mm.then_inc(wide_ready, 1)
                pe.wait_ge(prev_used, 3 * p + 3)
                for i in range(PARTS):
                    product(p, 3, i)
                pe.wait_ge(prep_ready, p + 1)
                for n in range(NTILE):
                    r = rows_of(n)
                    mm = pe.matmul(bank[0:r, 3, 2 * n:2 * n + 2], prT[:, n * P:n * P + r],
                                   const_view(const, "headsel"), start=True, stop=True)
                mm.then_inc(wide_ready, 1)

                pe.wait_ge(gate_read, p + 1)
                for q in range(7):
                    if q >= 2:
                        pe.wait_ge(tok_ready, 7 * p + q - 1)
                    for i in range(4 if q < 6 else 3):
                        which, n = (q // 2, 4 * (q % 2) + i) if q < 6 else (i, NT)
                        r = rows_of(n)
                        mm = pe.transpose(bank[0:r, 6 + q % 2, i * P:(i + 1) * P], (vT, beT, kaT)[which][:, n * P:n * P + r],
                                          ident[:, :])
                    mm.then_inc(tok_turned, 1)
                pe.wait_ge(tok_ready, 7 * (p + 1))

                for u in range(UNITS + 2):
                    if u == 0:
                        pe.wait_ge(kk_max, p + 1)
                        pe.wait_ge(bonus_done, p + 1)
                    elif u >= 8:
                        pe.wait_ge(am_ready, (UNITS + 2) * p + u - 7)
                    n, lo = (u // 2, u % 2 * HS)
                    r = rows_of(n)
                    for i, src in enumerate((beT, kaT)):
                        mm = pe.matmul(bank[0:r, u % 8, 2 * r * i:2 * r * i + 2 * r].rearrange("s (a t) -> s a t", a=2),
                                       src[lo:lo + HS, n * P:n * P + r], arT[lo:lo + HS, n, :, 0:r], start=True, stop=True)
                    mm.then_inc(am_mm, 1)
                pe.wait_ge(am_ready, (UNITS + 2) * (p + 1))

                for g in range(NG):
                    r, c, un = used(g)
                    pe.wait_ge(e0_ready, NG * p + g + 1)
                    for i in range(un):
                        mm = pe.transpose(bank[0:r, g, i * P:i * P + c], ee[0:r, g, i, 0:c], ident[0:r, 0:r])
                    mm.then_inc(d0_turned, 1)

                for lev in range(len(LEVELS)):
                    steps = [(k, g) for k, (lv, g) in enumerate(STEPS) if lv == lev]
                    for k, g in steps:
                        r, c, un = used(g)
                        if lev == 0:
                            pe.wait_ge(d0_ready, NG * p + g + 1)
                        else:
                            pe.wait_ge(d_ready, NLEV * p + prior(k, g) + 1)
                        for i in range(un):
                            mm = pe.matmul(bank[0:r, mbank(g), i * P:i * P + c], amat(g, i, 0), dd[0:r, g, i, 0:c],
                                           start=True, stop=True)
                        mm.then_inc(m_mm, 1)
                    for k, g in steps:
                        r, c, un = used(g)
                        pe.wait_ge(m_ready, NLEV * p + k + 1)
                        if lev >= 1:
                            pe.wait_ge(e_ready, NLEV * p + prior(k, g) + 1)
                        for i in range(un):
                            mm = pe.matmul(bank[0:r, mbank(g), i * P:i * P + c], ee[0:r, g, i, 0:c], mm_[0:r, g, i, 0:c],
                                           start=True, stop=True)
                        mm.then_inc(dm_mm, 1)
                    for k, g in steps:
                        r, c, un = used(g)
                        pe.wait_ge(d_ready, NLEV * p + k + 1)
                        if k >= 3:
                            pe.wait_ge(e_ready, NLEV * p + k - 2)
                        for i in range(un):
                            mm = pe.transpose(bank[0:r, 4 + k % 3, i * P:i * P + c], dd[0:r, g, i, 0:c], ident[0:r, 0:r])
                        mm.then_inc(e_turned, 1)
                pe.wait_ge(e_ready, NLEV * (p + 1))
                pe.wait_ge(d_ready, NLEV * (p + 1))

                def fill(n, step):
                    if p + 1 < PAIRS:
                        for i in FILL.get((n, step), ()):
                            projection_part(p + 1, i)

                for n in range(NT):
                    q = NT * p + n
                    pe.wait_ge(x_ready, (NT + 1) * p + n + 1)
                    x = xs[:, n % 2, :]
                    pe.matmul(bank[:, 0, 0:P], arT[:, n, 0, :], x, start=True, stop=False)
                    for hh in range(2):
                        d = slice(hh * HS, (hh + 1) * HS)
                        mm = pe.matmul(bank[:, 0, d], am[:, 2 * n + hh, 2, :], tok[:, 0, n, d], start=False, stop=(hh == 1))
                    mm.then_inc(r_mm, 1)
                    fill(n, 0)
                    pe.wait_ge(r_ready, q + 1)
                    for hh in range(2):
                        d = slice(hh * HS, (hh + 1) * HS)
                        u = 2 * n + hh
                        mm = pe.matmul(bank[:, 1, d], ee[:, u // 4, u % 4, :], r_sb[:, d], start=True, stop=True)
                    mm.then_inc(sa_mm, 1)
                    fill(n, 1)
                    pe.wait_ge(sa_ready, q + 1)
                    pe.matmul(bank[:, 4, 0:P], tok[:, 1, n, :], sa_sb[:, :], start=True, stop=False)
                    pe.matmul(bank[:, 4, 0:P], tok[:, 2, n, :], tok[:, 0, n, :], start=False, stop=True).then_inc(y_mm, 1)
                    if n >= 2:
                        pe.wait_ge(o_ready, (NT + 1) * p + n - 1)
                    ob = 2 + n % 2
                    pe.matmul(bank[:, ob, 0:P], arT[:, n, 1, :], x, start=True, stop=False)
                    for hh in range(2):
                        d = slice(hh * HS, (hh + 1) * HS)
                        pe.matmul(bank[:, ob, d], am[:, 2 * n + hh, 1, :], sa_sb[:, d], start=False, stop=False)
                        mm = pe.matmul(bank[:, ob, d], am[:, 2 * n + hh, 3, :], tok[:, 0, n, d], start=False, stop=(hh == 1))
                    mm.then_inc(o_mm, 1)
                    fill(n, 2)

                if p + 1 < PAIRS:
                    pe.wait_ge(th_ready, 3 * (p + 1) + 2)
                pe.wait_ge(s0_loaded, 32 * (p + 1))
                for b in range(B):
                    mm = pe.transpose(bank[:, 5 + b // 4, (b % 4) * P:(b % 4 + 1) * P], s0[:, 0, b, :], ident[:, :])
                mm.then_inc(s0_turned, 1)
                pe.wait_ge(s0_ready, p + 1)
                pe.wait_ge(masked_ready, p + 1)
                pe.wait_ge(x_ready, (NT + 1) * (p + 1))
                for b in range(B):
                    pe.matmul(bank[0:NS, 0, 0:P], masked[:, 0, b, :], s0[:, 1, b, :], start=(b == 0), stop=False)
                for hh in range(2):
                    d = slice(hh * HS, (hh + 1) * HS)
                    mm = pe.matmul(bank[0:NS, 0, d], ams[:, hh, 2, :], tok[0:NS, 0, NT, d], start=False, stop=(hh == 1))
                mm.then_inc(r_mm, 1)
                pe.wait_ge(sample_r_ready, p + 1)
                for hh in range(2):
                    d = slice(hh * HS, (hh + 1) * HS)
                    mm = pe.matmul(bank[0:NS, 1, d], ee[0:NS, GROUPS, hh, 0:NS], r_sb[0:NS, d], start=True, stop=True)
                mm.then_inc(sa_mm, 1)
                pe.wait_ge(sample_sa_ready, p + 1)
                pe.wait_ge(o_ready, (NT + 1) * p + NT)
                for b in range(B):
                    pe.matmul(bank[0:NS, 2, 0:P], masked[:, 1, b, :], s0[:, 1, b, :], start=(b == 0), stop=False)
                for hh in range(2):
                    d = slice(hh * HS, (hh + 1) * HS)
                    pe.matmul(bank[0:NS, 2, d], ams[:, hh, 1, :], sa_sb[0:NS, d], start=False, stop=False)
                    mm = pe.matmul(bank[0:NS, 2, d], ams[:, hh, 3, :], tok[0:NS, 0, NT, d], start=False, stop=(hh == 1))
                mm.then_inc(o_mm, 1)
                for half in range(2):
                    pe.matmul(bank[:, 5 + half, :], tok[0:NS, 1, NT, :], expd[:, 0, 4 * half:4 * half + 4, :],
                              start=True, stop=False)
                    mm = pe.matmul(bank[:, 5 + half, :], tok[0:NS, 2, NT, :], expd[:, 1, 4 * half:4 * half + 4, :],
                                   start=False, stop=True)
                mm.then_inc(ys_mm, 1)
                pe.wait_ge(ys_ready, p + 1)
                for b in range(B):
                    pe.transpose(bank[:, 5 + b // 4, (b % 4) * P:(b % 4 + 1) * P], s0[:, 1, b, :], ident[:, :])
                pe.transpose(bank[:, 7, 0:P], xs[:, NT % 2, :], ident[:, :]).then_inc(st_turned, 1)

                if p + 1 < PAIRS:
                    for i in range(2 * PARTS + 6, 3 * PARTS + 6):
                        projection_part(p + 1, i)

                pe.wait_ge(on_ready, p + 1)
                for n in range(NTILE):
                    r = rows_of(n)
                    mm = pe.transpose(bank[:, n // 4, (n % 4) * P:(n % 4) * P + r], o_all[0:r, n, :], ident[0:r, 0:r])
                mm.then_inc(y_turned, 1)

        @block.scalar
        def _(act):
            link = Chain(act, act_chain)
            act.wait_ge(hv_ready, 1)

            def mixing(q, i, m, chunk):
                act.wait_ge(wide_ready, WJ * q + i + 1)
                if 3 * q + m >= 1:
                    act.wait_ge(prev_used, 3 * q + m)
                mix_scaled(nc, wide[:, G:G + TX], vec(vecs, "mu", chunk), prev, prev_s).then_inc(prev_ready, 1)

            def tanh(q, i, out, bias):
                act.wait_ge(wide_ready, WJ * q + i + 1)
                nc.scalar.activation(out[:, :], wide[:, G:G + TT], ACT.Tanh, scale=0.5, bias=bias).then_inc(th_ready, 1)

            def after_tile(q, n):
                if n == 2:
                    mixing(q, 0, 0, 6 + q)
                if n == 3:
                    tanh(q, 1, sig, hv[:, 0, q:q + 1])
                if n == 6:
                    mixing(q, 2, 1, q)
                if n == 7:
                    tanh(q, 3, aT, hv[:, 1, q:q + 1])

            for n in range(NT):
                after_tile(0, n)
            mixing(0, 4, 2, 12)
            for p in range(PAIRS):
                kT = krv(p)[0]
                kkT, cum, decT = kk_cum_dec(p)
                rnT = cum
                r_sb, _, _, out_p, _ = small(p)
                o_all = tiled(turns[p % 2][1])
                act.wait_ge(prev_used, 3 * p + 1)
                if p >= 1:
                    act.wait_ge(on_ready, p)
                nc.scalar.activation(kkT[:, :], kT[:, :], ACT.Square, scale=vec(vecs, "k_k", p)).then_inc(sq_ready, 1)
                act.wait_ge(cc_ready, p + 1)
                nc.scalar.activation(decT[:, :], cum[:, :], ACT.Exp, scale=-W_GATE)
                nc.scalar.activation(dprevT, dprevT, ACT.Exp, scale=-W_GATE)
                nc.scalar.activation(pm[:, :], pm[:, :], ACT.Exp, scale=-W_GATE)
                nc.scalar.activation(dinvT, cum[:, :], ACT.Exp, scale=W_GATE).then_inc(dec_ready, 1)
                act.wait_ge(kk_max, p + 1)
                link(nc.scalar.activation(rnT[:, :], rnT[:, :], ACT.Ln))
                nc.scalar.activation(rnT[:, :], rnT[:, :], ACT.Exp, scale=-0.5).then_inc(rn_ready, 1)
                if p >= 1:
                    act.wait_ge(y_stored, 16 * p)
                tanh(p, 6, gT, 0.0)
                for q in range(7):
                    act.wait_ge(tok_turned, 7 * p + q + 1)
                    if q < 6:
                        ins = nc.scalar.copy(tok[:, q // 2, 4 * (q % 2):4 * (q % 2) + 4, :],
                                             bank[:, 6 + q % 2, :].rearrange("p (n c) -> p n c", n=4))
                    else:
                        ins = nc.scalar.copy(tok[0:NS, :, NT, :], bank[0:NS, 6, 0:3 * P].rearrange("p (n c) -> p n c", n=3))
                    ins.then_inc(tok_ready, 1)
                for g in range(NG):
                    r, c, un = used(g)
                    act.wait_ge(d0_turned, NG * p + g + 1)
                    nc.scalar.copy(dd[0:r, g, 0:un, 0:c], banks4(bank, g, r, c, un)).then_inc(d0_ready, 1)
                for k, (lev, g) in enumerate(STEPS):
                    r, c, un = used(g)
                    act.wait_ge(e_turned, NLEV * p + k + 1)
                    nc.scalar.copy(ee[0:r, g, 0:un, 0:c], banks4(bank, 4 + k % 3, r, c, un)).then_inc(e_ready, 1)
                for n in range(NTILE):
                    if n == NT:
                        act.wait_ge(s0_turned, p + 1)
                        nc.scalar.copy(s0[:, 1, :, :].rearrange("p b c -> p (b c)"), wide[:, 5 * 512:7 * 512]).then_inc(s0_ready, 1)
                    r = rows_of(n)
                    act.wait_ge(r_mm, NTILE * p + n + 1)
                    ins = nc.scalar.copy(r_sb[0:r, :], bank[0:r, 0, 0:P])
                    ins.then_inc(r_ready if n < NT else sample_r_ready, 1)
                    act.wait_ge(o_mm, NTILE * p + n + 1)
                    nc.scalar.copy(o_all[0:r, n, :], bank[0:r, 2 + n % 2, 0:P]).then_inc(o_ready, 1)
                    if p + 1 < PAIRS:
                        after_tile(p + 1, n)
                act.wait_ge(st_turned, p + 1)
                if p >= 1:
                    act.wait_ge(stored, 64 * p)
                nc.scalar.copy(out_p[:, :], bank[:, 7, 0:P])
                nc.scalar.copy(out_s[:, :, :].rearrange("p b c -> p (b c)"), wide[:, 5 * 512:7 * 512]).then_inc(st_ready, 1)
                act.wait_ge(var_ready, p + 1)
                link(nc.scalar.activation(stat[:, 2, :], stat[:, 1, :], ACT.Ln, scale=1.0 / HS, bias=eps_tile(nc)[:, 1:2]))
                nc.scalar.activation(stat[:, 3, :], stat[:, 2, :], ACT.Exp, scale=-0.5).then_inc(rs_ready, 1)
                if p + 1 < PAIRS:
                    mixing(p + 1, 4, 2, 12 + p + 1)

        @block.vector
        def _(dve):
            link = Chain(dve, dve_chain)
            for i in range(2):
                for j in range(2):
                    link(nc.vector.memset(turns[i][j][:, :], 0.0))
            nc.vector.memset(s0[:, :, :, :], 0.0).then_inc(s0_zeroed, 1)
            nc.vector.tensor_scalar(hv[:, 0, :], vec(vecs, "w0"), 0.5, None, ALU.mult)
            nc.vector.tensor_scalar(hv[:, 2, :], vec(vecs, "k_a"), -1.0, 1.0, ALU.mult, ALU.add)
            nc.vector.tensor_scalar(hv[:, 1, :], vec(vecs, "a0"), 0.5, None, ALU.mult).then_inc(hv_ready, 1)
            dve.wait_ge(hv_ready, 1)

            def mixing(q, m, chunk):
                dve.wait_ge(prev_ready, 3 * q + m + 1)
                if m != 1:
                    link(nc.vector.memset(prev[:, 0:1], 0.0))
                link(mix_rest(nc, krv(q)[m], wide[:, G:G + TX], omu[:, chunk:chunk + 1], prev, prev_s))
                dve.sem_inc(prev_used, 1)

            mixing(0, 0, 6)
            mixing(0, 1, 0)
            mixing(0, 2, 12)
            for p in range(PAIRS):
                kT, rT, vT = krv(p)
                kkT, cum, decT = kk_cum_dec(p)
                rnT = cum
                _, sa_sb, xsc, _, xs = small(p)
                ov, o_all = tiled(turns[p % 2][0]), tiled(turns[p % 2][1])
                if p >= 1:
                    dve.wait_ge(stored, 64 * p)
                dve.wait_ge(th_ready, 3 * p + 2)
                link(nc.vector.tensor_scalar(sig[:, :], sig[:, :], 0.5, 0.5, ALU.mult, ALU.add))
                link(nc.vector.tensor_tensor_scan(cum[:, :], const_view(const, "keep"), sig[:, :], 0.0, ALU.mult, ALU.add))
                cumt = cum[:, 0:SEQ].rearrange("p (n t) -> p n t", n=NT)
                link(nc.vector.tensor_copy(pm[:, :], cumt[:, :, P // 2]))
                link(nc.vector.tensor_tensor(cumt, cumt, bcast(pm[:, :].unsqueeze(2), [P, NT, P]), ALU.subtract))
                nc.vector.tensor_tensor(dprevT, cum[:, :], sig[:, :], ALU.subtract).then_inc(cc_ready, 1)
                link(nc.vector.tensor_scalar(aT[:, :], aT[:, :], 0.5, 0.5, ALU.mult, ALU.add))
                dve.wait_ge(wide_ready, WJ * p + 6)
                dve.wait_ge(dec_ready, p + 1)
                link(nc.vector.tensor_scalar(rnT[:, :], wide[:, 0:TT], 1e-24, None, ALU.max))
                dve.sem_inc(kk_max, 1)
                dve.wait_ge(rn_ready, p + 1)
                dve.wait_ge(dec_ready, p + 1)
                link(nc.vector.scalar_tensor_tensor(out=kkT[:, :], in0=kT[:, :], scalar=vec(vecs, "k_k", p), in1=rnT[:, :],
                                                    op0=ALU.mult, op1=ALU.mult))

                def tiles(t):
                    return t[:, 0:SEQ].rearrange("p (n t) -> p n t", n=NT)

                for c in range(2):
                    x0, x1, s = ((kkT, dprevT, -1.0), (rT, decT, 1.0))[c]
                    nc.vector.scalar_tensor_tensor(out=arT[:, 0:NT, c, :], in0=tiles(x0), scalar=s, in1=tiles(x1),
                                                   op0=ALU.mult, op1=ALU.mult)
                    nc.vector.scalar_tensor_tensor(out=arT[:, NT, c, 0:NS], in0=x0[:, SEQ:TT], scalar=s, in1=x1[:, SEQ:TT],
                                                   op0=ALU.mult, op1=ALU.mult)
                link(nc.vector.tensor_tensor(beT[:, :], kkT[:, :], aT[:, :], ALU.mult))
                link(nc.vector.tensor_tensor(beT[:, :], beT[:, :], dinvT, ALU.mult))
                link(nc.vector.tensor_scalar(aT[:, :], aT[:, :], vec(vecs, "k_a", p), hv[:, 2, p:p + 1], ALU.mult, ALU.add))
                link(nc.vector.tensor_tensor(kT[:, :], kT[:, :], aT[:, :], ALU.mult))
                nc.vector.tensor_tensor(kaT[:, :], kT[:, :], dinvT, ALU.mult)
                link(nc.vector.scalar_tensor_tensor(out=prT[:, :], in0=rT[:, :], scalar=vec(vecs, "r_k", p), in1=kT[:, :],
                                                    op0=ALU.mult, op1=ALU.mult))
                dve.sem_inc(prep_ready, 1)
                dve.wait_ge(th_ready, 3 * p + 3)
                link(nc.vector.scalar_tensor_tensor(out=gT[:, :], in0=gT[:, :], scalar=1.0, in1=wide[:, G:G + TT],
                                                    op0=ALU.add, op1=ALU.mult))
                dve.sem_inc(gate_read, 1)
                dve.wait_ge(wide_ready, WJ * p + 8)
                dve.wait_ge(tok_ready, 7 * (p + 1))
                bonus = bank[:, 3, 0:2 * NTILE]
                for rr, n0, n1 in ((P, 0, NT), (NS, NT, NTILE)):
                    link(nc.vector.tensor_tensor(ov[0:rr, n0:n1, :].rearrange("p n (h i) -> p (n h) i", h=2),
                                                 tok[0:rr, 0, n0:n1, :].rearrange("p n (h i) -> p (n h) i", h=2),
                                                 bcast(bonus[0:rr, 2 * n0:2 * n1].unsqueeze(2), [rr, 2 * (n1 - n0), HS]), ALU.mult))
                dve.sem_inc(bonus_done, 1)
                for u in range(UNITS + 2):
                    dve.wait_ge(am_mm, (UNITS + 2) * p + u + 1)
                    if u < UNITS:
                        ins = nc.vector.tensor_tensor(am[:, u, :, :].rearrange("p a t -> p (a t)"), bank[:, u % 8, :],
                                                      const_view(const, "mask4"), ALU.mult)
                    else:
                        ins = nc.vector.tensor_tensor(ams[:, u - UNITS, :, :].rearrange("p a t -> p (a t)"),
                                                      bank[0:NS, u % 8, 0:4 * NS], const_view(const, "mask4s")[0:NS, :], ALU.mult)
                    ins.then_inc(am_ready, 1)
                dve.wait_ge(am_ready, (UNITS + 2) * (p + 1))
                for g in range(NG):
                    r, c, un = used(g)
                    src = am[:, 4 * g:4 * g + 4, 0, :] if g < GROUPS else ams[:, :, 0, :]
                    e = ee[0:r, g, 0:un, 0:c]
                    link(nc.vector.tensor_tensor(e, src, bcast(const_view(const, "pair1")[0:r, 0:c].unsqueeze(1), [r, un, c]), ALU.mult))
                    nc.vector.tensor_tensor(e, e, bcast(ident[0:r, 0:c].unsqueeze(1), [r, un, c]), ALU.add).then_inc(e0_ready, 1)
                for lev, b in enumerate(LEVELS):
                    steps = [(k, g) for k, (lv, g) in enumerate(STEPS) if lv == lev]
                    for k, g in steps:
                        r, c, un = used(g)
                        dve.wait_ge(m_mm, NLEV * p + k + 1)
                        nc.vector.tensor_tensor(mm_[0:r, g, 0:un, 0:c], banks4(bank, mbank(g), r, c, un),
                                                bcast(const_view(const, f"pair{b}")[0:r, 0:c].unsqueeze(1), [r, un, c]),
                                                ALU.mult).then_inc(m_ready, 1)
                    for k, g in steps:
                        r, c, un = used(g)
                        dve.wait_ge(dm_mm, NLEV * p + k + 1)
                        nc.vector.tensor_tensor(dd[0:r, g, 0:un, 0:c], banks4(bank, mbank(g), r, c, un),
                                                dd[0:r, g, 0:un, 0:c], ALU.add).then_inc(d_ready, 1)
                ends = decT[:, 0:SEQ].rearrange("p (n t) -> p n t", n=NT)[:, :, P - 1]
                link(nc.vector.tensor_copy(xscale[:, :], ends))
                link(nc.vector.tensor_tensor(xscale[:, 0:NT - 1], xscale[:, 0:NT - 1], pm[:, 1:NT], ALU.mult))
                nc.vector.memset(xs[:, 0, :], 0.0).then_inc(x_ready, 1)
                dve.wait_ge(x_ready, (NT + 1) * p + 1)
                for n in range(NT):
                    link(nc.vector.tensor_scalar(xsc[:, :], xs[:, n % 2, :], xscale[:, n:n + 1], None, ALU.mult))
                    dve.wait_ge(sa_mm, NTILE * p + n + 1)
                    nc.vector.tensor_copy(sa_sb[:, :], bank[:, 1, 0:P]).then_inc(sa_ready, 1)
                    dve.wait_ge(y_mm, NT * p + n + 1)
                    if n >= 1:
                        dve.wait_ge(o_mm, NTILE * p + n)
                    xn = xs[:, (n + 1) % 2, :]
                    link(nc.vector.scalar_tensor_tensor(out=xn, in0=bank[:, 4, 0:P], scalar=xscale[:, n:n + 1],
                                                        in1=const_view(const, "headsum"), op0=ALU.mult, op1=ALU.mult))
                    nc.vector.tensor_tensor(xn, xn, xsc[:, :], ALU.add).then_inc(x_ready, 1)
                    dve.wait_ge(x_ready, (NT + 1) * p + n + 2)
                    if p + 1 < PAIRS and n == 2:
                        mixing(p + 1, 0, 6 + p + 1)
                    if p + 1 < PAIRS and n == 6:
                        mixing(p + 1, 1, p + 1)
                own = const_view(const, "owncols").rearrange("p (b t) -> p b t", b=B)
                for c in range(2):
                    ins = nc.vector.tensor_tensor(masked[:, c, :, :], own, bcast(arT[:, NT, c, 0:NS].unsqueeze(1), [P, B, NS]), ALU.mult)
                ins.then_inc(masked_ready, 1)
                dve.wait_ge(sa_mm, NTILE * p + NTILE)
                link(nc.vector.tensor_copy(sa_sb[0:NS, :], bank[0:NS, 1, 0:P]))
                ownseq = bcast(const_view(const, "ownseq")[0:NS, :].unsqueeze(2), [NS, B, P])
                nc.vector.tensor_tensor(expd[:, 0, :, :], ownseq, bcast(sa_sb[0:NS, :].unsqueeze(1), [NS, B, P]), ALU.mult)
                nc.vector.tensor_tensor(expd[:, 1, :, :], ownseq, bcast(tok[0:NS, 0, NT, :].unsqueeze(1), [NS, B, P]),
                                        ALU.mult).then_inc(sample_sa_ready, 1)
                dve.wait_ge(ys_mm, p + 1)
                s1 = s0[:, 1, :, :]
                link(nc.vector.tensor_tensor(s1.rearrange("p b c -> p (b c)"), wide[:, 5 * 512:7 * 512],
                                             s1.rearrange("p b c -> p (b c)"), ALU.add))
                ends = decT[:, SEQ:TT].rearrange("p (b t) -> p b t", b=B)[:, :, TS - 1:TS]
                nc.vector.tensor_tensor(s1, s1, bcast(ends, [P, B, P]), ALU.mult).then_inc(ys_ready, 1)

                dve.wait_ge(o_ready, NTILE * (p + 1))
                o = o_all[:, :, :].rearrange("p n (h i) -> p (n h) i", h=2)
                sq = sq_o.rearrange("p (n i) -> p n i", i=HS)
                link(nc.vector.tensor_reduce(stat[:, 0, :], o, X, ALU.add))
                link(nc.vector.tensor_scalar(stat[:, 0, :], stat[:, 0, :], 1.0 / HS, None, ALU.mult))
                link(nc.vector.tensor_tensor(o, o, bcast(stat[:, 0, :].unsqueeze(2), [P, 2 * NTILE, HS]), ALU.subtract))
                link(nc.vector.tensor_tensor(sq, o, o, ALU.mult))
                nc.vector.tensor_reduce(stat[:, 1, :], sq, X, ALU.add).then_inc(var_ready, 1)
                dve.wait_ge(rs_ready, p + 1)
                link(nc.vector.tensor_tensor(o, o, bcast(stat[:, 3, :].unsqueeze(2), [P, 2 * NTILE, HS]), ALU.mult))
                link(nc.vector.tensor_tensor(o_all[:, :, :], o_all[:, :, :],
                                             bcast(row(rows, "lnx_g", p * P, (p + 1) * P).unsqueeze(1), [P, NTILE, P]), ALU.mult))
                link(nc.vector.tensor_tensor(o_all[:, :, :], o_all[:, :, :],
                                             bcast(row(rows, "lnx_b", p * P, (p + 1) * P).unsqueeze(1), [P, NTILE, P]), ALU.add))
                nc.vector.tensor_tensor(o_all[:, :, :], o_all[:, :, :], ov[:, :, :], ALU.add).then_inc(on_ready, 1)
                dve.wait_ge(y_turned, p + 1)
                nc.vector.scalar_tensor_tensor(out=gT[:, :], in0=wide[:, 0:TT], scalar=0.5, in1=gT[:, :],
                                               op0=ALU.mult, op1=ALU.mult).then_inc(y_done, 1)
                if p + 1 < PAIRS:
                    mixing(p + 1, 2, 12 + p + 1)


def prior(k, g):
    return max(i for i, (_, gg) in enumerate(STEPS[:k]) if gg == g)


def mbank(g):
    return g if g < GROUPS else 7


def banks4(bank, j, r, c, un):
    return bank[0:r, j, 0:un * P].rearrange("p (u t) -> p u t", u=un)[:, :, 0:c]


def gates_and_queries(nc, name, w_d, chunks, xT, gain, vecs, mq_g, const, wide, mqT, gates):
    n_all = len(chunks)
    with Stage(nc, name) as st:
        w = st.sb("w", [P, 2, KC, P])
        sq = st.sb("sq", [P, 2, TT])
        w_loaded = [st.sem(f"w_loaded{i}") for i in range(2)]
        gained, ready, free, act_read, sq_ready, rn_ready, done, dve_chain, act_chain = st.sems(
            "gained ready free act_read sq_ready rn_ready done dve_chain act_chain")
        block = st.block()
        G = (0, 1536)

        @block.sync
        def _(sp):
            for j, c in enumerate(chunks):
                if j >= 2:
                    sp.wait_ge(ready, j - 1)
                sp.dma_start(w[:, j % 2, :, :].rearrange("p k c -> p (k c)"), w_d[c]).then_inc(w_loaded[j % 2], 16)

        if gain is not None:
            @block.gpsimd
            def _(pool):
                for j in range(n_all):
                    pool.wait_ge(w_loaded[j % 2], 16 * (j // 2 + 1))
                    nc.gpsimd.tensor_tensor(w[:, j % 2], w[:, j % 2], bcast(gain.unsqueeze(2), [P, KC, P]),
                                            ALU.mult).then_inc(gained, 1)

        @block.tensor
        def _(pe):
            for j in range(n_all):
                if j >= 2:
                    pe.wait_ge(free, j - 1)
                if gain is None:
                    pe.wait_ge(w_loaded[j % 2], 16 * (j // 2 + 1))
                else:
                    pe.wait_ge(gained, j + 1)
                project(pe, wide, G[j % 2], w[:, j % 2], xT, TT).then_inc(ready, 1)
            for c in range(2):
                j = n_all + c
                pe.wait_ge(free, j - 1)
                pe.wait_ge(sq_ready, c + 1)
                for a, b in COLS:
                    b = min(b, TT)
                    mm = pe.matmul(wide[:, G[j % 2] + a:G[j % 2] + b], const_view(const, "headsum"), sq[:, c, a:b],
                                   start=True, stop=True)
                mm.then_inc(ready, 1)

        @block.scalar
        def _(act):
            link = Chain(act, act_chain)
            for j in range(n_all):
                act.wait_ge(ready, j + 1)
                ps = wide[:, G[j % 2]:G[j % 2] + TT]
                if j < 2:
                    nc.scalar.activation(sq[:, j, :], ps, ACT.Square).then_inc(sq_ready, 1)
                else:
                    nc.scalar.activation(gates[:, j - 2, :], ps, ACT.Tanh, scale=0.5).then_inc(act_read, 1)
            for c in range(2):
                j = n_all + c
                act.wait_ge(ready, j + 1)
                link(nc.scalar.activation(sq[:, c, :], wide[:, G[j % 2]:G[j % 2] + TT], ACT.Ln, scale=1.0 / HS,
                                          bias=eps_tile(nc)[:, 0:1]))
            for c in range(2):
                nc.scalar.activation(sq[:, c, :], sq[:, c, :], ACT.Exp, scale=-0.5).then_inc(rn_ready, 1)

        @block.vector
        def _(dve):
            for j in range(n_all):
                dve.wait_ge(ready, j + 1)
                ps = wide[:, G[j % 2]:G[j % 2] + TT]
                if j < 2:
                    dve.wait_ge(sq_ready, j + 1)
                    nc.vector.tensor_copy(mqT[:, j, :], ps).then_inc(free, 1)
                else:
                    dve.wait_ge(act_read, j - 1)
                    g = gates[:, j - 2, :]
                    nc.vector.scalar_tensor_tensor(out=g, in0=g, scalar=1.0, in1=ps, op0=ALU.add, op1=ALU.mult).then_inc(free, 1)
            dve.wait_ge(free, n_all)
            for c in range(2):
                dve.wait_ge(rn_ready, c + 1)
                nc.vector.scalar_tensor_tensor(out=mqT[:, c, :], in0=mqT[:, c, :], scalar=mq_g, in1=sq[:, c, :],
                                               op0=ALU.mult, op1=ALU.mult).then_inc(done, 1)


def memory_attention(nc, name, layer, mqT, mkT, mv, cmk, cmv, gates, const, ones, bank, scratch=None):
    ident = const_view(const, "ident")
    SC = HS ** -0.5
    with Stage(nc, name) as st:
        both = st.sb("both", [P, 4096])
        pr = both[:, 0:2048].rearrange("p (r h t) -> p r h t", r=2, h=4)
        pT = both[:, 2048:4096].rearrange("p (r i t) -> p r i t", r=2, i=8)
        kT = both[:, :].rearrange("p (b c t) -> p b c t", b=B, c=2)
        mx = st.sb("mx", [P, 2, 4])
        ls = st.sb("ls", [P, 2, 4])
        if scratch is None:
            kn = st.sb("kn", [P, B, 2, MEMT])
            vn = st.sb("vn", [P, B, 2, MEMT])
        else:
            dead = scratch[:, :, :].rearrange("p k t -> p (k t)")
            kn, vn = (dead[:, i * 4096:(i + 1) * 4096].rearrange("p (b c d) -> p b c d", b=B, c=2) for i in range(2))
        qbd = st.sb("qbd", [P, 2, B, 2, TS])
        ps_ = st.sb("ps", [P, B, 2, 32])
        red = st.sb("red", [P, 256])
        mxT = st.sb("mxT", [P, 2])
        dg = st.sb("dg", [P, 256])
        bc = st.sb("bc", [P, 256])
        (k_loaded, v_loaded, qbd_ready, turned, kT_ready, ss_mm, red_ready, red_turned, dg_ready, bc_mm, bc_ready,
         sub_ready, exp_ready, sum_ready, sum_mm, ws_ready, os_mm, s_mm, mx_ready, pr_ready, w_ready, w_turned,
         pT_ready, o_mm, y_ready, dve_chain) = st.sems(
            "k_loaded v_loaded qbd_ready turned kT_ready ss_mm red_ready red_turned dg_ready bc_mm bc_ready "
            "sub_ready exp_ready sum_ready sum_mm ws_ready os_mm s_mm mx_ready pr_ready w_ready w_turned "
            "pT_ready o_mm y_ready dve_chain")
        block = st.block()

        @block.sync
        def _(sp):
            sp.dma_start(kn[:, :, :, :], cmk[layer].rearrange("b (c p) d -> p b c d", p=P)).then_inc(k_loaded, 16)
            sp.dma_start(vn[:, :, :, :], cmv[layer].rearrange("b (c p) d -> p b c d", p=P)).then_inc(v_loaded, 16)

        @block.tensor
        def _(pe):
            def scores(n):
                if n >= 2:
                    pe.wait_ge(pr_ready, n - 1)
                for hh in range(2):
                    for c in range(2):
                        mm = pe.matmul(bank[:, 2 * (n % 2) + hh, c * MEMT:(c + 1) * MEMT],
                                       mqT[hh * HS:(hh + 1) * HS, c, n * P:(n + 1) * P],
                                       mkT[hh * HS:(hh + 1) * HS, layer, c, :], start=True, stop=True)
                mm.then_inc(s_mm, 1)

            def values(n):
                pe.wait_ge(pT_ready, n + 1)
                if n >= 2:
                    pe.wait_ge(y_ready, n - 1)
                for hh in range(2):
                    for c in range(2):
                        for kc in range(2):
                            mm = pe.matmul(bank[hh * HS:(hh + 1) * HS, 6 + n % 2, c * P:(c + 1) * P],
                                           mv[:, layer, kc, (2 * c + hh) * HS:(2 * c + hh + 1) * HS],
                                           pT[:, n % 2, 4 * hh + 2 * c + kc, :], start=(kc == 0), stop=(kc == 1))
                mm.then_inc(o_mm, 1)

            scores(0)
            for n in range(NT):
                if n + 1 < NT:
                    scores(n + 1)
                pe.wait_ge(w_ready, n + 1)
                if n >= 1:
                    pe.wait_ge(pT_ready, n)
                for i in range(8):
                    mm = pe.transpose(bank[:, 4 + i // 4, (i % 4) * P:(i % 4 + 1) * P],
                                      pr[:, n % 2, i // 2, (i % 2) * P:(i % 2 + 1) * P], ident[:, :])
                mm.then_inc(w_turned, 1)
                if n >= 1:
                    values(n - 1)
            values(NT - 1)
            pe.wait_ge(k_loaded, 16)
            pe.wait_ge(pr_ready, NT)
            for b in range(B):
                if b >= 2:
                    pe.wait_ge(kT_ready, b - 1)
                for c in range(2):
                    for kc in range(2):
                        mm = pe.transpose(bank[:, b % 2, (2 * c + kc) * P:(2 * c + kc + 1) * P],
                                          kn[:, b, kc, c * P:(c + 1) * P], ident[:, :])
                mm.then_inc(turned, 1)
            pe.wait_ge(qbd_ready, 1)
            for b in range(B):
                pe.wait_ge(kT_ready, b + 1)
                for kc in range(2):
                    for c in range(2):
                        mm = pe.matmul(bank[:, 2, b * 64 + kc * 32 + c * 16:b * 64 + kc * 32 + c * 16 + 16],
                                       kT[:, b, c, kc * P:(kc + 1) * P], qbd[:, c, b, :, :].rearrange("p h t -> p (h t)"),
                                       start=True, stop=True)
            mm.then_inc(ss_mm, 1)
            pe.wait_ge(red_ready, 1)
            for i in range(2):
                mm = pe.transpose(bank[:, 3, i * P:(i + 1) * P], red[:, i * P:(i + 1) * P], ident[:, :])
            mm.then_inc(red_turned, 1)
            pe.wait_ge(dg_ready, 1)
            pe.matmul(bank[:, 0, 0:256], ones[:, :], dg[:, :], start=True, stop=True).then_inc(bc_mm, 1)
            pe.wait_ge(sum_ready, 1)
            pe.matmul(bank[:, 1, 0:256], ones[:, :], red[:, :], start=True, stop=True).then_inc(sum_mm, 1)
            pe.wait_ge(v_loaded, 16)
            pe.wait_ge(ws_ready, 1)
            pe.wait_ge(y_ready, NT)
            for b in range(B):
                for c in range(2):
                    for hh in range(2):
                        for kc in range(2):
                            at = kc * 32 + c * 16 + hh * 8
                            mm = pe.matmul(bank[hh * HS:(hh + 1) * HS, 6, c * NS + b * TS:c * NS + (b + 1) * TS],
                                           vn[:, b, kc, (2 * c + hh) * HS:(2 * c + hh + 1) * HS],
                                           ps_[:, b, at // 32, at % 32:at % 32 + 8], start=(kc == 0), stop=(kc == 1))
            mm.then_inc(os_mm, 1)

        @block.scalar
        def _(act):
            def turned_out(n):
                act.wait_ge(w_turned, n + 1)
                nc.scalar.copy(pT[:, n % 2, :, :].rearrange("p i t -> p (i t)"),
                               bank[:, 4:6, :].rearrange("p b c -> p (b c)")).then_inc(pT_ready, 1)

            for n in range(NT):
                if n >= 2:
                    act.wait_ge(w_turned, n - 1)
                act.wait_ge(mx_ready, n + 1)
                for i in range(4):
                    ins = nc.scalar.activation(pr[:, n % 2, i, :], bank[:, 2 * (n % 2) + i // 2, (i % 2) * MEMT:(i % 2 + 1) * MEMT],
                                               ACT.Exp, scale=SC, bias=mx[:, n % 2, i:i + 1], accum_out=ls[:, n % 2, i:i + 1])
                ins.then_inc(pr_ready, 1)
                if n >= 1:
                    turned_out(n - 1)
            turned_out(NT - 1)
            for b in range(B):
                act.wait_ge(turned, b + 1)
                nc.scalar.copy(kT[:, b, :, :].rearrange("p c t -> p (c t)"), bank[:, b % 2, :]).then_inc(kT_ready, 1)
            act.wait_ge(bc_mm, 1)
            nc.scalar.copy(bc[:, :], bank[:, 0, 0:256]).then_inc(bc_ready, 1)
            act.wait_ge(sub_ready, 1)
            nc.scalar.activation(ps_[:, :, :, :], ps_[:, :, :, :], ACT.Exp, scale=SC).then_inc(exp_ready, 1)

        @block.vector
        def _(dve):
            link = Chain(dve, dve_chain)
            link(nc.vector.memset(qbd[:, :, :, :, :], 0.0))
            for hh in range(2):
                d = slice(hh * HS, (hh + 1) * HS)
                link(nc.vector.tensor_copy(qbd[d, :, :, hh, :], mqT[d, :, SEQ:TT].rearrange("p c (b t) -> p c b t", b=B)))
            dve.sem_inc(qbd_ready, 1)

            def maxima(n):
                dve.wait_ge(s_mm, n + 1)
                link(nc.vector.tensor_reduce(mx[:, n % 2, :], bank[:, 2 * (n % 2):2 * (n % 2) + 2, :].rearrange("p b (c t) -> p (b c) t", c=2), X, ALU.max))
                nc.vector.tensor_scalar(mx[:, n % 2, :], mx[:, n % 2, :], -SC, None, ALU.mult).then_inc(mx_ready, 1)

            def gated(n):
                dve.wait_ge(o_mm, n + 1)
                y = gates[:, :, n * P:(n + 1) * P]
                nc.vector.scalar_tensor_tensor(out=y, in0=bank[:, 6 + n % 2, 0:2 * P].rearrange("p (c t) -> p c t", c=2),
                                               scalar=0.5, in1=y, op0=ALU.mult, op1=ALU.mult).then_inc(y_ready, 1)

            maxima(0)
            for n in range(NT):
                if n + 1 < NT:
                    maxima(n + 1)
                dve.wait_ge(pr_ready, n + 1)
                link(nc.vector.reciprocal(ls[:, n % 2, :], ls[:, n % 2, :]))
                nc.vector.tensor_tensor(pr[:, n % 2, :, :], pr[:, n % 2, :, :], bcast(ls[:, n % 2, :].unsqueeze(2), [P, 4, MEMT]),
                                        ALU.mult).then_inc(w_ready, 1)
                if n >= 1:
                    gated(n - 1)
            gated(NT - 1)
            dve.wait_ge(ss_mm, 1)
            s = bank[:, 2, :].rearrange("p (b k c) -> p b k c", b=B, k=2)
            nc.vector.tensor_reduce(red[:, :].rearrange("p (b c) -> p b c", b=B), s.rearrange("p b k c -> p b c k"), X,
                                    ALU.max).then_inc(red_ready, 1)
            dve.wait_ge(red_turned, 1)
            link(nc.vector.tensor_reduce(mxT[:, :], bank[:, 3, 0:256].rearrange("p (i k) -> p i k", i=2), X, ALU.max))
            for i in range(2):
                ins = nc.vector.tensor_scalar(dg[:, i * P:(i + 1) * P], ident[:, :], mxT[:, i:i + 1], None, ALU.mult)
            ins.then_inc(dg_ready, 1)
            dve.wait_ge(bc_ready, 1)
            nc.vector.tensor_tensor(ps_[:, :, :, :], s, bcast(bc[:, :].rearrange("p (b c) -> p b c", b=B).unsqueeze(2), [P, B, 2, 32]),
                                    ALU.subtract).then_inc(sub_ready, 1)
            dve.wait_ge(exp_ready, 1)
            nc.vector.tensor_reduce(red[:, :].rearrange("p (b c) -> p b c", b=B), ps_[:, :, :, :].rearrange("p b k c -> p b c k"), X,
                                    ALU.add).then_inc(sum_ready, 1)
            dve.wait_ge(sum_mm, 1)
            link(nc.vector.reciprocal(bc[:, :], bank[:, 1, 0:256]))
            nc.vector.tensor_tensor(ps_[:, :, :, :], ps_[:, :, :, :], bcast(bc[:, :].rearrange("p (b c) -> p b c", b=B).unsqueeze(2), [P, B, 2, 32]),
                                    ALU.mult).then_inc(ws_ready, 1)
            dve.wait_ge(os_mm, 1)
            y = gates[:, :, SEQ:TT]
            link(nc.vector.scalar_tensor_tensor(out=y, in0=bank[:, 6, 0:2 * NS].rearrange("p (c t) -> p c t", c=2), scalar=0.5,
                                                in1=y, op0=ALU.mult, op1=ALU.mult))


def out_project(nc, name, w_d, yT, h, bank, y_load=None, h_load=None, h_store=None, scratch=None):
    with Stage(nc, name) as st:
        w = st.sb("w", [P, KC, D]) if scratch is None else \
            scratch[:, :, :].rearrange("p k t -> p (k t)")[:, 0:KC * D].rearrange("p (k c) -> p k c", k=KC)
        if h is None:
            h = st.sb("h", [P, NTILE, D])
        w_loaded, y_loaded, mm_done, added, stored = st.sems("w_loaded y_loaded mm_done added stored")
        h_loaded = [st.sem(f"h_loaded{n}") for n in range(NTILE)]
        block = st.block()

        @block.sync
        def _(sp):
            for half in range(2):
                sp.dma_start(w[:, 4 * half:4 * half + 4, :].rearrange("p k c -> p (k c)"),
                             w_d[:, 4 * half * D:4 * (half + 1) * D]).then_inc(w_loaded, 16)
            if y_load is not None:
                for k in range(6):
                    sp.dma_start(yT[:, k, :], y_load[:, k, :]).then_inc(y_loaded, 16)
            for n in range(NTILE):
                r = rows_of(n)
                sp.dma_start(h[0:r, n, :], h_load[1] if n == NT else h_load[0][n * P:(n + 1) * P, :]).then_inc(h_loaded[n], 16)

        @block.gpsimd
        def _(pool):
            for n in range(NTILE):
                r = rows_of(n)
                pool.wait_ge(added, 2 * n + 2)
                pool.dma_start(h_store[1] if n == NT else h_store[0][n * P:(n + 1) * P, :], h[0:r, n, :]).then_inc(stored, 16)
            pool.wait_ge(stored, 16 * NTILE)

        @block.tensor
        def _(pe):
            pe.wait_ge(w_loaded, 32)
            if y_load is not None:
                pe.wait_ge(y_loaded, 96)
            for j in range(2 * NTILE):
                n, half = j // 2, j % 2
                if j >= 8:
                    pe.wait_ge(added, j - 7)
                r = rows_of(n)
                for k in range(KC):
                    mm = pe.matmul(bank[0:r, j % 8, :], yT[:, k, n * P:n * P + r], w[:, k, half * 512:(half + 1) * 512],
                                   start=(k == 0), stop=(k == KC - 1))
                mm.then_inc(mm_done, 1)

        @block.vector
        def _(dve):
            for j in range(2 * NTILE):
                n, half = j // 2, j % 2
                r = rows_of(n)
                dve.wait_ge(mm_done, j + 1)
                dve.wait_ge(h_loaded[n], 16)
                hh = h[0:r, n, half * 512:(half + 1) * 512]
                nc.vector.tensor_tensor(hh, hh, bank[0:r, j % 8, :], ALU.add).then_inc(added, 1)


def keys_values_queries(nc, kv_w, q_w, vecs, rows2, const, ident, xT, bank, KT, QT, V, k_out, v_out):
    W = 384
    with Stage(nc, "kvq") as st:
        w = st.sb("w", [P, 2, KC, W])
        raw = st.sb("raw", [P, NTILE, W])
        rot = st.sb("rot", [P, NTILE, W])
        sq = st.sb("sq", [P, 2, W])
        ss = st.sb("ss", [P, NTILE * 6])
        w_loaded = [st.sem(f"w_loaded{i}") for i in range(2)]
        (gained, mm_done, raw_ready, sq_ready, ss_ready, rs_ready, rot_ready, turned, turned_out, v_ready, k_stored,
         v_stored, zeroed, dve_chain, act_chain) = st.sems(
            "gained mm_done raw_ready sq_ready ss_ready rs_ready rot_ready turned turned_out v_ready k_stored "
            "v_stored zeroed dve_chain act_chain")
        block = st.block()
        GRP = [("k", 0), ("v", 0), ("k", 1), ("v", 1), ("q", 0), ("q", 1)]
        normed = [i for i, (kind, _) in enumerate(GRP) if kind != "v"]

        @block.sync
        def _(sp):
            for i, (kind, half) in enumerate(GRP):
                src = q_w[half] if kind == "q" else kv_w[half + 2 * (kind == "v")]
                if i >= 2:
                    sp.wait_ge(mm_done, NTILE * (i - 1))
                sp.dma_start(w[:, i % 2, :, :].rearrange("p k c -> p (k c)"), src).then_inc(w_loaded[i % 2], 16)

        @block.gpsimd
        def _(pool):
            def gained_weights(i):
                kind = GRP[i][0]
                g = vec(vecs, "bg" if kind == "q" else "kvg")
                pool.wait_ge(w_loaded[i % 2], 16 * (i // 2 + 1))
                nc.gpsimd.tensor_tensor(w[:, i % 2], w[:, i % 2], bcast(g.unsqueeze(2), [P, KC, W]), ALU.mult).then_inc(gained, 1)

            gained_weights(0)
            nk = nv = 0
            for i, (kind, half) in enumerate(GRP):
                if i + 1 < len(GRP):
                    gained_weights(i + 1)
                for n in range(NTILE):
                    r = rows_of(n)
                    if kind == "v":
                        dst = v_out[1] if n == NT else v_out[0][n * P:(n + 1) * P, :]
                        pool.wait_ge(v_ready, NTILE * nv + n + 1)
                        pool.dma_start(dst[:, half * W:(half + 1) * W], V[0:r, n, half * W:(half + 1) * W]).then_inc(v_stored, 16)
                    elif kind == "k":
                        dst = k_out[1] if n == NT else k_out[0][n * P:(n + 1) * P, :]
                        if n == 0:
                            pool.wait_ge(rot_ready, nk + 1)
                        pool.dma_start(dst[:, half * W:(half + 1) * W], rot[0:r, n, :]).then_inc(k_stored, 16)
                nk += kind != "v"
                nv += kind == "v"
            pool.wait_ge(k_stored, 32 * NTILE)
            pool.wait_ge(v_stored, 32 * NTILE)

        @block.tensor
        def _(pe):
            nn = 0

            def turn(g):
                pe.wait_ge(rot_ready, g + 1)
                for n in range(NTILE):
                    j = NTILE * g + n
                    r = rows_of(n)
                    if j >= 2:
                        pe.wait_ge(turned_out, j - 1)
                    for i in range(3):
                        mm = pe.transpose(bank[:, 6 + j % 2, i * P:i * P + r], rot[0:r, n, i * P:(i + 1) * P], ident[0:r, 0:r])
                    mm.then_inc(turned, 1)

            for i in range(len(GRP)):
                pe.wait_ge(gained, i + 1)
                for n in range(NTILE):
                    j = NTILE * i + n
                    r = rows_of(n)
                    if j >= 6:
                        pe.wait_ge(raw_ready, j - 5)
                    for k in range(KC):
                        mm = pe.matmul(bank[0:r, j % 6, 0:W], xT[:, k, n * P:n * P + r], w[:, i % 2, k, :],
                                       start=(k == 0), stop=(k == KC - 1))
                    mm.then_inc(mm_done, 1)
                if i >= 1 and GRP[i - 1][0] != "v":
                    turn(nn)
                    nn += 1
            turn(nn)

        @block.scalar
        def _(act):
            link = Chain(act, act_chain)
            nn = nv = 0

            def turn_out(g):
                dst, half = ((KT, 0), (KT, 1), (QT, 0), (QT, 1))[g]
                for n in range(NTILE):
                    j = NTILE * g + n
                    r = rows_of(n)
                    act.wait_ge(turned, j + 1)
                    nc.scalar.copy(dst[:, 3 * half:3 * half + 3, n * P:n * P + r],
                                   bank[:, 6 + j % 2, 0:W].rearrange("p (i t) -> p i t", i=3)[:, :, 0:r]).then_inc(turned_out, 1)

            act.wait_ge(zeroed, 1)
            for i, (kind, half) in enumerate(GRP):
                for n in range(NTILE):
                    j = NTILE * i + n
                    r = rows_of(n)
                    act.wait_ge(mm_done, j + 1)
                    if kind == "v":
                        link(nc.scalar.copy(V[0:r, n, half * W:(half + 1) * W], bank[0:r, j % 6, 0:W]))
                        act.sem_inc(raw_ready, 1)
                        act.sem_inc(v_ready, 1)
                    else:
                        m = NTILE * nn + n
                        if n == 0 and nn >= 1:
                            act.wait_ge(rot_ready, nn)
                        if m >= 2:
                            act.wait_ge(ss_ready, m - 1)
                        nc.scalar.activation(sq[0:r, m % 2, :], bank[0:r, j % 6, 0:W], ACT.Square).then_inc(sq_ready, 1)
                        nc.scalar.copy(raw[0:r, n, :], bank[0:r, j % 6, 0:W]).then_inc(raw_ready, 1)
                if kind != "v":
                    act.wait_ge(ss_ready, NTILE * (nn + 1))
                    link(nc.scalar.activation(ss[:, :], ss[:, :], ACT.Ln, scale=1.0 / HS, bias=eps_tile(nc)[:, 0:1]))
                    nc.scalar.activation(ss[:, :], ss[:, :], ACT.Exp, scale=-0.5).then_inc(rs_ready, 1)
                    nn += 1
                if i >= 1 and GRP[i - 1][0] != "v":
                    turn_out(sum(kk != "v" for kk, _ in GRP[:i]) - 1)
            turn_out(3)

        @block.vector
        def _(dve):
            link = Chain(dve, dve_chain)
            nc.vector.memset(raw[:, NT, :], 0.0)
            nc.vector.memset(ss[:, :], 1.0).then_inc(zeroed, 1)
            cos = bcast(const_view(const, "cos").rearrange("p (n d) -> p n d", n=NTILE).unsqueeze(2), [P, NTILE, 6, 32])
            sin = bcast(const_view(const, "sin").rearrange("p (n d) -> p n d", n=NTILE).unsqueeze(2), [P, NTILE, 6, 32])
            x = raw[:, :, :].rearrange("p n (h d) -> p n h d", h=6)
            y = rot[:, :, :].rearrange("p n (h d) -> p n h d", h=6)
            flat = raw[:, :, :].rearrange("p n (h d) -> p (n h) d", h=6)
            for g, i in enumerate(normed):
                kind = GRP[i][0]
                for n in range(NTILE):
                    m = NTILE * g + n
                    r = rows_of(n)
                    dve.wait_ge(sq_ready, m + 1)
                    nc.vector.tensor_reduce(ss[0:r, 6 * n:6 * n + 6], sq[0:r, m % 2, :].rearrange("p (h d) -> p h d", h=6), X,
                                            ALU.add).then_inc(ss_ready, 1)
                dve.wait_ge(rs_ready, g + 1)
                link(nc.vector.tensor_tensor(flat, flat, bcast(ss[:, :].unsqueeze(2), [P, 6 * NTILE, HS]), ALU.mult))
                link(nc.vector.tensor_tensor(flat, flat, bcast(row(rows2, "k_g" if kind == "k" else "q_g").unsqueeze(1),
                                                               [P, 6 * NTILE, HS]), ALU.mult))
                if g >= 1:
                    dve.wait_ge(turned, NTILE * g)
                    dve.wait_ge(k_stored, 16 * NTILE * min(g, 2))
                link(nc.vector.tensor_tensor(y[:, :, :, 0:32], x[:, :, :, 0:32], cos, ALU.mult))
                link(nc.vector.tensor_tensor(y[:, :, :, 32:64], x[:, :, :, 32:64], cos, ALU.mult))
                link(nc.vector.tensor_tensor(x[:, :, :, 0:32], x[:, :, :, 0:32], sin, ALU.mult))
                link(nc.vector.tensor_tensor(x[:, :, :, 32:64], x[:, :, :, 32:64], sin, ALU.mult))
                link(nc.vector.tensor_tensor(y[:, :, :, 0:32], y[:, :, :, 0:32], x[:, :, :, 32:64], ALU.subtract))
                nc.vector.tensor_tensor(y[:, :, :, 32:64], y[:, :, :, 32:64], x[:, :, :, 0:32], ALU.add).then_inc(rot_ready, 1)
                dve.wait_ge(rot_ready, g + 1)


def lambda_row(nc, rows2, lam, subs):
    with Stage(nc, "lam") as st:
        prod = st.sb("prod", [P, 2, HS])
        two = st.sb("two", [P, 2])
        summed, exp_ready, chain = st.sems("summed exp_ready chain")
        block = st.block()
        lv = row(rows2, "lam").rearrange("p (a b d) -> p a b d", a=2, b=2)

        @block.vector
        def _(dve):
            link = Chain(dve, chain)
            link(nc.vector.tensor_tensor(prod[:, :, :], lv[:, :, 0, :], lv[:, :, 1, :], ALU.mult))
            nc.vector.tensor_reduce(two[:, :], prod[:, :, :], X, ALU.add).then_inc(summed, 1)
            dve.wait_ge(exp_ready, 1)
            link(nc.vector.tensor_tensor(lam[:, :], two[:, 1:2], two[:, 0:1], ALU.subtract))
            link(nc.vector.tensor_scalar(lam[:, :], lam[:, :], -LAM_INIT, None, ALU.add))
            link(nc.vector.tensor_scalar(subs[:, :], row(rows2, "subln"), 1.0 - LAM_INIT, None, ALU.mult))

        @block.scalar
        def _(act):
            act.wait_ge(summed, 1)
            nc.scalar.activation(two[:, :], two[:, :], ACT.Exp).then_inc(exp_ready, 1)


def prompt_attention(nc, KT, QT, V, lam, causal, ident, wide, bank, scratch):
    SC = HS ** -0.5
    flat = scratch[:, :, :].rearrange("p k t -> p (k t)")
    pr = flat[:, 0:4096].rearrange("p (r c t) -> p r c t", r=2, c=2)
    wT = flat[:, 4096:6144].rearrange("p (r j q) -> p r j q", r=2, j=NT)
    N = DH * NT
    with Stage(nc, "attn") as st:
        mx = st.sb("mx", [P, 2, 2])
        ls = st.sb("ls", [P, 2, 2])
        s_mm, mx_ready, exp_ready, w_ready, w_turned, wT_ready, o_mm, o_out, dve_chain = st.sems(
            "s_mm mx_ready exp_ready w_ready w_turned wT_ready o_mm o_out dve_chain")
        block = st.block()

        def score_banks(i, L):
            if i < 4:
                return wide[:, (i % 2) * 1024:(i % 2) * 1024 + 1024].rearrange("p (c t) -> p c t", c=2)[:, :, 0:L]
            return wide[:, 0:2048].rearrange("p (c t) -> p c t", c=2)[:, :, 0:L]

        @block.tensor
        def _(pe):
            def scores(k):
                h, i = divmod(k, NT)
                L = (i + 1) * P
                before = k if (i == 0 or i >= 4) else k - 1
                if before >= 1:
                    pe.wait_ge(exp_ready, before)
                s = score_banks(i, L)
                for a in range(0, L, 512):
                    b = min(a + 512, L)
                    for c in range(2):
                        d = slice(c * HS, (c + 1) * HS)
                        mm = pe.matmul(s[:, c, a:b], QT[d, h, i * P:(i + 1) * P], KT[d, h, a:b], start=True, stop=True)
                mm.then_inc(s_mm, 1)

            def values(k):
                h, i = divmod(k, NT)
                pe.wait_ge(wT_ready, k + 1)
                if k >= 2:
                    pe.wait_ge(o_out, k - 1)
                for j in range(i + 1):
                    mm = pe.matmul(bank[:, 6 + k % 2, 0:P], wT[:, k % 2, j, :], V[:, j, h * P:(h + 1) * P],
                                   start=(j == 0), stop=(j == i))
                mm.then_inc(o_mm, 1)

            scores(0)
            for k in range(N):
                if k + 1 < N:
                    scores(k + 1)
                pe.wait_ge(w_ready, k + 1)
                if k >= 1:
                    pe.wait_ge(wT_ready, k)
                for j in range(k % NT + 1):
                    mm = pe.transpose(bank[:, 4 + j // 4, (j % 4) * P:(j % 4 + 1) * P], pr[:, k % 2, 0, j * P:(j + 1) * P], ident[:, :])
                mm.then_inc(w_turned, 1)
                if k >= 1:
                    values(k - 1)
            values(N - 1)

        @block.scalar
        def _(act):
            def turned_out(k):
                L = (k % NT + 1) * P
                act.wait_ge(w_turned, k + 1)
                nc.scalar.copy(wT[:, k % 2, :, :].rearrange("p j q -> p (j q)")[:, 0:L], wide[:, 2048:2048 + L]).then_inc(wT_ready, 1)

            def out(k):
                h, i = divmod(k, NT)
                act.wait_ge(o_mm, k + 1)
                nc.scalar.copy(QT[:, h, i * P:(i + 1) * P], bank[:, 6 + k % 2, 0:P]).then_inc(o_out, 1)

            for k in range(N):
                if k >= 1:
                    turned_out(k - 1)
                i = k % NT
                L = (i + 1) * P
                s = score_banks(i, L)
                act.wait_ge(mx_ready, k + 1)
                for c in range(2):
                    ins = nc.scalar.activation(pr[:, k % 2, c, 0:L], s[:, c, :], ACT.Exp, scale=SC, bias=mx[:, k % 2, c:c + 1],
                                               accum_out=ls[:, k % 2, c:c + 1])
                ins.then_inc(exp_ready, 1)
                if k >= 2:
                    out(k - 2)
            turned_out(N - 1)
            out(N - 2)
            out(N - 1)

        @block.vector
        def _(dve):
            link = Chain(dve, dve_chain)

            def maxima(k):
                i = k % NT
                L = (i + 1) * P
                s = score_banks(i, L)
                dve.wait_ge(s_mm, k + 1)
                diag = s[:, :, i * P:L]
                link(nc.vector.tensor_tensor(diag, diag, bcast(causal.unsqueeze(1), [P, 2, P]), ALU.add))
                link(nc.vector.tensor_reduce(mx[:, k % 2, :], s, X, ALU.max))
                nc.vector.tensor_scalar(mx[:, k % 2, :], mx[:, k % 2, :], -SC, None, ALU.mult).then_inc(mx_ready, 1)

            def weights(k):
                L = (k % NT + 1) * P
                l = ls[:, k % 2, :]
                dve.wait_ge(exp_ready, k + 1)
                link(nc.vector.reciprocal(l, l))
                link(nc.vector.tensor_tensor(l[:, 1:2], l[:, 1:2], lam[:, :], ALU.mult))
                p0, p1 = pr[:, k % 2, 0, 0:L], pr[:, k % 2, 1, 0:L]
                link(nc.vector.tensor_scalar(p0, p0, l[:, 0:1], None, ALU.mult))
                nc.vector.scalar_tensor_tensor(out=p0, in0=p1, scalar=l[:, 1:2], in1=p0, op0=ALU.mult, op1=ALU.add).then_inc(w_ready, 1)

            maxima(0)
            for k in range(N):
                early = k + 1 < N and 1 <= (k + 1) % NT < 4
                if early:
                    maxima(k + 1)
                weights(k)
                if k + 1 < N and not early:
                    maxima(k + 1)


def prompt_outputs(nc, QT, subs, gates, ident, bank):
    with Stage(nc, "attno") as st:
        sq = st.sb("sq", [P, 2, NT, P])
        ss = st.sb("ss", [P, DH * NT])
        sq_ready, ss_ready, rs_ready, on_ready, turned, y_ready, dve_chain, act_chain = st.sems(
            "sq_ready ss_ready rs_ready on_ready turned y_ready dve_chain act_chain")
        block = st.block()

        def o(h):
            return QT[:, h, 0:SEQ].rearrange("p (n e) -> p n e", n=NT)

        @block.scalar
        def _(act):
            link = Chain(act, act_chain)
            for h in range(DH):
                if h >= 2:
                    act.wait_ge(ss_ready, h - 1)
                nc.scalar.activation(sq[:, h % 2, :, :], o(h), ACT.Square).then_inc(sq_ready, 1)
            act.wait_ge(ss_ready, DH)
            link(nc.scalar.activation(ss[:, :], ss[:, :], ACT.Ln, scale=1.0 / P, bias=eps_tile(nc)[:, 0:1]))
            nc.scalar.activation(ss[:, :], ss[:, :], ACT.Exp, scale=-0.5).then_inc(rs_ready, 1)

        @block.vector
        def _(dve):
            link = Chain(dve, dve_chain)

            def gated(j):
                h, half = divmod(j, 2)
                dve.wait_ge(turned, j + 1)
                y = gates[:, h, half * 512:(half + 1) * 512]
                nc.vector.scalar_tensor_tensor(out=y, in0=bank[:, j % 8, :], scalar=0.5, in1=y, op0=ALU.mult,
                                               op1=ALU.mult).then_inc(y_ready, 1)

            for h in range(DH):
                dve.wait_ge(sq_ready, h + 1)
                nc.vector.tensor_reduce(ss[:, h * NT:(h + 1) * NT], sq[:, h % 2, :, :], X, ALU.add).then_inc(ss_ready, 1)
            dve.wait_ge(rs_ready, 1)
            for h in range(DH):
                link(nc.vector.tensor_tensor(o(h), o(h), bcast(ss[:, h * NT:(h + 1) * NT].unsqueeze(2), [P, NT, P]), ALU.mult))
                nc.vector.tensor_tensor(o(h), o(h), bcast(subs[:, :].unsqueeze(1), [P, NT, P]), ALU.mult).then_inc(on_ready, 1)
                if h >= 1:
                    gated(2 * h - 2)
                    gated(2 * h - 1)
            gated(2 * DH - 2)
            gated(2 * DH - 1)

        @block.tensor
        def _(pe):
            for j in range(2 * DH):
                h, half = divmod(j, 2)
                pe.wait_ge(on_ready, h + 1)
                if j >= 8:
                    pe.wait_ge(y_ready, j - 7)
                for i in range(4):
                    n = 4 * half + i
                    mm = pe.transpose(bank[:, j % 8, i * P:(i + 1) * P], QT[:, h, n * P:(n + 1) * P], ident[:, :])
                mm.then_inc(turned, 1)


def sample_attention(nc, pages_d, cache_k, cache_v, KT, QT, V, lam, sub_col, gates, newmask, ident, ones, bank, wide, scratch):
    SC = HS ** -0.5
    C = DH * 2 * TS
    H3 = 3
    flat = scratch[:, :, :].rearrange("p k t -> p (k t)")
    KR, VR = 6, 12
    with Stage(nc, "samp") as st:
        kp = flat[:, 0:KR * 768].rearrange("p (r c) -> p r c", r=KR)
        at = KR * 768
        kT = flat[:, at:at + 4 * 384].rearrange("p (r h c) -> p r h c", r=2, h=2)
        s_sb = flat[:, at + 1536:at + 1536 + 9 * C].rearrange("p (g c) -> p g c", g=9)
        p_sb = flat[:, at + 2400:at + 2400 + 9 * C].rearrange("p (g c) -> p g c", g=9)
        w_sb = flat[:, at + 3264:at + 3264 + 432].rearrange("p (g c) -> p g c", g=9)
        vp = st.sb("vp", [P, VR, 768])
        qbd = st.sb("qbd", [P, DH, B, 2, TS])
        red = st.sb("red", [P, 2, C])
        mxT = st.sb("mxT", [P, 1])
        dg = st.sb("dg", [P, C])
        bc = st.sb("bc", [P, C])
        oT = st.sb("oT", [P, DH * NS])
        osq = st.sb("osq", [P, DH * NS])
        pages = st.sb("pages", [1, B * PAGES], I32)
        k_loaded = [st.sem(f"k_loaded{i}") for i in range(KR)]
        v_loaded = [st.sem(f"v_loaded{i}") for i in range(VR)]
        (pages_loaded, qbd_ready, turned, act_out, dve_out, s_mm, s_ready, max_ready, max_turned, dg_ready, bc_mm,
         sub_ready, exp_ready, sum_ready, sum_mm, w_ready, o_mm, sq_ready, oss_mm, rs_ready, k_used, dve_chain,
         act_chain) = st.sems(
            "pages_loaded qbd_ready turned act_out dve_out s_mm s_ready max_ready max_turned dg_ready bc_mm "
            "sub_ready exp_ready sum_ready sum_mm w_ready o_mm sq_ready oss_mm rs_ready k_used dve_chain act_chain")
        block = st.block()
        NPG = B * PAGES

        @block.sync
        def _(sp):
            sp.dma_start(pages[:, :], pages_d).then_inc(pages_loaded, 16)
            sp.wait_ge(pages_loaded, 16)
            for g in range(NPG):
                page = sp.value_load(pages[0:1, g:g + 1], min_val=0, max_val=cache_k.shape[0] - 1)
                if g >= KR:
                    sp.wait_ge(turned, 2 * (g - KR + 1))
                sp.dma_start(kp[:, g % KR, :], cache_k[bass.ds(page, 1), :, :].rearrange("a p c -> p (a c)")).then_inc(k_loaded[g % KR], 16)

        @block.gpsimd
        def _(pool):
            pool.wait_ge(pages_loaded, 16)
            for g in range(NPG):
                page = pool.value_load(pages[0:1, g:g + 1], min_val=0, max_val=cache_k.shape[0] - 1)
                if g >= VR:
                    pool.wait_ge(o_mm, (g - VR) // PAGES + 1)
                pool.dma_start(vp[:, g % VR, :], cache_v[bass.ds(page, 1), :, :].rearrange("a p c -> p (a c)")).then_inc(v_loaded[g % VR], 16)

        def s_at(b, g, a=0, n=C):
            at = (b % 2) * 1024 + (g // 5) * 512 + (g % 5) * C + a
            return wide[:, at:at + n]

        @block.tensor
        def _(pe):
            pe.wait_ge(qbd_ready, 1)

            def turn(j):
                g, half = divmod(j, 2)
                if half == 0:
                    pe.wait_ge(k_loaded[g % KR], 16 * (g // KR + 1))
                if g >= 1:
                    pe.wait_ge(dve_out if half else act_out, g)
                for i in range(H3):
                    mm = pe.transpose(bank[:, 4 + half, i * P:(i + 1) * P], kp[:, g % KR, (H3 * half + i) * P:(H3 * half + i + 1) * P],
                                      ident[:, :])
                mm.then_inc(turned, 1)

            def scores(j):
                g, half = divmod(j, 2)
                b, pg = divmod(g, PAGES)
                if pg == 0 and half == 0 and b >= 2:
                    pe.wait_ge(s_ready, b - 1)
                pe.wait_ge(dve_out if half else act_out, g + 1)
                for i in range(H3):
                    h = H3 * half + i
                    mm = pe.matmul(s_at(b, pg, h * 16, 16), kT[:, g % 2, half, i * P:(i + 1) * P],
                                   qbd[:, h, b, :, :].rearrange("p c t -> p (c t)"), start=True, stop=True)
                if half == 1:
                    mm.then_inc(k_used, 1)

            def new_scores(b):
                for h in range(DH):
                    mm = pe.matmul(s_at(b, PAGES, h * 16, 16)[0:NS, :], KT[:, h, SEQ:TT],
                                   qbd[:, h, b, :, :].rearrange("p c t -> p (c t)"), start=True, stop=True)
                mm.then_inc(s_mm, 1)

            def max_over_keys(b):
                pe.wait_ge(max_ready, b + 1)
                pe.transpose(bank[0:C, 6, 0:P], red[:, 0, :], ident[:, :]).then_inc(max_turned, 1)

            def spread_max(b):
                pe.wait_ge(dg_ready, b + 1)
                pe.matmul(bank[:, 6, P:P + C], ones[0:C, :], dg[0:C, :], start=True, stop=True).then_inc(bc_mm, 1)

            def sum_over_keys(b):
                pe.wait_ge(sum_ready, b + 1)
                pe.matmul(bank[:, 6, 2 * P:2 * P + C], ones[:, :], red[:, 1, :], start=True, stop=True).then_inc(sum_mm, 1)

            def values(b):
                pe.wait_ge(w_ready, b + 1)
                for pg in range(PAGES):
                    g = b * PAGES + pg
                    pe.wait_ge(v_loaded[g % VR], 16 * (g // VR + 1))
                for h in range(DH):
                    for pg in range(PAGES):
                        pe.matmul(bank[:, 7, h * NS + b * TS:h * NS + (b + 1) * TS], vp[:, (b * PAGES + pg) % VR, h * P:(h + 1) * P],
                                  w_sb[:, pg, h * TS:(h + 1) * TS], start=(pg == 0), stop=False)
                    mm = pe.matmul(bank[:, 7, h * NS + b * TS:h * NS + (b + 1) * TS], V[0:NS, NT, h * P:(h + 1) * P],
                                   w_sb[0:NS, PAGES, h * TS:(h + 1) * TS], start=False, stop=True)
                mm.then_inc(o_mm, 1)

            for b in range(B + 1):
                for pg in range(PAGES):
                    if b < B:
                        j = 2 * (b * PAGES + pg)
                        turn(j)
                        turn(j + 1)
                        if pg:
                            scores(j - 2)
                            scores(j - 1)
                    if b >= 1:
                        if pg == 1:
                            max_over_keys(b - 1)
                        if pg == 2:
                            spread_max(b - 1)
                        if pg == 5:
                            sum_over_keys(b - 1)
                if b < B:
                    scores(2 * (b * PAGES + PAGES) - 2)
                    scores(2 * (b * PAGES + PAGES) - 1)
                    new_scores(b)
                if b >= 1:
                    values(b - 1)
            pe.wait_ge(sq_ready, 1)
            pe.matmul(bank[:, 4, 0:DH * NS], ones[:, :], osq[:, :], start=True, stop=True).then_inc(oss_mm, 1)

        @block.scalar
        def _(act):
            link = Chain(act, act_chain)

            def exponentials(b):
                act.wait_ge(sub_ready, b + 1)
                nc.scalar.activation(p_sb[:, :, :], p_sb[:, :, :], ACT.Exp, scale=SC).then_inc(exp_ready, 1)

            for b in range(B):
                for pg in range(PAGES):
                    g = b * PAGES + pg
                    act.wait_ge(turned, 2 * g + 1)
                    if g >= 2:
                        act.wait_ge(k_used, g - 1)
                    nc.scalar.copy(kT[:, g % 2, 0, :], bank[:, 4, 0:H3 * P]).then_inc(act_out, 1)
                    if pg == 3 and b >= 1:
                        exponentials(b - 1)
            exponentials(B - 1)
            act.wait_ge(o_mm, B)
            link(nc.scalar.copy(oT[:, :], bank[:, 7, 0:DH * NS]))
            nc.scalar.activation(osq[:, :], bank[:, 7, 0:DH * NS], ACT.Square).then_inc(sq_ready, 1)
            act.wait_ge(oss_mm, 1)
            link(nc.scalar.activation(osq[:, :], bank[:, 4, 0:DH * NS], ACT.Ln, scale=1.0 / P, bias=eps_tile(nc)[:, 0:1]))
            nc.scalar.activation(osq[:, :], osq[:, :], ACT.Exp, scale=-0.5).then_inc(rs_ready, 1)

        @block.vector
        def _(dve):
            link = Chain(dve, dve_chain)
            link(nc.vector.memset(qbd[:, :, :, :, :], 0.0))
            for c in range(2):
                d = slice(c * HS, (c + 1) * HS)
                link(nc.vector.tensor_copy(qbd[d, :, :, c, :], QT[d, :, SEQ:TT].rearrange("p h (b t) -> p h b t", b=B)))
            dve.sem_inc(qbd_ready, 1)
            link(nc.vector.memset(s_sb[NS:P, PAGES, :], NEG))

            def collect(b):
                dve.wait_ge(s_mm, b + 1)
                if b >= 1:
                    dve.wait_ge(exp_ready, b)
                nc.vector.tensor_copy(s_sb[:, 0:5, :].rearrange("p g c -> p (g c)"), s_at(b, 0, 0, 5 * C))
                nc.vector.tensor_copy(s_sb[:, 5:PAGES, :].rearrange("p g c -> p (g c)"), s_at(b, 5, 0, 3 * C))
                link(nc.vector.tensor_tensor(s_sb[0:NS, PAGES, :].rearrange("p (a t) -> p a t", t=TS),
                                             s_at(b, PAGES)[0:NS, :].rearrange("p (a t) -> p a t", t=TS),
                                             bcast(newmask[0:NS, b * TS:(b + 1) * TS].unsqueeze(1), [NS, 2 * DH, TS]), ALU.add))
                dve.sem_inc(s_ready, 1)
                nc.vector.tensor_reduce(red[:, 0, :], s_sb[:, :, :].rearrange("p g c -> p c g"), X, ALU.max).then_inc(max_ready, 1)

            def diagonal(b):
                dve.wait_ge(max_turned, b + 1)
                link(nc.vector.tensor_reduce(mxT[0:C, :], bank[0:C, 6, 0:P], X, ALU.max))
                nc.vector.tensor_scalar(dg[0:C, :], ident[0:C, 0:C], mxT[0:C, 0:1], None, ALU.mult).then_inc(dg_ready, 1)

            def shifted(b):
                dve.wait_ge(bc_mm, b + 1)
                nc.vector.tensor_tensor(p_sb[:, :, :], s_sb[:, :, :], bcast(bank[:, 6, P:P + C].unsqueeze(1), [P, 9, C]),
                                        ALU.subtract).then_inc(sub_ready, 1)

            def sums(b):
                dve.wait_ge(exp_ready, b + 1)
                nc.vector.tensor_reduce(red[:, 1, :], p_sb[:, :, :].rearrange("p g c -> p c g"), X, ALU.add).then_inc(sum_ready, 1)

            def weights(b):
                dve.wait_ge(sum_mm, b + 1)
                link(nc.vector.reciprocal(bc[:, :], bank[:, 6, 2 * P:2 * P + C]))
                rc = bc[:, :].rearrange("p (h c t) -> p h c t", h=DH, c=2)
                link(nc.vector.tensor_scalar(rc[:, :, 1, :], rc[:, :, 1, :], lam[:, 0:1], None, ALU.mult))
                link(nc.vector.tensor_tensor(p_sb[:, :, :], p_sb[:, :, :], bcast(bc[:, :].unsqueeze(1), [P, 9, C]), ALU.mult))
                if b >= 1:
                    dve.wait_ge(o_mm, b)
                pc = p_sb[:, :, :].rearrange("p g (h c t) -> p (g h) c t", h=DH, c=2)
                nc.vector.tensor_tensor(w_sb[:, :, :].rearrange("p g (h t) -> p (g h) t", h=DH), pc[:, :, 0, :], pc[:, :, 1, :],
                                        ALU.add).then_inc(w_ready, 1)

            for b in range(B + 1):
                for pg in range(PAGES):
                    if b < B:
                        g = b * PAGES + pg
                        dve.wait_ge(turned, 2 * g + 2)
                        if g >= 2:
                            dve.wait_ge(k_used, g - 1)
                        nc.vector.tensor_copy(kT[:, g % 2, 1, :], bank[:, 5, 0:H3 * P]).then_inc(dve_out, 1)
                    if b >= 1:
                        if pg == 1:
                            diagonal(b - 1)
                        if pg == 2:
                            shifted(b - 1)
                        if pg == 4:
                            sums(b - 1)
                        if pg == 5:
                            weights(b - 1)
                if b < B:
                    collect(b)
            dve.wait_ge(rs_ready, 1)
            link(nc.vector.scalar_tensor_tensor(out=oT[:, :], in0=oT[:, :], scalar=sub_col, in1=osq[:, :], op0=ALU.mult, op1=ALU.mult))
            y = gates[:, 0:DH, SEQ:TT]
            link(nc.vector.scalar_tensor_tensor(out=y, in0=oT[:, :].rearrange("p (h t) -> p h t", h=DH), scalar=0.5 * (1.0 - LAM_INIT),
                                                in1=y, op0=ALU.mult, op1=ALU.mult))


def build(nc, ins, outs):
    with ExitStack() as ctx:
        def sb(name, shape, dt=F32):
            return ctx.enter_context(nc.sbuf_tensor(name, shape, dt))

        psum = ctx.enter_context(nc.psum_tensor("psum", [P, 4096], F32))
        wide = psum[:, :]
        bank = psum[:, :].rearrange("p (b c) -> p b c", b=8)
        for name in STORES:
            STORE_SIGNALS[name] = nc.alloc_semaphore(name)
        base = sb("base", [P, _CONST[0].shape[1]])
        vecs = sb("vecs", [P, NVEC])
        eps = sb("eps", [P, 2])
        _EPS["tile"] = eps
        ident = const_view([base], "ident")
        (y_p, y_s, st_p, sh_p, k_p, v_p, mk_p, mv_p, st_s, sh_s, k_s, v_s) = outs
        i = ins
        load_tensors(nc, "cst", [(base[:, :], i["const0"]), (vecs[:, :], i["vecs"])], [(eps[:, 0:1], EPS), (eps[:, 1:2], LNX_EPS)])
        y_d = nc.dram_tensor("gated", (P, KC, TT), F32).ap()
        xT = sb("xT", [P, KC, TX])
        with nc.sbuf_tensor("x_rows", [P, NTILE, D], F32) as x_sb:
            norm_and_turn(nc, "norm0", x_sb, xT, bank, ident, i["norm_g0"], i["shift"], (sh_p, sh_s), (i["x_p"], i["x_s"]))
        with ExitStack() as c2:
            lora = c2.enter_context(nc.sbuf_tensor("lora", [P, TT], F32))
            up = c2.enter_context(nc.sbuf_tensor("up", [P, 6 * P], F32))
            omu = c2.enter_context(nc.sbuf_tensor("omu", [P, 19], F32))
            masks = c2.enter_context(nc.sbuf_tensor("masks", [P, _CONST[1].shape[1]], F32))
            rows = c2.enter_context(nc.sbuf_tensor("rows", [P, NROW], F32))
            const = [base, masks]
            load_tensors(nc, "cst1", [(masks[:, :], i["const1"]), (rows[:, :], i["rows"].partition_broadcast(P))])
            lora_inputs(nc, i["w_in"], i["w_up"], i["a_up"], vecs, omu, xT, wide, lora, up)
            rwkv_pairs(nc, i["w_in"], i["state"], st_p, st_s, const, vecs, rows, omu, xT, wide, bank, lora, up, y_d)
        late = sb("late", [P, _CONST[2].shape[1]])
        const = [base, None, late]
        rows2 = sb("rows2", [P, NROW2])
        ones = sb("ones", [P, P])
        mkT = sb("mkT", [P, 2, 2, MEMT])
        mv = sb("mv", [P, 2, 2, MEMT])
        load_tensors(nc, "cst2", [(late[:, :], i["const2"]), (rows2[:, :], i["rows2"].partition_broadcast(P))], [(ones[:, :], 1.0)])
        memory_keys(nc, i["mem"], i["mem_w_kv"], vecs, rows2, ident, bank, mkT, mv, mk_p, mv_p)
        h_d = nc.dram_tensor("residual", (TT, D), F32).ap()
        h_tiles = (h_d[0:SEQ, :], h_d[SEQ:TT, :])
        with ExitStack() as c1:
            yT = c1.enter_context(nc.sbuf_tensor("yT0", [P, KC, TT], F32))
            with nc.sbuf_tensor("mqT0", [P, 2, TT], F32) as mqT:
                gates_and_queries(nc, "gq0", i["w_in"], [19, 20, 27, 28], xT, None, vecs, vec(vecs, "mq0"), const, wide,
                                  mqT, yT[:, 6:8, :])
                memory_attention(nc, "mem0", 0, mqT, mkT, mv, i["cmk"], i["cmv"], yT[:, 6:8, :], const, ones, bank)
            with nc.sbuf_tensor("h0", [P, NTILE, D], F32) as h:
                out_project(nc, "out0", i["w_out"][0], yT, h, bank, y_load=y_d, h_load=(i["x_p"], i["x_s"]), h_store=h_tiles)
                norm_and_turn(nc, "norm1", h, xT, bank, ident, None)
        KT = sb("KT", [P, DH, TT])
        QT = sb("QT", [P, DH, TT])
        V = sb("V", [P, NTILE, 768])
        keys_values_queries(nc, i["kv_w"], i["b_q"], vecs, rows2, const, ident, xT, bank, KT, QT, V, (k_p, k_s), (v_p, v_s))
        yT = sb("yT1", [P, KC, TT])
        lam = sb("lam", [P, 1])
        subs = sb("subs", [P, P])
        lambda_row(nc, rows2, lam, subs)
        with nc.sbuf_tensor("mqT1", [P, 2, TT], F32) as mqT:
            gates_and_queries(nc, "gq1", i["b_in"], list(range(10)), xT, vec(vecs, "bg"), vecs, vec(vecs, "mq1"), const, wide,
                              mqT, yT[:, :, :])
            memory_attention(nc, "mem1", 1, mqT, mkT, mv, i["cmk"], i["cmv"], yT[:, 6:8, :], const, ones, bank, xT)
        prompt_attention(nc, KT, QT, V, lam, const_view(const, "causal"), ident, wide, bank, xT)
        sample_attention(nc, i["pages"], i["cache_k"], i["cache_v"], KT, QT, V, lam, vec(vecs, "subc"), yT,
                         const_view(const, "newmask"), ident, ones, bank, wide, xT)
        prompt_outputs(nc, QT, subs, yT, ident, bank)
        out_project(nc, "out1", i["w_out"][1], yT, None, bank, h_load=h_tiles, h_store=(y_p, y_s), scratch=xT)


_OUTS = [(SEQ, D), (NS, D), (HEADS, HS, HS), (1, D), (SEQ, 768), (SEQ, 768), (2, MEMT, 256), (2, MEMT, 256),
         (B, HEADS, HS, HS), (B, D), (NS, 768), (NS, 768)]
_SHAPES = [(1, SEQ, D), (B, TS, D), (1, 1, HEADS, HS, HS), (1, 1, D), (1, SEQ, 6, 2, 64), (1, SEQ, 6, 128),
           (2, 1, MEMT, 4, 64), (2, 1, MEMT, 4, 64), (1, B, HEADS, HS, HS), (1, B, D), (B, TS, 6, 2, 64), (B, TS, 6, 128)]


def _chunks(w, width):
    k, c = w.shape
    return np.ascontiguousarray(w.reshape(KC, P, c // width, width).transpose(2, 1, 0, 3)).reshape(c // width, P, KC * width)


def _layout(a):
    f = {k: np.asarray(v) for k, v in a.items()}

    def cols(v):
        return v.reshape(-1, P).T

    twice = lambda v: np.concatenate([v, v])
    vecs = np.concatenate([
        cols(f["a_mu_first"]), cols(f["a_w0"][0]), cols(f["a_a0"][0]), cols(f["a_k_k"][0]), cols(f["a_k_a"][0]),
        cols(f["a_r_k"][0]), cols(twice(f["mem_q_g"][0])), cols(twice(f["mem_q_g"][1])), cols(f["mem_norm_g"][0]),
        cols(f["mem_norm_g"][1]), cols(f["kv_norm_g"]), cols(f["norm_g"][1]), cols(f["b_subln_g"][0])], 1)
    rows = np.concatenate([f["a_lnx_g"][0], f["a_lnx_b"][0], f["kv_k_g"], f["b_q_g"][0], f["b_subln_g"][0],
                           f["b_lam"][0].reshape(-1), f["mem_k_g"][0], f["mem_k_g"][1]])
    b_in = f["b_w_in"][0]
    return {
        "const0": _CONST[0], "const1": _CONST[1], "const2": _CONST[2], "vecs": vecs, "rows": rows[:NROW], "rows2": rows[NROW:], "norm_g0": f["norm_g"][0],
        "x_p": f["x_prompt"][0], "x_s": f["x_sample"].reshape(NS, D), "mem": f["mem_prompt"][0],
        "shift": f["state_shift"][0], "state": f["state_wkv"][0],
        "w_in": _chunks(f["a_w_in_first"], P), "w_up": f["a_w_up"][0], "a_up": f["a_a_up"][0],
        "mem_w_kv": np.concatenate([_chunks(f["mem_w_kv"][layer], 512) for layer in range(2)]),
        "w_out": np.concatenate([_chunks(f["w_out"][layer], D) for layer in range(2)]),
        "kv_w": _chunks(f["kv_w"], 384), "b_q": _chunks(b_in[:, 0:768], 384), "b_in": _chunks(b_in[:, 768:], P),
        "cache_k": f["cache_k"].reshape(-1, P, 768), "cache_v": f["cache_v"].reshape(-1, P, 768),
        "cmk": f["cache_mem_k"].reshape(2, B, MEMT, 256), "cmv": f["cache_mem_v"].reshape(2, B, MEMT, 256),
        "pages": f["page_table"].reshape(1, -1),
    }


def kernel(**inputs):
    import concourse.bacc as _bacc
    from concourse.bass_utils import run_bass_kernel_spmd as _run

    nc = _bacc.Bacc("TRN2", target_bir_lowering=False, num_devices=1)
    arrays, ins = {}, {}
    for name, a in _layout(inputs).items():
        a = np.ascontiguousarray(a)
        arrays[f"in_{name}"] = a
        ins[name] = nc.dram_tensor(f"in_{name}", a.shape, mybir.dt.from_np(a.dtype), kind="ExternalInput").ap()
    outs = [nc.dram_tensor(f"out_{n}", shape, F32, kind="ExternalOutput").ap() for n, shape in enumerate(_OUTS)]
    build(nc, ins, outs)
    r = _run(nc, [arrays], core_ids=[0])
    return tuple(np.asarray(r.results[0][f"out_{n}"]).reshape(shape) for n, shape in enumerate(_SHAPES))
```

```python
import math
from contextlib import ExitStack

import numpy as np

import concourse.bass as bass
from concourse import mybir

F32 = mybir.dt.float32
I32 = mybir.dt.int32
ALU = mybir.AluOpType
ACT = mybir.ActivationFunctionType
X = mybir.AxisListType.X

P = 128
D = 1024
KC = D // P
SEQ = 1024
NT = SEQ // P
B = 8
TS = 8
NS = B * TS
TT = SEQ + NS
TX = TT + B
NTILE = NT + 1
HEADS = 12
HS = 64
PAIRS = HEADS // 2
NCH = 29
DH = 6
PAGES = 8
MEMT = 256
W_GATE = math.exp(-0.5)
EPS = 1e-6
LNX_EPS = 64e-5
NEG = -1e30
LAM_INIT = 0.8 - 0.6 * math.exp(-0.3)
LEVELS = [2, 4, 8, 16, 32, 64]
COLS = [(0, 512), (512, 1024), (1024, TX)]


def rows_of(n):
    return P if n < NT else NS


def make_constants():
    t = np.arange(P)
    parts, at = {}, 0
    out = []

    def put(name, a):
        nonlocal at
        a = np.asarray(a, np.float32).reshape(a.shape[0], -1)
        full = np.zeros((P, a.shape[1]), np.float32)
        full[:a.shape[0]] = a
        parts[name] = (at, a.shape[1])
        at += a.shape[1]
        out.append(full)

    s_, t_ = t[:, None], t[None, :]
    put("ident", np.eye(P))
    strict, incl = (s_ < t_), (s_ <= t_)
    put("headsum", s_ // HS == t_ // HS)
    early = at
    put("mask4", np.stack([strict, incl, strict, incl], 1))
    own = (s_[:NS] // TS == t_[:, :NS] // TS)
    put("mask4s", np.stack([strict[:NS, :NS] & own, incl[:NS, :NS] & own] * 2, 1))
    put("pair1", (s_ // 2 == t_ // 2) & (s_ < t_))
    for b in LEVELS:
        put(f"pair{b}", (s_ // b % 2 == 1) & (t_ // b == s_ // b - 1))
    put("headsel", s_ // HS == np.arange(2)[None, :])
    keep = np.ones(TT)
    keep[0:SEQ:P] = 0
    keep[SEQ::TS] = 0
    put("keep", np.broadcast_to(keep, (P, TT)))
    put("ownseq", (np.arange(NS)[:, None] // TS == np.arange(B)[None, :]))
    own_cols = (np.arange(B)[:, None] == (np.arange(NS) // TS)[None, :])
    put("owncols", np.broadcast_to(own_cols[None], (P, B, NS)))
    late = at
    put("causal", np.where(s_ >= t_, 0.0, NEG))
    r_ = np.arange(DH * 2 * TS)[:, None]
    c_, t8 = r_ // TS % 2, r_ % TS
    put("isc", c_ == np.arange(2)[None, :])
    put("join", r_ // (2 * TS) * TS + t8 == np.arange(DH * TS)[None, :])
    put("own8", np.where(np.arange(TS)[None, :] <= t8, 0.0, NEG))
    half = 32
    inv = 10000.0 ** (-np.arange(half, dtype=np.float32) / half)
    pos = np.zeros((NTILE, P), np.float32)
    pos[:NT] = np.arange(SEQ).reshape(NT, P)
    pos[NT, :NS] = SEQ + np.arange(NS) % TS
    ang = (pos.T[:, :, None] * inv).astype(np.float32)
    put("cos", np.cos(ang))
    put("sin", np.sin(ang))
    every = np.concatenate(out, 1)
    cuts = [0, early, late, at]
    where = {}
    for name, (a, w) in parts.items():
        part = max(i for i in range(3) if cuts[i] <= a)
        where[name] = (part, a - cuts[part], w)
    return [every[:, cuts[i]:cuts[i + 1]] for i in range(3)], where


_CONST, _AT = make_constants()

_VEC = {}
_n = 0
for _name, _w in (("mu", 19), ("w0", 6), ("a0", 6), ("k_k", 6), ("k_a", 6), ("r_k", 6), ("mq0", 1), ("mq1", 1),
                  ("memg0", 8), ("memg1", 8), ("kvg", 8), ("bg", 8), ("subc", 1)):
    _VEC[_name] = (_n, _w)
    _n += _w
NVEC = _n
_ROW = {}
_n = 0
for _name, _w in (("lnx_g", 768), ("lnx_b", 768), ("k_g", 64), ("q_g", 64), ("subln", 128), ("lam", 256),
                  ("memk0", 64), ("memk1", 64)):
    _ROW[_name] = (_n if _n < 1536 else _n - 1536, _w)
    _n += _w
NROW = 1536
NROW2 = _n - NROW


class Chain:

    def __init__(self, eng, sem):
        self.eng, self.sem, self.n = eng, sem, 0

    def __call__(self, ins):
        self.n += 1
        ins.then_inc(self.sem, 1)
        self.eng.wait_ge(self.sem, self.n)


STORE_SIGNALS = {}
STORES = ("norm0_shift_stored rwkv_stored rwkv_y_stored memkv_stored out0_stored kvq_k_stored kvq_v_stored "
          "out1_stored").split()


class Stage:

    def __init__(self, nc, name):
        self.nc, self.name = nc, name

    def __enter__(self):
        self.ctx = ExitStack()
        self.signals = []
        return self

    def __exit__(self, *a):
        self.ctx.__exit__(*a)
        if a[0] is None:
            self.nc.clear_and_free_semaphores(self.signals)
            self.nc.all_engine_barrier()

    def sb(self, name, shape, dt=F32):
        return self.ctx.enter_context(self.nc.sbuf_tensor(f"{self.name}_{name}", shape, dt))

    def sem(self, name):
        if "stored" in name:
            return STORE_SIGNALS[f"{self.name}_{name}"]
        self.signals.append(self.nc.alloc_semaphore(f"{self.name}_{name}"))
        return self.signals[-1]

    def sems(self, names):
        return [self.sem(x) for x in names.split()]

    def block(self):
        return self.ctx.enter_context(self.nc.Block())


def bcast(ap, shape):
    return ap.broadcast_to(shape)


def load_tensors(nc, name, pairs, fills=()):
    with Stage(nc, name) as st:
        loaded, filled = st.sems("loaded filled")
        block = st.block()

        @block.sync
        def _(sp):
            for dst, src in pairs:
                sp.dma_start(dst, src).then_inc(loaded, 16)
            sp.wait_ge(loaded, 16 * len(pairs))

        if fills:
            @block.vector
            def _(dve):
                for dst, value in fills:
                    nc.vector.memset(dst, value).then_inc(filled, 1)


def norm_and_turn(nc, name, x_sb, xT, bank, ident, gain, state_shift=None, shifts=None, source=None, ahead=()):
    with Stage(nc, name) as st:
        sq = st.sb("sq", [P, 2, D])
        scaled = st.sb("scaled", [P, 2, D]) if gain is None else None
        ss = st.sb("ss", [P, NTILE])
        rstd = st.sb("rstd", [P, NTILE])
        grow = st.sb("grow", [P, D]) if gain is not None else None
        x_loaded = [st.sem(f"x_loaded{n}") for n in range(NTILE)]
        (ss_clear, rstd_ready, xn_ready, turned, act_out, dve_out, act_chain, g_loaded, ahead_loaded) = st.sems(
            "ss_clear rstd_ready xn_ready turned act_out dve_out act_chain g_loaded ahead_loaded")
        shift_stored = st.sem("shift_stored") if shifts is not None else None
        block = st.block()
        last = NS + (B if state_shift is not None else 0)

        @block.sync
        def _(sp):
            if source is not None:
                x_prompt, x_sample = source
                for n in range(NT):
                    sp.dma_start(x_sb[:, n, :], x_prompt[n * P:(n + 1) * P, :]).then_inc(x_loaded[n], 16)
                sp.dma_start(x_sb[0:NS, NT, :], x_sample).then_inc(x_loaded[NT], 16)
                sp.dma_start(x_sb[NS:last, NT, :], state_shift).then_inc(x_loaded[NT], 16)
                sp.dma_start(grow[:, :], gain.partition_broadcast(P)).then_inc(g_loaded, 16)
                for dst, src in ahead:
                    sp.dma_start(dst, src).then_inc(ahead_loaded, 16)
                shift_p, shift_s = shifts
                sp.wait_ge(xn_ready, NTILE)
                sp.dma_start(shift_p, x_sb[P - 1:P, NT - 1, :]).then_inc(shift_stored, 16)
                for b in range(B):
                    sp.dma_start(shift_s[b:b + 1, :], x_sb[b * TS + TS - 1:b * TS + TS, NT, :]).then_inc(shift_stored, 16)
                sp.wait_ge(shift_stored, 16 * (B + 1))
                if ahead:
                    sp.wait_ge(ahead_loaded, 16 * len(ahead))

        @block.scalar
        def _(act):
            link = Chain(act, act_chain)
            act.wait_ge(ss_clear, 1)
            for n in range(NTILE):
                r = rows_of(n)
                if source is not None:
                    act.wait_ge(x_loaded[n], 16 if n < NT else 32)
                link(nc.scalar.activation(sq[0:r, n % 2, :], x_sb[0:r, n, :], ACT.Square, accum_out=ss[0:r, n:n + 1]))
            link(nc.scalar.activation(ss[:, :], ss[:, :], ACT.Ln, scale=1.0 / D, bias=eps_tile(nc)[:, 0:1]))
            nc.scalar.activation(rstd[:, :], ss[:, :], ACT.Exp, scale=-0.5).then_inc(rstd_ready, 1)
            for n in range(NTILE):
                act.wait_ge(turned, 2 * n + 1)
                c = last if n == NT else P
                nc.scalar.copy(xT[:, 0:4, n * P:n * P + c],
                               bank[:, (2 * n) % 8, :].rearrange("p (k t) -> p k t", k=4)[:, :, 0:c]).then_inc(act_out, 1)

        @block.vector
        def _(dve):
            def evac(n):
                dve.wait_ge(turned, 2 * n + 2)
                c = last if n == NT else P
                nc.vector.tensor_copy(xT[:, 4:8, n * P:n * P + c],
                                      bank[:, (2 * n + 1) % 8, :].rearrange("p (k t) -> p k t", k=4)[:, :, 0:c]
                                      ).then_inc(dve_out, 1)

            nc.vector.memset(ss[:, :], 1.0).then_inc(ss_clear, 1)
            dve.wait_ge(rstd_ready, 1)
            if gain is not None:
                dve.wait_ge(g_loaded, 16)
            for n in range(NTILE):
                r = rows_of(n)
                if gain is not None:
                    if source is not None:
                        dve.wait_ge(x_loaded[n], 16 if n < NT else 32)
                    nc.vector.scalar_tensor_tensor(out=x_sb[0:r, n, :], in0=x_sb[0:r, n, :], scalar=rstd[0:r, n:n + 1],
                                                   in1=grow[0:r, :], op0=ALU.mult, op1=ALU.mult).then_inc(xn_ready, 1)
                else:
                    if n >= 2:
                        dve.wait_ge(turned, 2 * n - 2)
                    nc.vector.tensor_scalar(scaled[0:r, n % 2, :], x_sb[0:r, n, :], rstd[0:r, n:n + 1], None,
                                            ALU.mult).then_inc(xn_ready, 1)
                if n >= 1:
                    evac(n - 1)
            evac(NTILE - 1)

        @block.tensor
        def _(pe):
            for n in range(NTILE):
                pe.wait_ge(xn_ready, n + 1)
                r = last if n == NT else P
                for half in range(2):
                    j = 2 * n + half
                    if n >= 4:
                        pe.wait_ge(dve_out if half else act_out, n - 3)
                    for k in range(4):
                        kk = 4 * half + k
                        src = x_sb[0:r, n, kk * P:(kk + 1) * P] if gain is not None else \
                            scaled[0:r, n % 2, kk * P:(kk + 1) * P]
                        mm = pe.transpose(bank[:, j % 8, k * P:k * P + r], src, ident[0:r, 0:r])
                    mm.then_inc(turned, 1)


_EPS = {}


def eps_tile(nc):
    return _EPS["tile"]


def memory_keys(nc, mem, w_kv, vecs, rows, ident, bank, mkT, mv, out_k, out_v):
    with Stage(nc, "memkv") as st:
        x = st.sb("x", [P, 2, D])
        sq = st.sb("sq", [P, D])
        ss = st.sb("ss", [P, 2])
        rstd = st.sb("rstd", [P, 2])
        xT = st.sb("xT", [P, KC, MEMT])
        xg = st.sb("xg", [P, 2, KC, MEMT])
        w = st.sb("w", [P, 2, KC, 512])
        kss = st.sb("kss", [P, 16])
        krstd = st.sb("krstd", [P, 16])
        kn = st.sb("kn", [P, 4, MEMT])
        x_loaded, = st.sems("x_loaded")
        w_loaded = [st.sem(f"w_loaded{layer}") for layer in range(2)]
        (rstd_ready, xh_ready, turned, xT_ready, xg_ready, kv_ready, sq_ready, kss_ready, krstd_ready, kn_ready,
         v_ready, kn_turned, act_chain, dve_chain, stored) = st.sems(
            "rstd_ready xh_ready turned xT_ready xg_ready kv_ready sq_ready kss_ready krstd_ready kn_ready v_ready "
            "kn_turned act_chain dve_chain stored")
        block = st.block()

        @block.sync
        def _(sp):
            for n in range(2):
                sp.dma_start(x[:, n, :], mem[n * P:(n + 1) * P, :]).then_inc(x_loaded, 16)
            for layer in range(2):
                sp.dma_start(w[:, layer, :, :].rearrange("p k c -> p (k c)"), w_kv[layer]).then_inc(w_loaded[layer], 16)
            for j in range(4):
                layer, n = j // 2, j % 2
                sp.wait_ge(v_ready, j + 1)
                sp.dma_start(out_v[layer, n * P:(n + 1) * P, :], mv[:, layer, n, :]).then_inc(stored, 16)
            for j in range(4):
                layer, n = j // 2, j % 2
                sp.wait_ge(kn_ready, j + 1)
                sp.dma_start(out_k[layer, n * P:(n + 1) * P, :], kn[:, j, :]).then_inc(stored, 16)
            sp.wait_ge(stored, 16 * 8)

        @block.scalar
        def _(act):
            link = Chain(act, act_chain)
            act.wait_ge(x_loaded, 32)
            for n in range(2):
                link(nc.scalar.activation(sq[:, :], x[:, n, :], ACT.Square, accum_out=ss[:, n:n + 1]))
            link(nc.scalar.activation(ss[:, :], ss[:, :], ACT.Ln, scale=1.0 / D, bias=eps_tile(nc)[:, 0:1]))
            nc.scalar.activation(rstd[:, :], ss[:, :], ACT.Exp, scale=-0.5).then_inc(rstd_ready, 1)
            for j in range(4):
                act.wait_ge(turned, j + 1)
                n, half = j // 2, j % 2
                nc.scalar.copy(xT[:, 4 * half:4 * half + 4, n * P:(n + 1) * P],
                               bank[:, j, :].rearrange("p (k t) -> p k t", k=4)).then_inc(xT_ready, 1)
            for j in range(4):
                act.wait_ge(kv_ready, j + 1)
                if j >= 1:
                    act.wait_ge(kss_ready, j)
                nc.scalar.activation(sq[:, 0:MEMT], bank[:, 4 + j, 0:MEMT], ACT.Square).then_inc(sq_ready, 1)
            act.wait_ge(kss_ready, 4)
            link(nc.scalar.activation(krstd[:, :], kss[:, :], ACT.Ln, scale=1.0 / HS, bias=eps_tile(nc)[:, 0:1]))
            nc.scalar.activation(krstd[:, :], krstd[:, :], ACT.Exp, scale=-0.5).then_inc(krstd_ready, 1)
            for j in range(4):
                act.wait_ge(kn_turned, j + 1)
                layer, n = j // 2, j % 2
                link(nc.scalar.copy(mkT[:, layer, :, n * P:(n + 1) * P],
                                    bank[:, j, 0:MEMT].rearrange("p (c t) -> p c t", c=2)))

        @block.vector
        def _(dve):
            link = Chain(dve, dve_chain)
            dve.wait_ge(rstd_ready, 1)
            for n in range(2):
                nc.vector.tensor_scalar(x[:, n, :], x[:, n, :], rstd[:, n:n + 1], None, ALU.mult).then_inc(xh_ready, 1)
            dve.wait_ge(xT_ready, 4)
            for layer in range(2):
                g = vec(vecs, f"memg{layer}")
                nc.vector.tensor_tensor(xg[:, layer, :, :], xT[:, :, :], bcast(g.unsqueeze(2), [P, KC, MEMT]),
                                        ALU.mult).then_inc(xg_ready, 1)
            for j in range(4):
                layer, n = j // 2, j % 2
                dve.wait_ge(sq_ready, j + 1)
                nc.vector.tensor_copy(mv[:, layer, n, :], bank[:, 4 + j, MEMT:2 * MEMT]).then_inc(v_ready, 1)
                nc.vector.tensor_reduce(kss[:, 4 * j:4 * j + 4], sq[:, 0:MEMT].rearrange("p (h d) -> p h d", h=4), X,
                                        ALU.add).then_inc(kss_ready, 1)
            dve.wait_ge(krstd_ready, 1)
            for j in range(4):
                kv = kn[:, j, :].rearrange("p (h d) -> p h d", h=4)
                link(nc.vector.tensor_tensor(kv, bank[:, 4 + j, 0:MEMT].rearrange("p (h d) -> p h d", h=4),
                                             bcast(krstd[:, 4 * j:4 * j + 4].unsqueeze(2), [P, 4, HS]), ALU.mult))
                nc.vector.tensor_tensor(kv, kv, bcast(row(rows, f"memk{j // 2}").unsqueeze(1), [P, 4, HS]),
                                        ALU.mult).then_inc(kn_ready, 1)

        @block.tensor
        def _(pe):
            for j in range(4):
                n, half = j // 2, j % 2
                pe.wait_ge(xh_ready, n + 1)
                for k in range(4):
                    kk = 4 * half + k
                    mm = pe.transpose(bank[:, j, k * P:(k + 1) * P], x[:, n, kk * P:(kk + 1) * P], ident[:, :])
                mm.then_inc(turned, 1)
            for j in range(4):
                layer, n = j // 2, j % 2
                pe.wait_ge(xg_ready, layer + 1)
                pe.wait_ge(w_loaded[layer], 16)
                for k in range(KC):
                    mm = pe.matmul(bank[:, 4 + j, :], xg[:, layer, k, n * P:(n + 1) * P], w[:, layer, k, :],
                                   start=(k == 0), stop=(k == KC - 1))
                mm.then_inc(kv_ready, 1)
            for j in range(4):
                pe.wait_ge(kn_ready, j + 1)
                for c in range(2):
                    mm = pe.transpose(bank[:, j, c * P:(c + 1) * P], kn[:, j, c * P:(c + 1) * P], ident[:, :])
                mm.then_inc(kn_turned, 1)


def vec(vecs, name, i=None):
    at, w = _VEC[name]
    return vecs[:, at:at + w] if i is None else vecs[:, at + i:at + i + 1]


def row(rows, name, a=0, b=None):
    at, w = _ROW[name]
    return rows[:, at + a:at + (w if b is None else b)]


def const_view(const, name):
    part, at, w = _AT[name]
    return const[part][:, at:at + w]


def project(pe, wide, base, w, xT, width=TX, k_outer=False):
    for a, b in COLS:
        b = min(b, width)
        for k in range(KC):
            mm = pe.matmul(wide[:, base + a:base + b], w[:, k, :], xT[:, k, a:b], start=(k == 0), stop=(k == KC - 1))
    return mm


def mix_scaled(nc, ps, mu, prev, prev_s):
    nc.scalar.activation(prev[:, 1:SEQ + 1], ps[:, 0:SEQ], ACT.Copy, scale=mu)
    nc.scalar.activation(prev_s[:, :, 1:TS + 1], ps[:, SEQ:TT].rearrange("p (b t) -> p b t", b=B), ACT.Copy, scale=mu)
    return nc.scalar.activation(prev_s[:, :, 0], ps[:, TT:TX], ACT.Copy, scale=mu)


def mix_rest(nc, out, ps, omu, prev, prev_s):
    nc.vector.scalar_tensor_tensor(out=out[:, 0:SEQ], in0=ps[:, 0:SEQ], scalar=omu, in1=prev[:, 0:SEQ],
                                   op0=ALU.mult, op1=ALU.add)
    return nc.vector.scalar_tensor_tensor(out=out[:, SEQ:TT].rearrange("p (b t) -> p b t", b=B),
                                          in0=ps[:, SEQ:TT].rearrange("p (b t) -> p b t", b=B), scalar=omu,
                                          in1=prev_s[:, :, 0:TS], op0=ALU.mult, op1=ALU.add)


def lora_inputs(nc, w_in, w_up_d, a_up_d, vecs, omu, xT, wide, lora, up):
    with Stage(nc, "lora") as st:
        w = st.sb("w", [P, KC, P])
        prev = st.sb("prev", [P, SEQ + 1])
        prev_s = st.sb("prev_s", [P, B, TS + 1])
        loaded, up_zeroed, up_loaded, projected, scaled, mixed, dve_chain, act_chain = st.sems(
            "loaded up_zeroed up_loaded projected scaled mixed dve_chain act_chain")
        block = st.block()

        @block.sync
        def _(sp):
            sp.dma_start(w[:, :, :].rearrange("p k c -> p (k c)"), w_in[18]).then_inc(loaded, 16)
            sp.wait_ge(up_zeroed, 1)
            sp.dma_start(up[0:HS, 0, :], w_up_d).then_inc(up_loaded, 16)
            sp.dma_start(up[HS:P, 1, :], a_up_d).then_inc(up_loaded, 16)
            sp.wait_ge(up_loaded, 32)

        @block.tensor
        def _(pe):
            pe.wait_ge(loaded, 16)
            project(pe, wide, 0, w, xT).then_inc(projected, 1)

        @block.scalar
        def _(act):
            act.wait_ge(projected, 1)
            mix_scaled(nc, wide, vec(vecs, "mu", 18), prev, prev_s).then_inc(scaled, 1)
            act.wait_ge(mixed, 1)
            Chain(act, act_chain)(nc.scalar.activation(lora[0:HS, :], lora[0:HS, :], ACT.Tanh))

        @block.vector
        def _(dve):
            link = Chain(dve, dve_chain)
            nc.vector.memset(up[:, :, :], 0.0).then_inc(up_zeroed, 1)
            link(nc.vector.memset(prev[:, 0:1], 0.0))
            link(nc.vector.tensor_scalar(omu[:, :], vec(vecs, "mu"), -1.0, 1.0, ALU.mult, ALU.add))
            dve.wait_ge(scaled, 1)
            mix_rest(nc, lora, wide, omu[:, 18:19], prev, prev_s).then_inc(mixed, 1)


UNITS = 2 * NT
GROUPS = UNITS // 4
STEPS = [(lev, g) for lev in range(len(LEVELS)) for g in range(GROUPS + 1) if g < GROUPS or LEVELS[lev] < TS]


def rwkv_pairs(nc, w_in, state_d, new_state_p, new_state_s, const, vecs, rows, omu, xT, wide, bank, lora, up, y_d):
    ident = const_view(const, "ident")
    with Stage(nc, "rwkv") as st:
        w = st.sb("w", [P, 2, KC, P])
        prev_s = st.sb("prev_s", [P, B, TS + 1])
        turns = [[st.sb(f"turn{i}{j}", [P, NTILE * P if j < 2 else TT]) for j in range(3)] for i in range(2)]
        aT = st.sb("aT", [P, TT])
        gT = st.sb("gT", [P, TT])
        sig_pr = st.sb("sig_pr", [P, TT])
        dec_mm = st.sb("dec_mm", [P, 5, 4, P])
        be_dd = st.sb("be_dd", [P, 5, 4, P])
        arT = st.sb("arT", [P, NTILE, 2, P])
        tok = st.sb("tok", [P, 2, NTILE, P])
        v_tok = st.sb("v_tok", [P, NTILE, 4, HS])
        ends_s = st.sb("ends_s", [P, B])
        am = st.sb("am", [P, UNITS, 4, P])
        ams = st.sb("ams", [NS, 2, 4, NS])
        ee = st.sb("ee", [P, GROUPS + 1, 4, P])
        stat = st.sb("stat", [P, 4, 2 * NTILE])
        xscale = st.sb("xscale", [P, NT])
        pm = st.sb("pm", [P, NT])
        hv = st.sb("hv", [P, 4, PAIRS])
        s0 = st.sb("s0", [P, B, P])
        s1 = ee[:, 0:2, :, :].rearrange("p g u t -> p (g u) t")
        sig = prT = sig_pr

        def krv(p):
            return [t[:, 0:TT] for t in turns[p % 2]]

        def kk_cum_dec(p):
            return [t[:, 0:TT] for t in turns[1 - p % 2]]

        def tiled(t):
            return t[:, :].rearrange("p (n c) -> p n c", n=NTILE)

        def small(p):
            v = turns[p % 2][2]
            return [v[:, a:a + 2 * P].rearrange("p (a i) -> p a i", i=HS) for a in (0, 2 * P)] + \
                [v[:, i * P:(i + 1) * P] for i in (4, 5)] + [v[:, 6 * P:8 * P].rearrange("p (a i) -> p a i", a=2)]

        def one_head(p):
            kkT, cum, decT = kk_cum_dec(p)
            return (kkT, cum), (aT, decT)

        def both(t):
            return t[:, 0:4:3, :]

        def padded(t, hh):
            return t[:, 2 * hh:2 * hh + 2, :]

        def heads(t):
            return t.rearrange("p (h i) -> p h i", h=2)

        flat_mm = dec_mm[:, :, :, :].rearrange("p a b c -> p (a b c)")
        flat_dd = be_dd[:, :, :, :].rearrange("p a b c -> p (a b c)")
        dprevT, dinvT = flat_mm[:, 0:TT], flat_mm[:, TT:2 * TT]
        mm_, dd = dec_mm, be_dd
        sq_o = flat_mm[:, 0:NTILE * P]
        masked = flat_mm[:, 0:2 * B * NS].rearrange("p (c b t) -> p c b t", c=2, b=B)
        out_s = flat_mm[:, NTILE * P:NTILE * P + B * P].rearrange("p (b c) -> p b c", b=B)
        beT, kaT = flat_dd[:, 0:TT], flat_dd[:, TT:2 * TT]
        prev = flat_dd[:, TT:TT + SEQ + 1]
        expd = flat_dd[0:NS, 0:2 * B * P].rearrange("p (c b i) -> p c b i", c=2, b=B)
        w_loaded = [st.sem(f"w_loaded{i}") for i in range(2)]
        (s0_loaded, s0_zeroed, hv_ready, wide_ready, prev_ready, prev_used, th_ready, th_used, sq_ready,
         kk_max, rn_ready, cc_ready, dec_ready, prep_ready, tok_turned, tok_ready, am_mm, am_ready, e0_ready,
         d0_turned, d0_ready, m_mm, m_ready, dm_mm, d_ready, e_turned, e_ready, x_ready, r_mm, r_ready, sa_mm,
         sa_ready, y_mm, o_mm, o_ready, s0_turned, s0_ready, masked_ready, sample_r_ready, sample_sa_ready, ys_mm, ys_ready, st_turned,
         st_ready, stored, alone_ready, var_ready, rs_ready, on_ready, y_turned, y_done, gate_read, bonus_done, y_stored, dve_chain,
         act_chain, pool_chain) = st.sems(
            "s0_loaded s0_zeroed hv_ready wide_ready prev_ready prev_used th_ready th_used sq_ready kk_max "
            "rn_ready cc_ready dec_ready prep_ready tok_turned tok_ready am_mm am_ready e0_ready d0_turned d0_ready "
            "m_mm m_ready dm_mm d_ready e_turned e_ready x_ready r_mm r_ready sa_mm sa_ready y_mm o_mm o_ready "
            "s0_turned s0_ready masked_ready sample_r_ready sample_sa_ready ys_mm ys_ready st_turned st_ready stored alone_ready var_ready rs_ready "
            "on_ready y_turned y_done gate_read bonus_done y_stored dve_chain act_chain pool_chain")
        block = st.block()

        NG = GROUPS + 1
        NLEV = len(STEPS)
        G = 5 * 512
        LOADS = [(6, 0), (0, 2), (12, 4), (21, 6)]
        WJ = 8
        PARTS = 3 * KC
        FILL = {}
        for at, first, count in ((0, 0, PARTS), (10, PARTS, 3), (12, PARTS + 3, PARTS), (22, 2 * PARTS + 3, 3)):
            for i in range(0, count, 3):
                FILL[divmod(at + i // 3, 3)] = range(first + i, first + i + 3)

        def used(g):
            return (P, P, 4) if g < GROUPS else (NS, NS, 2)

        def amat(g, i, kind, hh=None):
            if g < GROUPS:
                return am[:, 4 * g + i, kind, :]
            return ams[:, i, kind, :]

        @block.sync
        def _(sp):
            for p in range(PAIRS):
                for i, (chunk, wide_job) in enumerate(LOADS):
                    if 4 * p + i >= 2:
                        q, j = divmod(4 * p + i - 2, 4)
                        sp.wait_ge(wide_ready, WJ * q + LOADS[j][1] + 1)
                    sp.dma_start(w[:, i % 2, :, :].rearrange("p k c -> p (k c)"), w_in[chunk + p]).then_inc(w_loaded[i % 2], 16)
                if p == 0:
                    sp.wait_ge(s0_zeroed, 1)
                else:
                    sp.wait_ge(s0_turned, p)
                for hh in range(2):
                    sp.dma_start(s0[hh * HS:(hh + 1) * HS, :, hh * HS:(hh + 1) * HS],
                                 state_d[:, 2 * p + hh, :, :].rearrange("b i j -> i b j")).then_inc(s0_loaded, 16)

        @block.gpsimd
        def _(pool):
            for p in range(PAIRS):
                pool.wait_ge(prep_ready, p + 1)
                for c in range(2):
                    out = one_head(p)[1][c]
                    nc.gpsimd.tensor_scalar(out[:, 0:SEQ].rearrange("p (n t) -> p n t", n=NT), arT[:, 0:NT, c, :],
                                            const_view(const, "headsel")[:, 1:2], None, ALU.mult).then_inc(alone_ready, 1)
                    nc.gpsimd.tensor_scalar(out[:, SEQ:TT], arT[:, NT, c, 0:NS],
                                            const_view(const, "headsel")[:, 1:2], None, ALU.mult).then_inc(alone_ready, 1)
                pool.wait_ge(st_ready, p + 1)
                out_p = small(p)[3]
                for hh in range(2):
                    d = slice(hh * HS, (hh + 1) * HS)
                    pool.dma_start(new_state_s[:, 2 * p + hh, :, :].rearrange("b i j -> i b j"), out_s[d, :, d]).then_inc(stored, 16)
                    pool.dma_start(new_state_p[2 * p + hh, :, :], out_p[d, d]).then_inc(stored, 16)
                pool.wait_ge(y_done, p + 1)
                pool.dma_start(y_d[:, p, :], gT[:, :]).then_inc(y_stored, 16)
            pool.wait_ge(stored, 16 * 4 * PAIRS)
            pool.wait_ge(y_stored, 16 * PAIRS)

        @block.tensor
        def _(pe):
            def product(q, load, i):
                if i == 0:
                    pe.wait_ge(w_loaded[load % 2], 16 * (2 * q + load // 2 + 1))
                (a, b), k = COLS[i // KC], i % KC
                mm = pe.matmul(wide[:, G + a:G + b], w[:, load % 2, k, :], xT[:, k, a:b], start=(k == 0), stop=(k == KC - 1))
                if i == PARTS - 1:
                    mm.then_inc(wide_ready, 1)

            def low_rank(q, lo, i):
                a, b = COLS[i][0], min(COLS[i][1], TT)
                mm = pe.matmul(wide[:, G + a:G + b], up[:, lo, q * P:(q + 1) * P], lora[:, a:b], start=True, stop=True)
                if i == 2:
                    mm.then_inc(wide_ready, 1)

            def projection_part(q, i):
                if i < PARTS:
                    if i == 0 and q >= 1:
                        pe.wait_ge(gate_read, q)
                    product(q, 0, i)
                elif i < PARTS + 3:
                    if i == PARTS:
                        pe.wait_ge(prev_used, 3 * q + 1)
                    low_rank(q, 0, i - PARTS)
                elif i < 2 * PARTS + 3:
                    if i == PARTS + 3:
                        pe.wait_ge(th_ready, 3 * q + 1)
                    product(q, 1, i - PARTS - 3)
                elif i < 2 * PARTS + 6:
                    if i == 2 * PARTS + 3:
                        pe.wait_ge(prev_used, 3 * q + 2)
                    low_rank(q, 1, i - 2 * PARTS - 3)
                else:
                    if i == 2 * PARTS + 6:
                        pe.wait_ge(th_ready, 3 * q + 2)
                        if q >= 1:
                            pe.wait_ge(st_ready, q)
                    product(q, 2, i - 2 * PARTS - 6)

            for p in range(PAIRS):
                if p == 0:
                    for i in range(3 * PARTS + 6):
                        projection_part(0, i)
                kT, rT, vT = krv(p)
                kkT = kk_cum_dec(p)[0]
                r_sb, sa_sb, _, _, xs = small(p)
                o_all = tiled(turns[p % 2][1])
                if p >= 1:
                    pe.wait_ge(y_done, p)
                pe.wait_ge(sq_ready, p + 1)
                for a, b in COLS:
                    b = min(b, TT)
                    mm = pe.matmul(wide[:, a:b], const_view(const, "headsum"), kkT[:, a:b], start=True, stop=True)
                mm.then_inc(wide_ready, 1)
                pe.wait_ge(prev_used, 3 * p + 3)
                for i in range(PARTS):
                    product(p, 3, i)
                pe.wait_ge(prep_ready, p + 1)
                for n in range(NTILE):
                    r = rows_of(n)
                    mm = pe.matmul(bank[0:r, 3, 2 * n:2 * n + 2], prT[:, n * P:n * P + r],
                                   const_view(const, "headsel"), start=True, stop=True)
                mm.then_inc(wide_ready, 1)

                pe.wait_ge(gate_read, p + 1)
                for q in range(7):
                    if q >= 2:
                        pe.wait_ge(tok_ready, 7 * p + q - 1)
                    for i in range(4 if q < 6 else 3):
                        which, n = (q // 2, 4 * (q % 2) + i) if q < 6 else (i, NT)
                        r = rows_of(n)
                        mm = pe.transpose(bank[0:r, 6 + q % 2, i * P:(i + 1) * P], (vT, beT, kaT)[which][:, n * P:n * P + r],
                                          ident[:, :])
                    mm.then_inc(tok_turned, 1)
                pe.wait_ge(tok_ready, 7 * (p + 1))

                for u in range(UNITS + 2):
                    if u == 0:
                        pe.wait_ge(kk_max, p + 1)
                        pe.wait_ge(bonus_done, p + 1)
                    elif u >= 8:
                        pe.wait_ge(am_ready, (UNITS + 2) * p + u - 7)
                    n, hh = divmod(u, 2)
                    r = rows_of(n)
                    if u == 0:
                        pe.wait_ge(alone_ready, 8 * (p + 1))
                    for i, src in enumerate((beT, kaT)):
                        for c in range(2):
                            mm = pe.matmul(bank[0:r, u % 8, (2 * i + c) * r:(2 * i + c + 1) * r], src[:, n * P:n * P + r],
                                           one_head(p)[hh][c][:, n * P:n * P + r], start=True, stop=True)
                    mm.then_inc(am_mm, 1)
                pe.wait_ge(am_ready, (UNITS + 2) * (p + 1))

                for g in range(NG):
                    r, c, un = used(g)
                    pe.wait_ge(e0_ready, NG * p + g + 1)
                    for i in range(un):
                        mm = pe.transpose(bank[0:r, g, i * P:i * P + c], ee[0:r, g, i, 0:c], ident[0:r, 0:r])
                    mm.then_inc(d0_turned, 1)

                for lev in range(len(LEVELS)):
                    steps = [(k, g) for k, (lv, g) in enumerate(STEPS) if lv == lev]
                    for k, g in steps:
                        r, c, un = used(g)
                        if lev == 0:
                            pe.wait_ge(d0_ready, NG * p + g + 1)
                        else:
                            pe.wait_ge(d_ready, NLEV * p + prior(k, g) + 1)
                        for i in range(un):
                            mm = pe.matmul(bank[0:r, mbank(g), i * P:i * P + c], amat(g, i, 0), dd[0:r, g, i, 0:c],
                                           start=True, stop=True)
                        mm.then_inc(m_mm, 1)
                    for k, g in steps:
                        r, c, un = used(g)
                        pe.wait_ge(m_ready, NLEV * p + k + 1)
                        if lev >= 1:
                            pe.wait_ge(e_ready, NLEV * p + prior(k, g) + 1)
                        for i in range(un):
                            mm = pe.matmul(bank[0:r, mbank(g), i * P:i * P + c], ee[0:r, g, i, 0:c], mm_[0:r, g, i, 0:c],
                                           start=True, stop=True)
                        mm.then_inc(dm_mm, 1)
                    for k, g in steps:
                        r, c, un = used(g)
                        pe.wait_ge(d_ready, NLEV * p + k + 1)
                        if k >= 3:
                            pe.wait_ge(e_ready, NLEV * p + k - 2)
                        for i in range(un):
                            mm = pe.transpose(bank[0:r, 4 + k % 3, i * P:i * P + c], dd[0:r, g, i, 0:c], ident[0:r, 0:r])
                        mm.then_inc(e_turned, 1)
                pe.wait_ge(e_ready, NLEV * (p + 1))
                pe.wait_ge(d_ready, NLEV * (p + 1))

                def fill(n, step):
                    if p + 1 < PAIRS:
                        for i in FILL.get((n, step), ()):
                            projection_part(p + 1, i)

                for n in range(NT):
                    q = NT * p + n
                    pe.wait_ge(x_ready, (NT + 1) * p + n + 1)
                    x = xs[:, n % 2, :]
                    pe.matmul(bank[:, 0, 0:P], arT[:, n, 0, :], x, start=True, stop=False)
                    for hh in range(2):
                        mm = pe.matmul(heads(bank[:, 0, 0:P]), am[:, 2 * n + hh, 2, :], padded(v_tok[:, n], hh), start=False, stop=(hh == 1))
                    mm.then_inc(r_mm, 1)
                    fill(n, 0)
                    pe.wait_ge(r_ready, q + 1)
                    for hh in range(2):
                        u = 2 * n + hh
                        mm = pe.matmul(heads(bank[:, 1, 0:P]), ee[:, u // 4, u % 4, :], padded(r_sb, hh), start=(hh == 0), stop=(hh == 1))
                    mm.then_inc(sa_mm, 1)
                    fill(n, 1)
                    pe.wait_ge(sa_ready, q + 1)
                    pe.matmul(heads(bank[:, 4, 0:P]), tok[:, 0, n, :], both(sa_sb), start=True, stop=False)
                    pe.matmul(heads(bank[:, 4, 0:P]), tok[:, 1, n, :], both(v_tok[:, n]), start=False, stop=True).then_inc(y_mm, 1)
                    if n >= 2:
                        pe.wait_ge(o_ready, (NT + 1) * p + n - 1)
                    ob = 2 + n % 2
                    pe.matmul(bank[:, ob, 0:P], arT[:, n, 1, :], x, start=True, stop=False)
                    for hh in range(2):
                        pe.matmul(heads(bank[:, ob, 0:P]), am[:, 2 * n + hh, 1, :], padded(sa_sb, hh), start=False, stop=False)
                        mm = pe.matmul(heads(bank[:, ob, 0:P]), am[:, 2 * n + hh, 3, :], padded(v_tok[:, n], hh), start=False, stop=(hh == 1))
                    mm.then_inc(o_mm, 1)
                    fill(n, 2)

                if p + 1 < PAIRS:
                    pe.wait_ge(th_ready, 3 * (p + 1) + 2)
                pe.wait_ge(s0_loaded, 32 * (p + 1))
                for b in range(B):
                    mm = pe.transpose(bank[:, 5 + b // 4, (b % 4) * P:(b % 4 + 1) * P], s0[:, b, :], ident[:, :])
                mm.then_inc(s0_turned, 1)
                pe.wait_ge(s0_ready, p + 1)
                pe.wait_ge(masked_ready, p + 1)
                pe.wait_ge(x_ready, (NT + 1) * (p + 1))
                for b in range(B):
                    pe.matmul(bank[0:NS, 0, 0:P], masked[:, 0, b, :], s1[:, b, :], start=(b == 0), stop=False)
                for hh in range(2):
                    d = slice(hh * HS, (hh + 1) * HS)
                    mm = pe.matmul(bank[0:NS, 0, d], ams[:, hh, 2, :], v_tok[0:NS, NT, 3 * hh, :], start=False, stop=(hh == 1))
                mm.then_inc(r_mm, 1)
                pe.wait_ge(sample_r_ready, p + 1)
                for hh in range(2):
                    d = slice(hh * HS, (hh + 1) * HS)
                    mm = pe.matmul(bank[0:NS, 1, d], ee[0:NS, GROUPS, hh, 0:NS], r_sb[0:NS, 3 * hh, :], start=True, stop=True)
                mm.then_inc(sa_mm, 1)
                pe.wait_ge(sample_sa_ready, p + 1)
                pe.wait_ge(o_ready, (NT + 1) * p + NT)
                for b in range(B):
                    pe.matmul(bank[0:NS, 2, 0:P], masked[:, 1, b, :], s1[:, b, :], start=(b == 0), stop=False)
                for hh in range(2):
                    d = slice(hh * HS, (hh + 1) * HS)
                    pe.matmul(bank[0:NS, 2, d], ams[:, hh, 1, :], sa_sb[0:NS, 3 * hh, :], start=False, stop=False)
                    mm = pe.matmul(bank[0:NS, 2, d], ams[:, hh, 3, :], v_tok[0:NS, NT, 3 * hh, :], start=False, stop=(hh == 1))
                mm.then_inc(o_mm, 1)
                for half in range(2):
                    pe.matmul(bank[:, 5 + half, :], tok[0:NS, 0, NT, :], expd[:, 0, 4 * half:4 * half + 4, :],
                              start=True, stop=False)
                    mm = pe.matmul(bank[:, 5 + half, :], tok[0:NS, 1, NT, :], expd[:, 1, 4 * half:4 * half + 4, :],
                                   start=False, stop=True)
                mm.then_inc(ys_mm, 1)
                pe.wait_ge(ys_ready, p + 1)
                for b in range(B):
                    pe.transpose(bank[:, 5 + b // 4, (b % 4) * P:(b % 4 + 1) * P], s1[:, b, :], ident[:, :])
                pe.transpose(bank[:, 7, 0:P], xs[:, NT % 2, :], ident[:, :]).then_inc(st_turned, 1)

                if p + 1 < PAIRS:
                    for i in range(2 * PARTS + 6, 3 * PARTS + 6):
                        projection_part(p + 1, i)

                pe.wait_ge(on_ready, p + 1)
                for n in range(NTILE):
                    r = rows_of(n)
                    mm = pe.transpose(bank[:, n // 4, (n % 4) * P:(n % 4) * P + r], o_all[0:r, n, :], ident[0:r, 0:r])
                mm.then_inc(y_turned, 1)

        @block.scalar
        def _(act):
            link = Chain(act, act_chain)
            act.wait_ge(hv_ready, 1)

            def mixing(q, i, m, chunk):
                act.wait_ge(wide_ready, WJ * q + i + 1)
                if 3 * q + m >= 1:
                    act.wait_ge(prev_used, 3 * q + m)
                mix_scaled(nc, wide[:, G:G + TX], vec(vecs, "mu", chunk), prev, prev_s).then_inc(prev_ready, 1)

            def tanh(q, i, out, bias):
                act.wait_ge(wide_ready, WJ * q + i + 1)
                nc.scalar.activation(out[:, :], wide[:, G:G + TT], ACT.Tanh, scale=0.5, bias=bias).then_inc(th_ready, 1)

            def after_tile(q, n):
                if n == 2:
                    mixing(q, 0, 0, 6 + q)
                if n == 3:
                    tanh(q, 1, sig, hv[:, 0, q:q + 1])
                    act.wait_ge(th_ready, 3 * q + 1)
                    nc.scalar.activation(sig[:, :], sig[:, :], ACT.Copy, scale=0.5, bias=0.5)
                if n == 6:
                    mixing(q, 2, 1, q)
                if n == 7:
                    tanh(q, 3, aT, hv[:, 1, q:q + 1])

            for n in range(NT):
                after_tile(0, n)
            mixing(0, 4, 2, 12)
            for p in range(PAIRS):
                kT = krv(p)[0]
                kkT, cum, decT = kk_cum_dec(p)
                rnT = cum
                r_sb, _, _, out_p, _ = small(p)
                o_all = tiled(turns[p % 2][1])
                act.wait_ge(prev_used, 3 * p + 1)
                if p >= 1:
                    act.wait_ge(on_ready, p)
                nc.scalar.activation(kkT[:, :], kT[:, :], ACT.Square, scale=vec(vecs, "k_k", p)).then_inc(sq_ready, 1)
                act.wait_ge(cc_ready, p + 1)
                nc.scalar.activation(decT[:, :], cum[:, :], ACT.Exp, scale=-W_GATE)
                nc.scalar.activation(dprevT, dprevT, ACT.Exp, scale=-W_GATE)
                nc.scalar.activation(pm[:, :], pm[:, :], ACT.Exp, scale=-W_GATE)
                nc.scalar.activation(dinvT, cum[:, :], ACT.Exp, scale=W_GATE).then_inc(dec_ready, 1)
                act.wait_ge(kk_max, p + 1)
                link(nc.scalar.activation(rnT[:, :], rnT[:, :], ACT.Ln))
                nc.scalar.activation(rnT[:, :], rnT[:, :], ACT.Exp, scale=-0.5).then_inc(rn_ready, 1)
                if p >= 1:
                    act.wait_ge(y_stored, 16 * p)
                tanh(p, 6, gT, 0.0)
                act.wait_ge(prep_ready, p + 1)
                for c in range(2):
                    out = one_head(p)[0][c]
                    nc.scalar.activation(out[:, 0:SEQ].rearrange("p (n t) -> p n t", n=NT), arT[:, 0:NT, c, :], ACT.Copy,
                                         scale=const_view(const, "headsel")[:, 0:1]).then_inc(alone_ready, 1)
                    nc.scalar.activation(out[:, SEQ:TT], arT[:, NT, c, 0:NS], ACT.Copy,
                                         scale=const_view(const, "headsel")[:, 0:1]).then_inc(alone_ready, 1)
                for q in range(7):
                    act.wait_ge(tok_turned, 7 * p + q + 1)
                    if q < 2:
                        ins = nc.scalar.copy(v_tok[:, 4 * q:4 * q + 4, 0:4:3, :],
                                             bank[:, 6 + q, :].rearrange("p (n h i) -> p n h i", n=4, h=2))
                    elif q < 6:
                        ins = nc.scalar.copy(tok[:, q // 2 - 1, 4 * (q % 2):4 * (q % 2) + 4, :],
                                             bank[:, 6 + q % 2, :].rearrange("p (n c) -> p n c", n=4))
                    else:
                        nc.scalar.copy(v_tok[0:NS, NT, 0:4:3, :], heads(bank[0:NS, 6, 0:P]))
                        ins = nc.scalar.copy(tok[0:NS, :, NT, :], bank[0:NS, 6, P:3 * P].rearrange("p (n c) -> p n c", n=2))
                    ins.then_inc(tok_ready, 1)
                for g in range(NG):
                    r, c, un = used(g)
                    act.wait_ge(d0_turned, NG * p + g + 1)
                    nc.scalar.copy(dd[0:r, g, 0:un, 0:c], banks4(bank, g, r, c, un)).then_inc(d0_ready, 1)
                for k, (lev, g) in enumerate(STEPS):
                    r, c, un = used(g)
                    act.wait_ge(e_turned, NLEV * p + k + 1)
                    nc.scalar.copy(ee[0:r, g, 0:un, 0:c], banks4(bank, 4 + k % 3, r, c, un)).then_inc(e_ready, 1)
                for n in range(NTILE):
                    if n == NT:
                        act.wait_ge(s0_turned, p + 1)
                        nc.scalar.copy(s1.rearrange("p b c -> p (b c)"), wide[:, 5 * 512:7 * 512]).then_inc(s0_ready, 1)
                    r = rows_of(n)
                    act.wait_ge(r_mm, NTILE * p + n + 1)
                    ins = nc.scalar.copy(both(r_sb[0:r]), heads(bank[0:r, 0, 0:P]))
                    ins.then_inc(r_ready if n < NT else sample_r_ready, 1)
                    act.wait_ge(o_mm, NTILE * p + n + 1)
                    nc.scalar.copy(o_all[0:r, n, :], bank[0:r, 2 + n % 2, 0:P]).then_inc(o_ready, 1)
                    if p + 1 < PAIRS:
                        after_tile(p + 1, n)
                act.wait_ge(st_turned, p + 1)
                if p >= 1:
                    act.wait_ge(stored, 64 * p)
                nc.scalar.copy(out_p[:, :], bank[:, 7, 0:P])
                nc.scalar.copy(out_s[:, :, :].rearrange("p b c -> p (b c)"), wide[:, 5 * 512:7 * 512]).then_inc(st_ready, 1)
                act.wait_ge(var_ready, p + 1)
                link(nc.scalar.activation(stat[:, 2, :], stat[:, 1, :], ACT.Ln, scale=1.0 / HS, bias=eps_tile(nc)[:, 1:2]))
                nc.scalar.activation(stat[:, 3, :], stat[:, 2, :], ACT.Exp, scale=-0.5).then_inc(rs_ready, 1)
                if p + 1 < PAIRS:
                    mixing(p + 1, 4, 2, 12 + p + 1)

        @block.vector
        def _(dve):
            link = Chain(dve, dve_chain)
            for i in range(2):
                for j in range(2):
                    link(nc.vector.memset(turns[i][j][:, :], 0.0))
            link(nc.vector.memset(v_tok[:, :, :, :], 0.0))
            nc.vector.memset(s0[:, :, :], 0.0).then_inc(s0_zeroed, 1)
            nc.vector.tensor_scalar(hv[:, 0, :], vec(vecs, "w0"), 0.5, None, ALU.mult)
            nc.vector.tensor_scalar(hv[:, 2, :], vec(vecs, "k_a"), -0.5, 1.0, ALU.mult, ALU.add)
            nc.vector.tensor_scalar(hv[:, 3, :], vec(vecs, "k_a"), 0.5, None, ALU.mult)
            nc.vector.tensor_scalar(hv[:, 1, :], vec(vecs, "a0"), 0.5, None, ALU.mult).then_inc(hv_ready, 1)
            dve.wait_ge(hv_ready, 1)

            def mixing(q, m, chunk):
                dve.wait_ge(prev_ready, 3 * q + m + 1)
                if m != 1:
                    link(nc.vector.memset(prev[:, 0:1], 0.0))
                link(mix_rest(nc, krv(q)[m], wide[:, G:G + TX], omu[:, chunk:chunk + 1], prev, prev_s))
                dve.sem_inc(prev_used, 1)

            mixing(0, 0, 6)
            mixing(0, 1, 0)
            mixing(0, 2, 12)
            for p in range(PAIRS):
                kT, rT, vT = krv(p)
                kkT, cum, decT = kk_cum_dec(p)
                rnT = cum
                r_sb, sa_sb, xsc, _, xs = small(p)
                ov, o_all = tiled(turns[p % 2][0]), tiled(turns[p % 2][1])
                if p >= 1:
                    dve.wait_ge(stored, 64 * p)
                dve.wait_ge(th_ready, 3 * p + 2)
                link(nc.vector.tensor_tensor_scan(cum[:, :], const_view(const, "keep"), sig[:, :], 0.0, ALU.mult, ALU.add))
                cumt = cum[:, 0:SEQ].rearrange("p (n t) -> p n t", n=NT)
                link(nc.vector.tensor_copy(pm[:, :], cumt[:, :, P // 2]))
                link(nc.vector.tensor_tensor(cumt, cumt, bcast(pm[:, :].unsqueeze(2), [P, NT, P]), ALU.subtract))
                nc.vector.tensor_tensor(dprevT, cum[:, :], sig[:, :], ALU.subtract).then_inc(cc_ready, 1)
                dve.wait_ge(wide_ready, WJ * p + 6)
                dve.wait_ge(dec_ready, p + 1)
                link(nc.vector.tensor_scalar(rnT[:, :], wide[:, 0:TT], 1e-24, None, ALU.max))
                dve.sem_inc(kk_max, 1)
                dve.wait_ge(rn_ready, p + 1)
                dve.wait_ge(dec_ready, p + 1)
                link(nc.vector.scalar_tensor_tensor(out=kkT[:, :], in0=kT[:, :], scalar=vec(vecs, "k_k", p), in1=rnT[:, :],
                                                    op0=ALU.mult, op1=ALU.mult))

                def tiles(t):
                    return t[:, 0:SEQ].rearrange("p (n t) -> p n t", n=NT)

                for c in range(2):
                    x0, x1, s = ((kkT, dprevT, -1.0), (rT, decT, 1.0))[c]
                    nc.vector.scalar_tensor_tensor(out=arT[:, 0:NT, c, :], in0=tiles(x0), scalar=s, in1=tiles(x1),
                                                   op0=ALU.mult, op1=ALU.mult)
                    nc.vector.scalar_tensor_tensor(out=arT[:, NT, c, 0:NS], in0=x0[:, SEQ:TT], scalar=s, in1=x1[:, SEQ:TT],
                                                   op0=ALU.mult, op1=ALU.mult)
                link(nc.vector.scalar_tensor_tensor(out=beT[:, :], in0=aT[:, :], scalar=1.0, in1=kkT[:, :], op0=ALU.add, op1=ALU.mult))
                link(nc.vector.scalar_tensor_tensor(out=beT[:, :], in0=beT[:, :], scalar=0.5, in1=dinvT, op0=ALU.mult, op1=ALU.mult))
                link(nc.vector.tensor_scalar(aT[:, :], aT[:, :], hv[:, 3, p:p + 1], hv[:, 2, p:p + 1], ALU.mult, ALU.add))
                link(nc.vector.tensor_tensor(kT[:, :], kT[:, :], aT[:, :], ALU.mult))
                nc.vector.tensor_tensor(kaT[:, :], kT[:, :], dinvT, ALU.mult)
                link(nc.vector.scalar_tensor_tensor(out=prT[:, :], in0=rT[:, :], scalar=vec(vecs, "r_k", p), in1=kT[:, :],
                                                    op0=ALU.mult, op1=ALU.mult))
                ends = decT[:, 0:SEQ].rearrange("p (n t) -> p n t", n=NT)[:, :, P - 1]
                link(nc.vector.tensor_copy(xscale[:, :], ends))
                link(nc.vector.tensor_tensor(xscale[:, 0:NT - 1], xscale[:, 0:NT - 1], pm[:, 1:NT], ALU.mult))
                link(nc.vector.tensor_copy(ends_s[:, :], decT[:, SEQ:TT].rearrange("p (b t) -> p b t", b=B)[:, :, TS - 1]))
                dve.sem_inc(prep_ready, 1)
                dve.wait_ge(th_ready, 3 * p + 3)
                link(nc.vector.scalar_tensor_tensor(out=gT[:, :], in0=gT[:, :], scalar=1.0, in1=wide[:, G:G + TT],
                                                    op0=ALU.add, op1=ALU.mult))
                dve.sem_inc(gate_read, 1)
                dve.wait_ge(wide_ready, WJ * p + 8)
                dve.wait_ge(tok_ready, 7 * (p + 1))
                bonus = bank[:, 3, 0:2 * NTILE]
                for rr, n0, n1 in ((P, 0, NT), (NS, NT, NTILE)):
                    link(nc.vector.tensor_tensor(ov[0:rr, n0:n1, :].rearrange("p n (h i) -> p n h i", h=2),
                                                 v_tok[0:rr, n0:n1, 0:4:3, :],
                                                 bcast(bonus[0:rr, 2 * n0:2 * n1].rearrange("p (n h) -> p n h", h=2).unsqueeze(3),
                                                       [rr, n1 - n0, 2, HS]), ALU.mult))
                dve.sem_inc(bonus_done, 1)
                for u in range(UNITS + 2):
                    dve.wait_ge(am_mm, (UNITS + 2) * p + u + 1)
                    if u < UNITS:
                        ins = nc.vector.tensor_tensor(am[:, u, :, :].rearrange("p a t -> p (a t)"), bank[:, u % 8, :],
                                                      const_view(const, "mask4"), ALU.mult)
                    else:
                        ins = nc.vector.tensor_tensor(ams[:, u - UNITS, :, :].rearrange("p a t -> p (a t)"),
                                                      bank[0:NS, u % 8, 0:4 * NS], const_view(const, "mask4s")[0:NS, :], ALU.mult)
                    ins.then_inc(am_ready, 1)
                dve.wait_ge(am_ready, (UNITS + 2) * (p + 1))
                for g in range(NG):
                    r, c, un = used(g)
                    src = am[:, 4 * g:4 * g + 4, 0, :] if g < GROUPS else ams[:, :, 0, :]
                    e = ee[0:r, g, 0:un, 0:c]
                    link(nc.vector.tensor_tensor(e, src, bcast(const_view(const, "pair1")[0:r, 0:c].unsqueeze(1), [r, un, c]), ALU.mult))
                    nc.vector.tensor_tensor(e, e, bcast(ident[0:r, 0:c].unsqueeze(1), [r, un, c]), ALU.add).then_inc(e0_ready, 1)
                for lev, b in enumerate(LEVELS):
                    steps = [(k, g) for k, (lv, g) in enumerate(STEPS) if lv == lev]
                    for k, g in steps:
                        r, c, un = used(g)
                        dve.wait_ge(m_mm, NLEV * p + k + 1)
                        nc.vector.tensor_tensor(mm_[0:r, g, 0:un, 0:c], banks4(bank, mbank(g), r, c, un),
                                                bcast(const_view(const, f"pair{b}")[0:r, 0:c].unsqueeze(1), [r, un, c]),
                                                ALU.mult).then_inc(m_ready, 1)
                    for k, g in steps:
                        r, c, un = used(g)
                        dve.wait_ge(dm_mm, NLEV * p + k + 1)
                        nc.vector.tensor_tensor(dd[0:r, g, 0:un, 0:c], banks4(bank, mbank(g), r, c, un),
                                                dd[0:r, g, 0:un, 0:c], ALU.add).then_inc(d_ready, 1)
                for t in (r_sb, sa_sb):
                    link(nc.vector.memset(t[:, 1:3, :], 0.0))
                nc.vector.memset(xs[:, 0, :], 0.0).then_inc(x_ready, 1)
                dve.wait_ge(x_ready, (NT + 1) * p + 1)
                for n in range(NT):
                    link(nc.vector.tensor_scalar(xsc[:, :], xs[:, n % 2, :], xscale[:, n:n + 1], None, ALU.mult))
                    dve.wait_ge(sa_mm, NTILE * p + n + 1)
                    nc.vector.tensor_copy(both(sa_sb), heads(bank[:, 1, 0:P])).then_inc(sa_ready, 1)
                    dve.wait_ge(y_mm, NT * p + n + 1)
                    if n >= 1:
                        dve.wait_ge(o_mm, NTILE * p + n)
                    xn = xs[:, (n + 1) % 2, :]
                    link(nc.vector.scalar_tensor_tensor(out=xn, in0=bank[:, 4, 0:P], scalar=xscale[:, n:n + 1],
                                                        in1=const_view(const, "headsum"), op0=ALU.mult, op1=ALU.mult))
                    nc.vector.tensor_tensor(xn, xn, xsc[:, :], ALU.add).then_inc(x_ready, 1)
                    dve.wait_ge(x_ready, (NT + 1) * p + n + 2)
                    if p + 1 < PAIRS and n == 2:
                        mixing(p + 1, 0, 6 + p + 1)
                    if p + 1 < PAIRS and n == 6:
                        mixing(p + 1, 1, p + 1)
                own = const_view(const, "owncols").rearrange("p (b t) -> p b t", b=B)
                for c in range(2):
                    ins = nc.vector.tensor_tensor(masked[:, c, :, :], own, bcast(arT[:, NT, c, 0:NS].unsqueeze(1), [P, B, NS]), ALU.mult)
                ins.then_inc(masked_ready, 1)
                dve.wait_ge(sa_mm, NTILE * p + NTILE)
                link(nc.vector.tensor_copy(both(sa_sb[0:NS]), heads(bank[0:NS, 1, 0:P])))
                ownseq = bcast(const_view(const, "ownseq")[0:NS, :].unsqueeze(2).unsqueeze(3), [NS, B, 2, HS])
                for c, t in ((0, both(sa_sb[0:NS])), (1, v_tok[0:NS, NT, 0:4:3, :])):
                    ins = nc.vector.tensor_tensor(expd[:, c, :, :].rearrange("p b (h i) -> p b h i", h=2), ownseq,
                                                  bcast(t.unsqueeze(1), [NS, B, 2, HS]), ALU.mult)
                ins.then_inc(sample_sa_ready, 1)
                dve.wait_ge(ys_mm, p + 1)
                link(nc.vector.tensor_tensor(s1.rearrange("p b c -> p (b c)"), wide[:, 5 * 512:7 * 512],
                                             s1.rearrange("p b c -> p (b c)"), ALU.add))
                nc.vector.tensor_tensor(s1, s1, bcast(ends_s[:, :].unsqueeze(2), [P, B, P]), ALU.mult).then_inc(ys_ready, 1)

                dve.wait_ge(o_ready, NTILE * (p + 1))
                o = o_all[:, :, :].rearrange("p n (h i) -> p (n h) i", h=2)
                sq = sq_o.rearrange("p (n i) -> p n i", i=HS)
                link(nc.vector.tensor_reduce(stat[:, 0, :], o, X, ALU.add))
                link(nc.vector.tensor_scalar(stat[:, 0, :], stat[:, 0, :], 1.0 / HS, None, ALU.mult))
                link(nc.vector.tensor_tensor(o, o, bcast(stat[:, 0, :].unsqueeze(2), [P, 2 * NTILE, HS]), ALU.subtract))
                link(nc.vector.tensor_tensor(sq, o, o, ALU.mult))
                nc.vector.tensor_reduce(stat[:, 1, :], sq, X, ALU.add).then_inc(var_ready, 1)
                dve.wait_ge(rs_ready, p + 1)
                link(nc.vector.tensor_tensor(o, o, bcast(stat[:, 3, :].unsqueeze(2), [P, 2 * NTILE, HS]), ALU.mult))
                link(nc.vector.tensor_tensor(o_all[:, :, :], o_all[:, :, :],
                                             bcast(row(rows, "lnx_g", p * P, (p + 1) * P).unsqueeze(1), [P, NTILE, P]), ALU.mult))
                link(nc.vector.tensor_tensor(o_all[:, :, :], o_all[:, :, :],
                                             bcast(row(rows, "lnx_b", p * P, (p + 1) * P).unsqueeze(1), [P, NTILE, P]), ALU.add))
                nc.vector.tensor_tensor(o_all[:, :, :], o_all[:, :, :], ov[:, :, :], ALU.add).then_inc(on_ready, 1)
                dve.wait_ge(y_turned, p + 1)
                nc.vector.scalar_tensor_tensor(out=gT[:, :], in0=wide[:, 0:TT], scalar=0.5, in1=gT[:, :],
                                               op0=ALU.mult, op1=ALU.mult).then_inc(y_done, 1)
                if p + 1 < PAIRS:
                    mixing(p + 1, 2, 12 + p + 1)


def prior(k, g):
    return max(i for i, (_, gg) in enumerate(STEPS[:k]) if gg == g)


def mbank(g):
    return g if g < GROUPS else 7


def banks4(bank, j, r, c, un):
    return bank[0:r, j, 0:un * P].rearrange("p (u t) -> p u t", u=un)[:, :, 0:c]


def gates_and_queries(nc, name, w_d, chunks, xT, gain, vecs, mq_g, const, wide, mqT, gates):
    n_all = len(chunks)
    with Stage(nc, name) as st:
        w = st.sb("w", [P, 2, KC, P])
        sq = st.sb("sq", [P, 2, TT])
        w_loaded = [st.sem(f"w_loaded{i}") for i in range(2)]
        gained, ready, free, act_read, sq_ready, rn_ready, done, dve_chain, act_chain = st.sems(
            "gained ready free act_read sq_ready rn_ready done dve_chain act_chain")
        block = st.block()
        G = (0, 1536)

        @block.sync
        def _(sp):
            for j, c in enumerate(chunks):
                if j >= 2:
                    sp.wait_ge(ready, j - 1)
                sp.dma_start(w[:, j % 2, :, :].rearrange("p k c -> p (k c)"), w_d[c]).then_inc(w_loaded[j % 2], 16)

        if gain is not None:
            @block.gpsimd
            def _(pool):
                for j in range(n_all):
                    pool.wait_ge(w_loaded[j % 2], 16 * (j // 2 + 1))
                    nc.gpsimd.tensor_tensor(w[:, j % 2], w[:, j % 2], bcast(gain.unsqueeze(2), [P, KC, P]),
                                            ALU.mult).then_inc(gained, 1)

        @block.tensor
        def _(pe):
            for j in range(n_all):
                if j >= 2:
                    pe.wait_ge(free, j - 1)
                if gain is None:
                    pe.wait_ge(w_loaded[j % 2], 16 * (j // 2 + 1))
                else:
                    pe.wait_ge(gained, j + 1)
                project(pe, wide, G[j % 2], w[:, j % 2], xT, TT).then_inc(ready, 1)
            for c in range(2):
                j = n_all + c
                pe.wait_ge(free, j - 1)
                pe.wait_ge(sq_ready, c + 1)
                for a, b in COLS:
                    b = min(b, TT)
                    mm = pe.matmul(wide[:, G[j % 2] + a:G[j % 2] + b], const_view(const, "headsum"), sq[:, c, a:b],
                                   start=True, stop=True)
                mm.then_inc(ready, 1)

        @block.scalar
        def _(act):
            link = Chain(act, act_chain)
            for j in range(n_all):
                act.wait_ge(ready, j + 1)
                ps = wide[:, G[j % 2]:G[j % 2] + TT]
                if j < 2:
                    nc.scalar.activation(sq[:, j, :], ps, ACT.Square).then_inc(sq_ready, 1)
                else:
                    nc.scalar.activation(gates[:, j - 2, :], ps, ACT.Tanh, scale=0.5).then_inc(act_read, 1)
            for c in range(2):
                j = n_all + c
                act.wait_ge(ready, j + 1)
                link(nc.scalar.activation(sq[:, c, :], wide[:, G[j % 2]:G[j % 2] + TT], ACT.Ln, scale=1.0 / HS,
                                          bias=eps_tile(nc)[:, 0:1]))
            for c in range(2):
                nc.scalar.activation(sq[:, c, :], sq[:, c, :], ACT.Exp, scale=-0.5).then_inc(rn_ready, 1)

        @block.vector
        def _(dve):
            for j in range(n_all):
                dve.wait_ge(ready, j + 1)
                ps = wide[:, G[j % 2]:G[j % 2] + TT]
                if j < 2:
                    dve.wait_ge(sq_ready, j + 1)
                    nc.vector.tensor_copy(mqT[:, j, :], ps).then_inc(free, 1)
                else:
                    dve.wait_ge(act_read, j - 1)
                    g = gates[:, j - 2, :]
                    nc.vector.scalar_tensor_tensor(out=g, in0=g, scalar=1.0, in1=ps, op0=ALU.add, op1=ALU.mult).then_inc(free, 1)
            dve.wait_ge(free, n_all)
            for c in range(2):
                dve.wait_ge(rn_ready, c + 1)
                nc.vector.scalar_tensor_tensor(out=mqT[:, c, :], in0=mqT[:, c, :], scalar=mq_g, in1=sq[:, c, :],
                                               op0=ALU.mult, op1=ALU.mult).then_inc(done, 1)


def memory_attention(nc, name, layer, mqT, mkT, mv, cmk, cmv, gates, const, ones, bank, scratch=None, ahead=()):
    ident = const_view(const, "ident")
    SC = HS ** -0.5
    with Stage(nc, name) as st:
        both = st.sb("both", [P, 4096])
        pr = both[:, 0:2048].rearrange("p (r h t) -> p r h t", r=2, h=4)
        pT = both[:, 2048:4096].rearrange("p (r i t) -> p r i t", r=2, i=8)
        kT = both[:, :].rearrange("p (b c t) -> p b c t", b=B, c=2)
        mx = st.sb("mx", [P, 2, 4])
        mkz = st.sb("mkz", [P, 2, 2, MEMT])
        ls = st.sb("ls", [P, 2, 4])
        if scratch is None:
            kn = st.sb("kn", [P, B, 2, MEMT])
            vn = st.sb("vn", [P, B, 2, MEMT])
        else:
            dead = scratch[:, :, :].rearrange("p k t -> p (k t)")
            kn, vn = (dead[:, i * 4096:(i + 1) * 4096].rearrange("p (b c d) -> p b c d", b=B, c=2) for i in range(2))
        qbd = st.sb("qbd", [P, 2, B, 2, TS])
        ps_ = st.sb("ps", [P, B, 2, 32])
        red = st.sb("red", [P, 256])
        mxT = st.sb("mxT", [P, 2])
        dg = st.sb("dg", [P, 256])
        bc = st.sb("bc", [P, 256])
        (k_loaded, v_loaded, qbd_ready, turned, kT_ready, ss_mm, red_ready, red_turned, dg_ready, bc_mm, bc_ready,
         sub_ready, exp_ready, sum_ready, sum_mm, ws_ready, os_mm, s_mm, mx_ready, pr_ready, w_ready, w_turned,
         pT_ready, o_mm, y_ready, dve_chain, mkz_ready, ahead_loaded) = st.sems(
            "k_loaded v_loaded qbd_ready turned kT_ready ss_mm red_ready red_turned dg_ready bc_mm bc_ready "
            "sub_ready exp_ready sum_ready sum_mm ws_ready os_mm s_mm mx_ready pr_ready w_ready w_turned "
            "pT_ready o_mm y_ready dve_chain mkz_ready ahead_loaded")
        block = st.block()

        @block.sync
        def _(sp):
            sp.dma_start(kn[:, :, :, :], cmk[layer].rearrange("b (c p) d -> p b c d", p=P)).then_inc(k_loaded, 16)
            sp.dma_start(vn[:, :, :, :], cmv[layer].rearrange("b (c p) d -> p b c d", p=P)).then_inc(v_loaded, 16)
            for dst, src in ahead:
                sp.dma_start(dst, src).then_inc(ahead_loaded, 16)
            if ahead:
                sp.wait_ge(ahead_loaded, 16 * len(ahead))

        @block.tensor
        def _(pe):
            def scores(n):
                if n >= 2:
                    pe.wait_ge(pr_ready, n - 1)
                for hh in range(2):
                    for c in range(2):
                        mm = pe.matmul(bank[:, 2 * (n % 2) + hh, c * MEMT:(c + 1) * MEMT], mqT[:, c, n * P:(n + 1) * P],
                                       mkz[:, c, hh, :], start=True, stop=True)
                mm.then_inc(s_mm, 1)

            def values(n):
                pe.wait_ge(pT_ready, n + 1)
                if n >= 2:
                    pe.wait_ge(y_ready, n - 1)
                for hh in range(2):
                    for c in range(2):
                        for kc in range(2):
                            mm = pe.matmul(bank[hh * HS:(hh + 1) * HS, 6 + n % 2, c * P:(c + 1) * P],
                                           mv[:, layer, kc, (2 * c + hh) * HS:(2 * c + hh + 1) * HS],
                                           pT[:, n % 2, 4 * hh + 2 * c + kc, :], start=(kc == 0), stop=(kc == 1))
                mm.then_inc(o_mm, 1)

            pe.wait_ge(mkz_ready, 1)
            scores(0)
            for n in range(NT):
                if n + 1 < NT:
                    scores(n + 1)
                pe.wait_ge(w_ready, n + 1)
                if n >= 1:
                    pe.wait_ge(pT_ready, n)
                for i in range(8):
                    mm = pe.transpose(bank[:, 4 + i // 4, (i % 4) * P:(i % 4 + 1) * P],
                                      pr[:, n % 2, i // 2, (i % 2) * P:(i % 2 + 1) * P], ident[:, :])
                mm.then_inc(w_turned, 1)
                if n >= 1:
                    values(n - 1)
            values(NT - 1)
            pe.wait_ge(k_loaded, 16)
            pe.wait_ge(pr_ready, NT)
            for b in range(B):
                if b >= 2:
                    pe.wait_ge(kT_ready, b - 1)
                for c in range(2):
                    for kc in range(2):
                        mm = pe.transpose(bank[:, b % 2, (2 * c + kc) * P:(2 * c + kc + 1) * P],
                                          kn[:, b, kc, c * P:(c + 1) * P], ident[:, :])
                mm.then_inc(turned, 1)
            pe.wait_ge(qbd_ready, 1)
            for b in range(B):
                pe.wait_ge(kT_ready, b + 1)
                for kc in range(2):
                    for c in range(2):
                        mm = pe.matmul(bank[:, 2, b * 64 + kc * 32 + c * 16:b * 64 + kc * 32 + c * 16 + 16],
                                       kT[:, b, c, kc * P:(kc + 1) * P], qbd[:, c, b, :, :].rearrange("p h t -> p (h t)"),
                                       start=True, stop=True)
            mm.then_inc(ss_mm, 1)
            pe.wait_ge(red_ready, 1)
            for i in range(2):
                mm = pe.transpose(bank[:, 3, i * P:(i + 1) * P], red[:, i * P:(i + 1) * P], ident[:, :])
            mm.then_inc(red_turned, 1)
            pe.wait_ge(dg_ready, 1)
            pe.matmul(bank[:, 0, 0:256], ones[:, :], dg[:, :], start=True, stop=True).then_inc(bc_mm, 1)
            pe.wait_ge(sum_ready, 1)
            pe.matmul(bank[:, 1, 0:256], ones[:, :], red[:, :], start=True, stop=True).then_inc(sum_mm, 1)
            pe.wait_ge(v_loaded, 16)
            pe.wait_ge(ws_ready, 1)
            pe.wait_ge(y_ready, NT)
            for b in range(B):
                for c in range(2):
                    for hh in range(2):
                        for kc in range(2):
                            at = kc * 32 + c * 16 + hh * 8
                            mm = pe.matmul(bank[hh * HS:(hh + 1) * HS, 6, c * NS + b * TS:c * NS + (b + 1) * TS],
                                           vn[:, b, kc, (2 * c + hh) * HS:(2 * c + hh + 1) * HS],
                                           ps_[:, b, at // 32, at % 32:at % 32 + 8], start=(kc == 0), stop=(kc == 1))
            mm.then_inc(os_mm, 1)

        @block.scalar
        def _(act):
            def turned_out(n):
                act.wait_ge(w_turned, n + 1)
                nc.scalar.copy(pT[:, n % 2, :, :].rearrange("p i t -> p (i t)"),
                               bank[:, 4:6, :].rearrange("p b c -> p (b c)")).then_inc(pT_ready, 1)

            for n in range(NT):
                if n >= 2:
                    act.wait_ge(w_turned, n - 1)
                act.wait_ge(mx_ready, n + 1)
                for i in range(4):
                    ins = nc.scalar.activation(pr[:, n % 2, i, :], bank[:, 2 * (n % 2) + i // 2, (i % 2) * MEMT:(i % 2 + 1) * MEMT],
                                               ACT.Exp, scale=SC, bias=mx[:, n % 2, i:i + 1], accum_out=ls[:, n % 2, i:i + 1])
                ins.then_inc(pr_ready, 1)
                if n >= 1:
                    turned_out(n - 1)
            turned_out(NT - 1)
            for b in range(B):
                act.wait_ge(turned, b + 1)
                nc.scalar.copy(kT[:, b, :, :].rearrange("p c t -> p (c t)"), bank[:, b % 2, :]).then_inc(kT_ready, 1)
            act.wait_ge(bc_mm, 1)
            nc.scalar.copy(bc[:, :], bank[:, 0, 0:256]).then_inc(bc_ready, 1)
            act.wait_ge(sub_ready, 1)
            nc.scalar.activation(ps_[:, :, :, :], ps_[:, :, :, :], ACT.Exp, scale=SC).then_inc(exp_ready, 1)

        @block.vector
        def _(dve):
            link = Chain(dve, dve_chain)
            link(nc.vector.memset(mkz[:, :, :, :], 0.0))
            for hh in range(2):
                d = slice(hh * HS, (hh + 1) * HS)
                link(nc.vector.tensor_copy(mkz[d, :, hh, :], mkT[d, layer, :, :]))
            dve.sem_inc(mkz_ready, 1)
            link(nc.vector.memset(qbd[:, :, :, :, :], 0.0))
            for hh in range(2):
                d = slice(hh * HS, (hh + 1) * HS)
                link(nc.vector.tensor_copy(qbd[d, :, :, hh, :], mqT[d, :, SEQ:TT].rearrange("p c (b t) -> p c b t", b=B)))
            dve.sem_inc(qbd_ready, 1)

            def maxima(n):
                dve.wait_ge(s_mm, n + 1)
                link(nc.vector.tensor_reduce(mx[:, n % 2, :], bank[:, 2 * (n % 2):2 * (n % 2) + 2, :].rearrange("p b (c t) -> p (b c) t", c=2), X, ALU.max))
                nc.vector.tensor_scalar(mx[:, n % 2, :], mx[:, n % 2, :], -SC, None, ALU.mult).then_inc(mx_ready, 1)

            def gated(n):
                dve.wait_ge(o_mm, n + 1)
                y = gates[:, :, n * P:(n + 1) * P]
                nc.vector.scalar_tensor_tensor(out=y, in0=bank[:, 6 + n % 2, 0:2 * P].rearrange("p (c t) -> p c t", c=2),
                                               scalar=0.5, in1=y, op0=ALU.mult, op1=ALU.mult).then_inc(y_ready, 1)

            maxima(0)
            for n in range(NT):
                if n + 1 < NT:
                    maxima(n + 1)
                dve.wait_ge(pr_ready, n + 1)
                link(nc.vector.reciprocal(ls[:, n % 2, :], ls[:, n % 2, :]))
                nc.vector.tensor_tensor(pr[:, n % 2, :, :], pr[:, n % 2, :, :], bcast(ls[:, n % 2, :].unsqueeze(2), [P, 4, MEMT]),
                                        ALU.mult).then_inc(w_ready, 1)
                if n >= 1:
                    gated(n - 1)
            gated(NT - 1)
            dve.wait_ge(ss_mm, 1)
            s = bank[:, 2, :].rearrange("p (b k c) -> p b k c", b=B, k=2)
            nc.vector.tensor_reduce(red[:, :].rearrange("p (b c) -> p b c", b=B), s.rearrange("p b k c -> p b c k"), X,
                                    ALU.max).then_inc(red_ready, 1)
            dve.wait_ge(red_turned, 1)
            link(nc.vector.tensor_reduce(mxT[:, :], bank[:, 3, 0:256].rearrange("p (i k) -> p i k", i=2), X, ALU.max))
            for i in range(2):
                ins = nc.vector.tensor_scalar(dg[:, i * P:(i + 1) * P], ident[:, :], mxT[:, i:i + 1], None, ALU.mult)
            ins.then_inc(dg_ready, 1)
            dve.wait_ge(bc_ready, 1)
            nc.vector.tensor_tensor(ps_[:, :, :, :], s, bcast(bc[:, :].rearrange("p (b c) -> p b c", b=B).unsqueeze(2), [P, B, 2, 32]),
                                    ALU.subtract).then_inc(sub_ready, 1)
            dve.wait_ge(exp_ready, 1)
            nc.vector.tensor_reduce(red[:, :].rearrange("p (b c) -> p b c", b=B), ps_[:, :, :, :].rearrange("p b k c -> p b c k"), X,
                                    ALU.add).then_inc(sum_ready, 1)
            dve.wait_ge(sum_mm, 1)
            link(nc.vector.reciprocal(bc[:, :], bank[:, 1, 0:256]))
            nc.vector.tensor_tensor(ps_[:, :, :, :], ps_[:, :, :, :], bcast(bc[:, :].rearrange("p (b c) -> p b c", b=B).unsqueeze(2), [P, B, 2, 32]),
                                    ALU.mult).then_inc(ws_ready, 1)
            dve.wait_ge(os_mm, 1)
            y = gates[:, :, SEQ:TT]
            link(nc.vector.scalar_tensor_tensor(out=y, in0=bank[:, 6, 0:2 * NS].rearrange("p (c t) -> p c t", c=2), scalar=0.5,
                                                in1=y, op0=ALU.mult, op1=ALU.mult))


def weights_in(scratch):
    return scratch[:, :, :].rearrange("p k t -> p (k t)")[:, 0:KC * D].rearrange("p (k c) -> p k c", k=KC)


def out_project(nc, name, w_d, yT, h, bank, scratch, h_load, h_store):
    with Stage(nc, name) as st:
        w = weights_in(scratch)
        if h is None:
            h = st.sb("h", [P, NTILE, D])
        w_loaded, mm_done, added, stored = st.sems("w_loaded mm_done added stored")
        h_loaded = [st.sem(f"h_loaded{n}") for n in range(NTILE)]
        block = st.block()

        @block.sync
        def _(sp):
            if w_d is not None:
                for half in range(2):
                    sp.dma_start(w[:, 4 * half:4 * half + 4, :].rearrange("p k c -> p (k c)"),
                                 w_d[:, 4 * half * D:4 * (half + 1) * D]).then_inc(w_loaded, 16)
            for n in range(NTILE):
                r = rows_of(n)
                sp.dma_start(h[0:r, n, :], h_load[1] if n == NT else h_load[0][n * P:(n + 1) * P, :]).then_inc(h_loaded[n], 16)

        @block.gpsimd
        def _(pool):
            for n in range(NTILE):
                r = rows_of(n)
                pool.wait_ge(added, 2 * n + 2)
                pool.dma_start(h_store[1] if n == NT else h_store[0][n * P:(n + 1) * P, :], h[0:r, n, :]).then_inc(stored, 16)
            pool.wait_ge(stored, 16 * NTILE)

        @block.tensor
        def _(pe):
            if w_d is not None:
                pe.wait_ge(w_loaded, 32)
            for j in range(2 * NTILE):
                n, half = j // 2, j % 2
                if j >= 8:
                    pe.wait_ge(added, j - 7)
                r = rows_of(n)
                for k in range(KC):
                    mm = pe.matmul(bank[0:r, j % 8, :], yT[:, k, n * P:n * P + r], w[:, k, half * 512:(half + 1) * 512],
                                   start=(k == 0), stop=(k == KC - 1))
                mm.then_inc(mm_done, 1)

        @block.vector
        def _(dve):
            for j in range(2 * NTILE):
                n, half = j // 2, j % 2
                r = rows_of(n)
                dve.wait_ge(mm_done, j + 1)
                dve.wait_ge(h_loaded[n], 16)
                hh = h[0:r, n, half * 512:(half + 1) * 512]
                nc.vector.tensor_tensor(hh, hh, bank[0:r, j % 8, :], ALU.add).then_inc(added, 1)


def keys_values_queries(nc, kv_w, q_w, vecs, rows2, const, ident, xT, bank, KT, QT, V, k_out, v_out):
    W = 384
    with Stage(nc, "kvq") as st:
        w = st.sb("w", [P, 2, KC, W])
        raw = st.sb("raw", [P, NTILE, W])
        rot = st.sb("rot", [P, NTILE, W])
        sq = st.sb("sq", [P, 2, W])
        ss = st.sb("ss", [P, NTILE * 6])
        w_loaded = [st.sem(f"w_loaded{i}") for i in range(2)]
        (gained, mm_done, raw_ready, sq_ready, ss_ready, rs_ready, rot_ready, turned, turned_out, v_ready, k_stored,
         v_stored, zeroed, dve_chain, act_chain) = st.sems(
            "gained mm_done raw_ready sq_ready ss_ready rs_ready rot_ready turned turned_out v_ready k_stored "
            "v_stored zeroed dve_chain act_chain")
        block = st.block()
        GRP = [("k", 0), ("v", 0), ("k", 1), ("v", 1), ("q", 0), ("q", 1)]
        normed = [i for i, (kind, _) in enumerate(GRP) if kind != "v"]

        @block.sync
        def _(sp):
            for i, (kind, half) in enumerate(GRP):
                src = q_w[half] if kind == "q" else kv_w[half + 2 * (kind == "v")]
                if i >= 2:
                    sp.wait_ge(mm_done, NTILE * (i - 1))
                sp.dma_start(w[:, i % 2, :, :].rearrange("p k c -> p (k c)"), src).then_inc(w_loaded[i % 2], 16)

        @block.gpsimd
        def _(pool):
            def gained_weights(i):
                kind = GRP[i][0]
                g = vec(vecs, "bg" if kind == "q" else "kvg")
                pool.wait_ge(w_loaded[i % 2], 16 * (i // 2 + 1))
                nc.gpsimd.tensor_tensor(w[:, i % 2], w[:, i % 2], bcast(g.unsqueeze(2), [P, KC, W]), ALU.mult).then_inc(gained, 1)

            gained_weights(0)
            nk = nv = 0
            for i, (kind, half) in enumerate(GRP):
                if i + 1 < len(GRP):
                    gained_weights(i + 1)
                for n in range(NTILE):
                    r = rows_of(n)
                    if kind == "v":
                        dst = v_out[1] if n == NT else v_out[0][n * P:(n + 1) * P, :]
                        pool.wait_ge(v_ready, NTILE * nv + n + 1)
                        pool.dma_start(dst[:, half * W:(half + 1) * W], V[0:r, n, half * W:(half + 1) * W]).then_inc(v_stored, 16)
                    elif kind == "k":
                        dst = k_out[1] if n == NT else k_out[0][n * P:(n + 1) * P, :]
                        if n == 0:
                            pool.wait_ge(rot_ready, nk + 1)
                        pool.dma_start(dst[:, half * W:(half + 1) * W], rot[0:r, n, :]).then_inc(k_stored, 16)
                nk += kind != "v"
                nv += kind == "v"
            pool.wait_ge(k_stored, 32 * NTILE)
            pool.wait_ge(v_stored, 32 * NTILE)

        @block.tensor
        def _(pe):
            nn = 0

            def turn(g):
                pe.wait_ge(rot_ready, g + 1)
                for n in range(NTILE):
                    j = NTILE * g + n
                    r = rows_of(n)
                    if j >= 2:
                        pe.wait_ge(turned_out, j - 1)
                    for i in range(3):
                        mm = pe.transpose(bank[:, 6 + j % 2, i * P:i * P + r], rot[0:r, n, i * P:(i + 1) * P], ident[0:r, 0:r])
                    mm.then_inc(turned, 1)

            for i in range(len(GRP)):
                pe.wait_ge(gained, i + 1)
                for n in range(NTILE):
                    j = NTILE * i + n
                    r = rows_of(n)
                    if j >= 6:
                        pe.wait_ge(raw_ready, j - 5)
                    for k in range(KC):
                        mm = pe.matmul(bank[0:r, j % 6, 0:W], xT[:, k, n * P:n * P + r], w[:, i % 2, k, :],
                                       start=(k == 0), stop=(k == KC - 1))
                    mm.then_inc(mm_done, 1)
                if i >= 1 and GRP[i - 1][0] != "v":
                    turn(nn)
                    nn += 1
            turn(nn)

        @block.scalar
        def _(act):
            link = Chain(act, act_chain)
            nn = nv = 0

            def turn_out(g):
                dst, half = ((KT, 0), (KT, 1), (QT, 0), (QT, 1))[g]
                for n in range(NTILE):
                    j = NTILE * g + n
                    r = rows_of(n)
                    act.wait_ge(turned, j + 1)
                    nc.scalar.copy(dst[:, 3 * half:3 * half + 3, n * P:n * P + r],
                                   bank[:, 6 + j % 2, 0:W].rearrange("p (i t) -> p i t", i=3)[:, :, 0:r]).then_inc(turned_out, 1)

            act.wait_ge(zeroed, 1)
            for i, (kind, half) in enumerate(GRP):
                for n in range(NTILE):
                    j = NTILE * i + n
                    r = rows_of(n)
                    act.wait_ge(mm_done, j + 1)
                    if kind == "v":
                        link(nc.scalar.copy(V[0:r, n, half * W:(half + 1) * W], bank[0:r, j % 6, 0:W]))
                        act.sem_inc(raw_ready, 1)
                        act.sem_inc(v_ready, 1)
                    else:
                        m = NTILE * nn + n
                        if n == 0 and nn >= 1:
                            act.wait_ge(rot_ready, nn)
                        if m >= 2:
                            act.wait_ge(ss_ready, m - 1)
                        nc.scalar.activation(sq[0:r, m % 2, :], bank[0:r, j % 6, 0:W], ACT.Square).then_inc(sq_ready, 1)
                        nc.scalar.copy(raw[0:r, n, :], bank[0:r, j % 6, 0:W]).then_inc(raw_ready, 1)
                if kind != "v":
                    act.wait_ge(ss_ready, NTILE * (nn + 1))
                    link(nc.scalar.activation(ss[:, :], ss[:, :], ACT.Ln, scale=1.0 / HS, bias=eps_tile(nc)[:, 0:1]))
                    nc.scalar.activation(ss[:, :], ss[:, :], ACT.Exp, scale=-0.5).then_inc(rs_ready, 1)
                    nn += 1
                if i >= 1 and GRP[i - 1][0] != "v":
                    turn_out(sum(kk != "v" for kk, _ in GRP[:i]) - 1)
            turn_out(3)

        @block.vector
        def _(dve):
            link = Chain(dve, dve_chain)
            nc.vector.memset(raw[:, NT, :], 0.0)
            nc.vector.memset(ss[:, :], 1.0).then_inc(zeroed, 1)
            cos = bcast(const_view(const, "cos").rearrange("p (n d) -> p n d", n=NTILE).unsqueeze(2), [P, NTILE, 6, 32])
            sin = bcast(const_view(const, "sin").rearrange("p (n d) -> p n d", n=NTILE).unsqueeze(2), [P, NTILE, 6, 32])
            x = raw[:, :, :].rearrange("p n (h d) -> p n h d", h=6)
            y = rot[:, :, :].rearrange("p n (h d) -> p n h d", h=6)
            flat = raw[:, :, :].rearrange("p n (h d) -> p (n h) d", h=6)
            for g, i in enumerate(normed):
                kind = GRP[i][0]
                for n in range(NTILE):
                    m = NTILE * g + n
                    r = rows_of(n)
                    dve.wait_ge(sq_ready, m + 1)
                    nc.vector.tensor_reduce(ss[0:r, 6 * n:6 * n + 6], sq[0:r, m % 2, :].rearrange("p (h d) -> p h d", h=6), X,
                                            ALU.add).then_inc(ss_ready, 1)
                dve.wait_ge(rs_ready, g + 1)
                link(nc.vector.tensor_tensor(flat, flat, bcast(ss[:, :].unsqueeze(2), [P, 6 * NTILE, HS]), ALU.mult))
                link(nc.vector.tensor_tensor(flat, flat, bcast(row(rows2, "k_g" if kind == "k" else "q_g").unsqueeze(1),
                                                               [P, 6 * NTILE, HS]), ALU.mult))
                if g >= 1:
                    dve.wait_ge(turned, NTILE * g)
                    dve.wait_ge(k_stored, 16 * NTILE * min(g, 2))
                link(nc.vector.tensor_tensor(y[:, :, :, 0:32], x[:, :, :, 0:32], cos, ALU.mult))
                link(nc.vector.tensor_tensor(y[:, :, :, 32:64], x[:, :, :, 32:64], cos, ALU.mult))
                link(nc.vector.tensor_tensor(x[:, :, :, 0:32], x[:, :, :, 0:32], sin, ALU.mult))
                link(nc.vector.tensor_tensor(x[:, :, :, 32:64], x[:, :, :, 32:64], sin, ALU.mult))
                link(nc.vector.tensor_tensor(y[:, :, :, 0:32], y[:, :, :, 0:32], x[:, :, :, 32:64], ALU.subtract))
                nc.vector.tensor_tensor(y[:, :, :, 32:64], y[:, :, :, 32:64], x[:, :, :, 0:32], ALU.add).then_inc(rot_ready, 1)
                dve.wait_ge(rot_ready, g + 1)


def lambda_row(nc, rows2, lam, subs):
    with Stage(nc, "lam") as st:
        prod = st.sb("prod", [P, 2, HS])
        two = st.sb("two", [P, 2])
        summed, exp_ready, chain = st.sems("summed exp_ready chain")
        block = st.block()
        lv = row(rows2, "lam").rearrange("p (a b d) -> p a b d", a=2, b=2)

        @block.vector
        def _(dve):
            link = Chain(dve, chain)
            link(nc.vector.tensor_tensor(prod[:, :, :], lv[:, :, 0, :], lv[:, :, 1, :], ALU.mult))
            nc.vector.tensor_reduce(two[:, :], prod[:, :, :], X, ALU.add).then_inc(summed, 1)
            dve.wait_ge(exp_ready, 1)
            link(nc.vector.tensor_tensor(lam[:, :], two[:, 1:2], two[:, 0:1], ALU.subtract))
            link(nc.vector.tensor_scalar(lam[:, :], lam[:, :], -LAM_INIT, None, ALU.add))
            link(nc.vector.tensor_scalar(subs[:, :], row(rows2, "subln"), 1.0 - LAM_INIT, None, ALU.mult))

        @block.scalar
        def _(act):
            act.wait_ge(summed, 1)
            nc.scalar.activation(two[:, :], two[:, :], ACT.Exp).then_inc(exp_ready, 1)


def prompt_attention(nc, KT, QT, V, lam, causal, ident, wide, bank, scratch):
    SC = HS ** -0.5
    flat = scratch[:, :, :].rearrange("p k t -> p (k t)")
    pr = flat[:, 0:4096].rearrange("p (r c t) -> p r c t", r=2, c=2)
    wT = flat[:, 4096:6144].rearrange("p (r j q) -> p r j q", r=2, j=NT)
    N = DH * NT
    with Stage(nc, "attn") as st:
        mx = st.sb("mx", [P, 2, 2])
        ls = st.sb("ls", [P, 2, 2])
        inv = st.sb("inv", [P, 4, 2])
        ratio = st.sb("ratio", [P, 1])
        qc = st.sb("qc", [P, 3, 2, P])
        q_alone, pool_chain, s_mm, mx_ready, exp_ready, w_ready, w_turned, wT_ready, o_mm, o_out, dve_chain = st.sems(
            "q_alone pool_chain s_mm mx_ready exp_ready w_ready w_turned wT_ready o_mm o_out dve_chain")
        block = st.block()

        def score_banks(i, c):
            at = c * 1024 + (i % 2 * 512 if i < 4 else 0)
            return wide[:, at:at + (i + 1) * P]

        @block.gpsimd
        def _(pool):
            Chain(pool, pool_chain)(nc.gpsimd.memset(qc[:, :, :, :], 0.0))
            for k in range(N):
                h, i = divmod(k, NT)
                if k >= 3:
                    pool.wait_ge(s_mm, 2 * (k - 2))
                for c in range(2):
                    d = slice(c * HS, (c + 1) * HS)
                    nc.gpsimd.tensor_copy(qc[d, k % 3, c, :], QT[d, h, i * P:(i + 1) * P]).then_inc(q_alone, 1)

        @block.tensor
        def _(pe):
            def scores(k):
                h, i = divmod(k, NT)
                L = (i + 1) * P
                pe.wait_ge(q_alone, 2 * k + 2)
                before = k if (i == 0 or i >= 4) else k - 1
                for c in range(2):
                    if before >= 1:
                        pe.wait_ge(exp_ready, 2 * before - 1 + c)
                    s = score_banks(i, c)
                    for a in range(0, L, 512):
                        b = min(a + 512, L)
                        mm = pe.matmul(s[:, a:b], qc[:, k % 3, c, :], KT[:, h, a:b], start=True, stop=True)
                    mm.then_inc(s_mm, 1)

            def values(k):
                h, i = divmod(k, NT)
                pe.wait_ge(wT_ready, k + 1)
                if k >= 2:
                    pe.wait_ge(o_out, k - 1)
                for j in range(i + 1):
                    mm = pe.matmul(bank[:, 6 + k % 2, 0:P], wT[:, k % 2, j, :], V[:, j, h * P:(h + 1) * P],
                                   start=(j == 0), stop=(j == i))
                mm.then_inc(o_mm, 1)

            scores(0)
            for k in range(N):
                if k + 1 < N:
                    scores(k + 1)
                pe.wait_ge(w_ready, k + 1)
                if k >= 1:
                    pe.wait_ge(wT_ready, k)
                for j in range(k % NT + 1):
                    mm = pe.transpose(bank[:, 4 + j // 4, (j % 4) * P:(j % 4 + 1) * P], pr[:, k % 2, 0, j * P:(j + 1) * P], ident[:, :])
                mm.then_inc(w_turned, 1)
                if k >= 1:
                    values(k - 1)
            values(N - 1)

        @block.scalar
        def _(act):
            def turned_out(k):
                L = (k % NT + 1) * P
                act.wait_ge(w_turned, k + 1)
                nc.scalar.copy(wT[:, k % 2, :, :].rearrange("p j q -> p (j q)")[:, 0:L], wide[:, 2048:2048 + L]).then_inc(wT_ready, 1)

            def out(k):
                h, i = divmod(k, NT)
                act.wait_ge(o_mm, k + 1)
                nc.scalar.activation(QT[:, h, i * P:(i + 1) * P], bank[:, 6 + k % 2, 0:P], ACT.Copy,
                                     scale=inv[:, k % 4, 0:1]).then_inc(o_out, 1)

            for k in range(N):
                i = k % NT
                L = (i + 1) * P
                for c in range(2):
                    act.wait_ge(mx_ready, 2 * k + c + 1)
                    nc.scalar.activation(pr[:, k % 2, c, 0:L], score_banks(i, c), ACT.Exp, scale=SC, bias=mx[:, k % 2, c:c + 1],
                                         accum_out=ls[:, k % 2, c:c + 1]).then_inc(exp_ready, 1)
                if k >= 1:
                    turned_out(k - 1)
                if k >= 2:
                    out(k - 2)
            turned_out(N - 1)
            out(N - 2)
            out(N - 1)

        @block.vector
        def _(dve):
            link = Chain(dve, dve_chain)

            def maxima(k, c):
                i = k % NT
                s = score_banks(i, c)
                dve.wait_ge(s_mm, 2 * k + c + 1)
                diag = s[:, i * P:(i + 1) * P]
                link(nc.vector.tensor_tensor(diag, diag, causal, ALU.add))
                link(nc.vector.tensor_reduce(mx[:, k % 2, c:c + 1], s, X, ALU.max))
                nc.vector.tensor_scalar(mx[:, k % 2, c:c + 1], mx[:, k % 2, c:c + 1], -SC, None, ALU.mult).then_inc(mx_ready, 1)

            def weights(k):
                L = (k % NT + 1) * P
                dve.wait_ge(exp_ready, 2 * k + 2)
                link(nc.vector.reciprocal(inv[:, k % 4, :], ls[:, k % 2, :]))
                link(nc.vector.scalar_tensor_tensor(out=ratio[:, :], in0=ls[:, k % 2, 0:1], scalar=inv[:, k % 4, 1:2], in1=lam[:, :],
                                                    op0=ALU.mult, op1=ALU.mult))
                p0, p1 = pr[:, k % 2, 0, 0:L], pr[:, k % 2, 1, 0:L]
                nc.vector.scalar_tensor_tensor(out=p0, in0=p1, scalar=ratio[:, 0:1], in1=p0, op0=ALU.mult, op1=ALU.add).then_inc(w_ready, 1)

            maxima(0, 0)
            maxima(0, 1)
            for k in range(N):
                if k + 1 < N:
                    maxima(k + 1, 0)
                weights(k)
                if k + 1 < N:
                    maxima(k + 1, 1)


def prompt_outputs(nc, QT, subs, gates, ident, bank):
    with Stage(nc, "attno") as st:
        sq = st.sb("sq", [P, 2, NT, P])
        ss = st.sb("ss", [P, DH * NT])
        sq_ready, ss_ready, rs_ready, on_ready, turned, y_ready, dve_chain, act_chain = st.sems(
            "sq_ready ss_ready rs_ready on_ready turned y_ready dve_chain act_chain")
        block = st.block()

        def o(h):
            return QT[:, h, 0:SEQ].rearrange("p (n e) -> p n e", n=NT)

        @block.scalar
        def _(act):
            link = Chain(act, act_chain)
            for h in range(DH):
                if h >= 2:
                    act.wait_ge(ss_ready, h - 1)
                nc.scalar.activation(sq[:, h % 2, :, :], o(h), ACT.Square).then_inc(sq_ready, 1)
            act.wait_ge(ss_ready, DH)
            link(nc.scalar.activation(ss[:, :], ss[:, :], ACT.Ln, scale=1.0 / P, bias=eps_tile(nc)[:, 0:1]))
            nc.scalar.activation(ss[:, :], ss[:, :], ACT.Exp, scale=-0.5).then_inc(rs_ready, 1)

        @block.vector
        def _(dve):
            link = Chain(dve, dve_chain)

            def gated(j):
                h, half = divmod(j, 2)
                dve.wait_ge(turned, j + 1)
                y = gates[:, h, half * 512:(half + 1) * 512]
                nc.vector.scalar_tensor_tensor(out=y, in0=bank[:, j % 8, :], scalar=0.5, in1=y, op0=ALU.mult,
                                               op1=ALU.mult).then_inc(y_ready, 1)

            for h in range(DH):
                dve.wait_ge(sq_ready, h + 1)
                nc.vector.tensor_reduce(ss[:, h * NT:(h + 1) * NT], sq[:, h % 2, :, :], X, ALU.add).then_inc(ss_ready, 1)
            dve.wait_ge(rs_ready, 1)
            for h in range(DH):
                link(nc.vector.tensor_tensor(o(h), o(h), bcast(ss[:, h * NT:(h + 1) * NT].unsqueeze(2), [P, NT, P]), ALU.mult))
                nc.vector.tensor_tensor(o(h), o(h), bcast(subs[:, :].unsqueeze(1), [P, NT, P]), ALU.mult).then_inc(on_ready, 1)
                if h >= 1:
                    gated(2 * h - 2)
                    gated(2 * h - 1)
            gated(2 * DH - 2)
            gated(2 * DH - 1)

        @block.tensor
        def _(pe):
            for j in range(2 * DH):
                h, half = divmod(j, 2)
                pe.wait_ge(on_ready, h + 1)
                if j >= 8:
                    pe.wait_ge(y_ready, j - 7)
                for i in range(4):
                    n = 4 * half + i
                    mm = pe.transpose(bank[:, j % 8, i * P:(i + 1) * P], QT[:, h, n * P:(n + 1) * P], ident[:, :])
                mm.then_inc(turned, 1)


def sample_attention(nc, pages_d, cache_k, cache_v, KT, QT, V, lam, subs, gates, const, ident, bank, wide, scratch):
    SC = HS ** -0.5
    R = DH * 2 * TS
    W = DH * TS
    H3 = 3
    STEP = R + 2 * TS
    flat = scratch[:, :, :].rearrange("p k t -> p (k t)")
    KR, VR = 6, 10
    NPG = B * PAGES
    isc, join, own8 = (const_view(const, x) for x in ("isc", "join", "own8"))
    with Stage(nc, "samp") as st:
        kp = flat[:, 0:KR * 768].rearrange("p (r c) -> p r c", r=KR)
        at = KR * 768
        kT = flat[:, at:at + 4 * 384].rearrange("p (r h c) -> p r h c", r=2, h=2)
        probs = flat[0:R, at + 1536:at + 1536 + PAGES * P]
        squares = flat[0:NS, 0:768]
        normed = flat[0:NS, 768:1536]
        vp = st.sb("vp", [P, VR, 768])
        weights = st.sb("weights", [P, PAGES + 1, DH, NS])
        queries = flat[:, at + 2560:at + 2560 + 2 * DH * STEP].rearrange("p (r c) -> p r c", r=2)
        new_probs = st.sb("new_probs", [R, NS])
        joined = st.sb("joined", [R, W])
        mx = st.sb("mx", [R, 2])
        ls = st.sb("ls", [R, 2])
        coef = st.sb("coef", [R, 1])
        ss = st.sb("ss", [NS, DH])
        pages = st.sb("pages", [1, NPG], I32)
        k_loaded = [st.sem(f"k_loaded{i}") for i in range(KR)]
        v_loaded = [st.sem(f"v_loaded{i}") for i in range(VR)]
        (pages_loaded, q_ready, turned, act_out, dve_out, k_used, s_mm, mx_ready, exp_ready, join_ready, w_mm, w_ready, o_mm,
         sq_ready, ss_ready, rs_ready, o_ready, o_turned, dve_chain, act_chain) = st.sems(
            "pages_loaded q_ready turned act_out dve_out k_used s_mm mx_ready exp_ready join_ready w_mm w_ready o_mm "
            "sq_ready ss_ready rs_ready o_ready o_turned dve_chain act_chain")
        block = st.block()
        scores_of = wide[0:R, 0:PAGES * P]
        new_of = bank[0:R, 6, PAGES * W + W:PAGES * W + W + TS]
        w_of = bank[:, 6, 0:(PAGES + 1) * W].rearrange("p (g h t) -> p g h t", g=PAGES + 1, h=DH)
        out_of = wide[0:NS, 2 * 512:2 * 512 + 768]

        @block.sync
        def _(sp):
            sp.dma_start(pages[:, :], pages_d).then_inc(pages_loaded, 16)
            sp.wait_ge(pages_loaded, 16)
            for g in range(NPG):
                page = sp.value_load(pages[0:1, g:g + 1], min_val=0, max_val=cache_k.shape[0] - 1)
                if g >= KR:
                    sp.wait_ge(turned, 2 * (g - KR + 1))
                sp.dma_start(kp[:, g % KR, :], cache_k[bass.ds(page, 1), :, :].rearrange("a p c -> p (a c)")).then_inc(k_loaded[g % KR], 16)

        @block.gpsimd
        def _(pool):
            pool.wait_ge(pages_loaded, 16)
            for g in range(NPG):
                page = pool.value_load(pages[0:1, g:g + 1], min_val=0, max_val=cache_k.shape[0] - 1)
                if g >= VR:
                    pool.wait_ge(o_mm, (g - VR) // PAGES + 1)
                pool.dma_start(vp[:, g % VR, :], cache_v[bass.ds(page, 1), :, :].rearrange("a p c -> p (a c)")).then_inc(v_loaded[g % VR], 16)

        @block.tensor
        def _(pe):
            def turn(j):
                g, half = divmod(j, 2)
                if half == 0:
                    pe.wait_ge(k_loaded[g % KR], 16 * (g // KR + 1))
                if g >= 1:
                    pe.wait_ge(dve_out if half else act_out, g)
                for i in range(H3):
                    mm = pe.transpose(bank[:, 4 + half, i * P:(i + 1) * P], kp[:, g % KR, (H3 * half + i) * P:(H3 * half + i + 1) * P],
                                      ident[:, :])
                mm.then_inc(turned, 1)

            def query_of(b, h):
                return queries[:, b % 2, h * R:(h + 1) * R]

            def scores(g):
                b, pg = divmod(g, PAGES)
                if pg == 0:
                    pe.wait_ge(q_ready, b + 1)
                for half in range(2):
                    pe.wait_ge(dve_out if half else act_out, g + 1)
                    for i in range(H3):
                        h = H3 * half + i
                        mm = pe.matmul(scores_of[:, pg * P:(pg + 1) * P], query_of(b, h), kT[:, g % 2, half, i * P:(i + 1) * P],
                                       start=(h == 0), stop=(h == DH - 1))
                mm.then_inc(k_used, 1)

            def new_scores(b):
                if b >= 1:
                    pe.wait_ge(w_ready, b)
                for h in range(DH):
                    mm = pe.matmul(new_of, query_of(b, h), KT[:, h, SEQ + b * TS:SEQ + (b + 1) * TS], start=(h == 0), stop=(h == DH - 1))
                mm.then_inc(s_mm, 1)

            def turn_weights(b):
                pe.wait_ge(join_ready, b + 1)
                for pg in range(PAGES):
                    pe.matmul(bank[:, 6, pg * W:(pg + 1) * W], probs[:, pg * P:(pg + 1) * P], joined[:, :], start=True, stop=True)
                pe.matmul(bank[0:NS, 6, PAGES * W:(PAGES + 1) * W], new_probs[:, :], joined[:, :], start=True, stop=True).then_inc(w_mm, 1)

            def values(b):
                pe.wait_ge(w_ready, b + 1)
                for pg in range(PAGES):
                    g = b * PAGES + pg
                    pe.wait_ge(v_loaded[g % VR], 16 * (g // VR + 1))
                for h in range(DH):
                    out = out_of[:, h * P:(h + 1) * P]
                    for pg in range(PAGES):
                        pe.matmul(out, weights[:, pg, h, :], vp[:, (b * PAGES + pg) % VR, h * P:(h + 1) * P],
                                  start=False, stop=False)
                    mm = pe.matmul(out, weights[0:NS, PAGES, h, :], V[0:NS, NT, h * P:(h + 1) * P], start=False,
                                   stop=(b == B - 1 and h in (3, DH - 1)))
                mm.then_inc(o_mm, 1)

            pe.wait_ge(q_ready, 1)
            for a, n in ((0, 512), (512, 256)):
                pe.matmul(out_of[:, a:a + n], weights[:, 0, 0, :], KT[:, 0, 0:n], start=True, stop=False)

            for b in range(B):
                for pg in range(PAGES):
                    g = b * PAGES + pg
                    turn(2 * g)
                    turn(2 * g + 1)
                    if pg:
                        scores(g - 1)
                scores(b * PAGES + PAGES - 1)
                new_scores(b)
                if b >= 1:
                    values(b - 1)
                turn_weights(b)
            values(B - 1)
            pe.wait_ge(o_ready, 1)
            for h in range(DH):
                mm = pe.transpose(bank[:, 4, h * NS:(h + 1) * NS], normed[:, h * P:(h + 1) * P], ident[0:NS, 0:NS])
            mm.then_inc(o_turned, 1)

        @block.scalar
        def _(act):
            link = Chain(act, act_chain)
            for b in range(B):
                for pg in range(PAGES):
                    g = b * PAGES + pg
                    act.wait_ge(turned, 2 * g + 1)
                    if g >= 2:
                        act.wait_ge(k_used, g - 1)
                    nc.scalar.copy(kT[:, g % 2, 0, :], bank[:, 4, 0:H3 * P]).then_inc(act_out, 1)
                act.wait_ge(mx_ready, b + 1)
                nc.scalar.activation(probs, scores_of, ACT.Exp, scale=SC, bias=mx[:, 0:1], accum_out=ls[:, 0:1])
                nc.scalar.activation(new_probs[:, b * TS:(b + 1) * TS], new_of, ACT.Exp, scale=SC, bias=mx[:, 0:1],
                                     accum_out=ls[:, 1:2]).then_inc(exp_ready, 1)
            act.wait_ge(o_mm, B)
            nc.scalar.activation(squares, out_of, ACT.Square).then_inc(sq_ready, 1)
            act.wait_ge(ss_ready, 1)
            link(nc.scalar.activation(ss[:, :], ss[:, :], ACT.Ln, scale=1.0 / P, bias=eps_tile(nc)[0:NS, 0:1]))
            nc.scalar.activation(ss[:, :], ss[:, :], ACT.Exp, scale=-0.5).then_inc(rs_ready, 1)

        @block.vector
        def _(dve):
            link = Chain(dve, dve_chain)
            link(nc.vector.memset(queries[:, :, :], 0.0))
            link(nc.vector.memset(weights[:, :, :, :], 0.0))
            link(nc.vector.memset(new_probs[:, :], 0.0))
            link(nc.vector.scalar_tensor_tensor(out=coef[:, :], in0=isc[0:R, 1:2], scalar=lam[0:R, 0:1], in1=isc[0:R, 0:1],
                                                op0=ALU.mult, op1=ALU.add))

            def fill_queries(b):
                for c in range(2):
                    d = slice(c * HS, (c + 1) * HS)
                    link(nc.vector.tensor_copy(queries[d, b % 2, :].rearrange("p (h x) -> p h x", h=DH)[:, :, c * TS:(c + 1) * TS],
                                               QT[d, :, SEQ + b * TS:SEQ + (b + 1) * TS]))
                dve.sem_inc(q_ready, 1)

            fill_queries(0)
            for b in range(B):
                own = slice(b * TS, (b + 1) * TS)
                before = slice((b - 1) * TS, b * TS)
                for pg in range(PAGES):
                    g = b * PAGES + pg
                    dve.wait_ge(turned, 2 * g + 2)
                    if g >= 2:
                        dve.wait_ge(k_used, g - 1)
                    nc.vector.tensor_copy(kT[:, g % 2, 1, :], bank[:, 5, 0:H3 * P]).then_inc(dve_out, 1)
                if b + 1 < B:
                    fill_queries(b + 1)
                dve.wait_ge(s_mm, b + 1)
                link(nc.vector.tensor_tensor(new_of, new_of, own8[0:R, :], ALU.add))
                nc.vector.tensor_reduce(mx[:, 0:1], scores_of, X, ALU.max)
                link(nc.vector.tensor_reduce(mx[:, 1:2], new_of, X, ALU.max))
                if b >= 1:
                    link(nc.vector.memset(new_probs[:, before], 0.0))
                link(nc.vector.tensor_tensor(mx[:, 0:1], mx[:, 0:1], mx[:, 1:2], ALU.max))
                nc.vector.tensor_scalar(mx[:, 0:1], mx[:, 0:1], -SC, None, ALU.mult).then_inc(mx_ready, 1)
                dve.wait_ge(exp_ready, b + 1)
                link(nc.vector.tensor_tensor(ls[:, 0:1], ls[:, 0:1], ls[:, 1:2], ALU.add))
                link(nc.vector.reciprocal(ls[:, 0:1], ls[:, 0:1]))
                link(nc.vector.tensor_tensor(ls[:, 0:1], ls[:, 0:1], coef[:, :], ALU.mult))
                nc.vector.tensor_scalar(joined[:, :], join[0:R, :], ls[:, 0:1], None, ALU.mult).then_inc(join_ready, 1)
                if b >= 1:
                    dve.wait_ge(o_mm, b)
                    nc.vector.memset(weights[:, :, :, before], 0.0)
                dve.wait_ge(w_mm, b + 1)
                link(nc.vector.tensor_copy(weights[:, 0:PAGES, :, own], w_of[:, 0:PAGES]))
                nc.vector.tensor_copy(weights[0:NS, PAGES, :, own], w_of[0:NS, PAGES]).then_inc(w_ready, 1)
            dve.wait_ge(sq_ready, 1)
            nc.vector.tensor_reduce(ss[:, :], squares.rearrange("p (h e) -> p h e", h=DH), X, ALU.add).then_inc(ss_ready, 1)
            dve.wait_ge(rs_ready, 1)
            o = normed.rearrange("p (h e) -> p h e", h=DH)
            link(nc.vector.tensor_tensor(o, out_of.rearrange("p (h e) -> p h e", h=DH), bcast(ss[:, :].unsqueeze(2), [NS, DH, P]), ALU.mult))
            nc.vector.tensor_tensor(o, o, bcast(subs[0:NS, :].unsqueeze(1), [NS, DH, P]), ALU.mult).then_inc(o_ready, 1)
            dve.wait_ge(o_turned, 1)
            y = gates[:, 0:DH, SEQ:TT]
            link(nc.vector.scalar_tensor_tensor(out=y, in0=bank[:, 4, 0:DH * NS].rearrange("p (h t) -> p h t", h=DH), scalar=0.5,
                                                in1=y, op0=ALU.mult, op1=ALU.mult))


def build(nc, ins, outs):
    with ExitStack() as ctx:
        def sb(name, shape, dt=F32):
            return ctx.enter_context(nc.sbuf_tensor(name, shape, dt))

        psum = ctx.enter_context(nc.psum_tensor("psum", [P, 4096], F32))
        wide = psum[:, :]
        bank = psum[:, :].rearrange("p (b c) -> p b c", b=8)
        for name in STORES:
            STORE_SIGNALS[name] = nc.alloc_semaphore(name)
        base = sb("base", [P, _CONST[0].shape[1]])
        vecs = sb("vecs", [P, NVEC])
        eps = sb("eps", [P, 2])
        _EPS["tile"] = eps
        ident = const_view([base], "ident")
        (y_p, y_s, st_p, sh_p, k_p, v_p, mk_p, mv_p, st_s, sh_s, k_s, v_s) = outs
        i = ins
        load_tensors(nc, "cst", [(base[:, :], i["const0"]), (vecs[:, :], i["vecs"])], [(eps[:, 0:1], EPS), (eps[:, 1:2], LNX_EPS)])
        y_d = nc.dram_tensor("gated", (P, KC, TT), F32).ap()
        xT = sb("xT", [P, KC, TX])
        with ExitStack() as c2:
            lora = c2.enter_context(nc.sbuf_tensor("lora", [P, TT], F32))
            up = c2.enter_context(nc.sbuf_tensor("up", [P, 2, 6 * P], F32))
            omu = c2.enter_context(nc.sbuf_tensor("omu", [P, 19], F32))
            masks = c2.enter_context(nc.sbuf_tensor("masks", [P, _CONST[1].shape[1]], F32))
            rows = c2.enter_context(nc.sbuf_tensor("rows", [P, NROW], F32))
            const = [base, masks]
            with nc.sbuf_tensor("x_rows", [P, NTILE, D], F32) as x_sb:
                norm_and_turn(nc, "norm0", x_sb, xT, bank, ident, i["norm_g0"], i["shift"], (sh_p, sh_s), (i["x_p"], i["x_s"]),
                              ahead=[(masks[:, :], i["const1"]), (rows[:, :], i["rows"].partition_broadcast(P))])
            lora_inputs(nc, i["w_in"], i["w_up"], i["a_up"], vecs, omu, xT, wide, lora, up)
            rwkv_pairs(nc, i["w_in"], i["state"], st_p, st_s, const, vecs, rows, omu, xT, wide, bank, lora, up, y_d)
        late = sb("late", [P, _CONST[2].shape[1]])
        const = [base, None, late]
        rows2 = sb("rows2", [P, NROW2])
        ones = sb("ones", [P, P])
        mkT = sb("mkT", [P, 2, 2, MEMT])
        mv = sb("mv", [P, 2, 2, MEMT])
        load_tensors(nc, "cst2", [(late[:, :], i["const2"]), (rows2[:, :], i["rows2"].partition_broadcast(P))], [(ones[:, :], 1.0)])
        memory_keys(nc, i["mem"], i["mem_w_kv"], vecs, rows2, ident, bank, mkT, mv, mk_p, mv_p)
        h_d = nc.dram_tensor("residual", (TT, D), F32).ap()
        h_tiles = (h_d[0:SEQ, :], h_d[SEQ:TT, :])
        with ExitStack() as c1:
            yT = c1.enter_context(nc.sbuf_tensor("yT0", [P, KC, TT], F32))
            with nc.sbuf_tensor("mqT0", [P, 2, TT], F32) as mqT:
                gates_and_queries(nc, "gq0", i["w_in"], [19, 20, 27, 28], xT, None, vecs, vec(vecs, "mq0"), const, wide,
                                  mqT, yT[:, 6:8, :])
                memory_attention(nc, "mem0", 0, mqT, mkT, mv, i["cmk"], i["cmv"], yT[:, 6:8, :], const, ones, bank,
                                 ahead=[(weights_in(xT)[:, k, :], i["w_out"][0][:, k * D:(k + 1) * D]) for k in range(KC)] +
                                 [(yT[:, k, :], y_d[:, k, :]) for k in range(6)])
            with nc.sbuf_tensor("h0", [P, NTILE, D], F32) as h:
                out_project(nc, "out0", None, yT, h, bank, xT, (i["x_p"], i["x_s"]), h_tiles)
                norm_and_turn(nc, "norm1", h, xT, bank, ident, None)
        KT = sb("KT", [P, DH, TT])
        QT = sb("QT", [P, DH, TT])
        V = sb("V", [P, NTILE, 768])
        keys_values_queries(nc, i["kv_w"], i["b_q"], vecs, rows2, const, ident, xT, bank, KT, QT, V, (k_p, k_s), (v_p, v_s))
        yT = sb("yT1", [P, KC, TT])
        lam = sb("lam", [P, 1])
        subs = sb("subs", [P, P])
        lambda_row(nc, rows2, lam, subs)
        with nc.sbuf_tensor("mqT1", [P, 2, TT], F32) as mqT:
            gates_and_queries(nc, "gq1", i["b_in"], list(range(10)), xT, vec(vecs, "bg"), vecs, vec(vecs, "mq1"), const, wide,
                              mqT, yT[:, :, :])
            memory_attention(nc, "mem1", 1, mqT, mkT, mv, i["cmk"], i["cmv"], yT[:, 6:8, :], const, ones, bank, xT)
        prompt_attention(nc, KT, QT, V, lam, const_view(const, "causal"), ident, wide, bank, xT)
        sample_attention(nc, i["pages"], i["cache_k"], i["cache_v"], KT, QT, V, lam, subs, yT, const, ident, bank, wide, xT)
        prompt_outputs(nc, QT, subs, yT, ident, bank)
        out_project(nc, "out1", i["w_out"][1], yT, None, bank, xT, h_tiles, (y_p, y_s))


_OUTS = [(SEQ, D), (NS, D), (HEADS, HS, HS), (1, D), (SEQ, 768), (SEQ, 768), (2, MEMT, 256), (2, MEMT, 256),
         (B, HEADS, HS, HS), (B, D), (NS, 768), (NS, 768)]
_SHAPES = [(1, SEQ, D), (B, TS, D), (1, 1, HEADS, HS, HS), (1, 1, D), (1, SEQ, 6, 2, 64), (1, SEQ, 6, 128),
           (2, 1, MEMT, 4, 64), (2, 1, MEMT, 4, 64), (1, B, HEADS, HS, HS), (1, B, D), (B, TS, 6, 2, 64), (B, TS, 6, 128)]


def _chunks(w, width):
    k, c = w.shape
    return np.ascontiguousarray(w.reshape(KC, P, c // width, width).transpose(2, 1, 0, 3)).reshape(c // width, P, KC * width)


def _layout(a):
    f = {k: np.asarray(v) for k, v in a.items()}

    def cols(v):
        return v.reshape(-1, P).T

    twice = lambda v: np.concatenate([v, v])
    vecs = np.concatenate([
        cols(f["a_mu_first"]), cols(f["a_w0"][0]), cols(f["a_a0"][0]), cols(f["a_k_k"][0]), cols(f["a_k_a"][0]),
        cols(f["a_r_k"][0]), cols(twice(f["mem_q_g"][0])), cols(twice(f["mem_q_g"][1])), cols(f["mem_norm_g"][0]),
        cols(f["mem_norm_g"][1]), cols(f["kv_norm_g"]), cols(f["norm_g"][1]), cols(f["b_subln_g"][0])], 1)
    rows = np.concatenate([f["a_lnx_g"][0], f["a_lnx_b"][0], f["kv_k_g"], f["b_q_g"][0], f["b_subln_g"][0],
                           f["b_lam"][0].reshape(-1), f["mem_k_g"][0], f["mem_k_g"][1]])
    b_in = f["b_w_in"][0]
    return {
        "const0": _CONST[0], "const1": _CONST[1], "const2": _CONST[2], "vecs": vecs, "rows": rows[:NROW], "rows2": rows[NROW:], "norm_g0": f["norm_g"][0],
        "x_p": f["x_prompt"][0], "x_s": f["x_sample"].reshape(NS, D), "mem": f["mem_prompt"][0],
        "shift": f["state_shift"][0], "state": f["state_wkv"][0],
        "w_in": _chunks(f["a_w_in_first"], P), "w_up": f["a_w_up"][0], "a_up": f["a_a_up"][0],
        "mem_w_kv": np.concatenate([_chunks(f["mem_w_kv"][layer], 512) for layer in range(2)]),
        "w_out": np.concatenate([_chunks(f["w_out"][layer], D) for layer in range(2)]),
        "kv_w": _chunks(f["kv_w"], 384), "b_q": _chunks(b_in[:, 0:768], 384), "b_in": _chunks(b_in[:, 768:], P),
        "cache_k": f["cache_k"].reshape(-1, P, 768), "cache_v": f["cache_v"].reshape(-1, P, 768),
        "cmk": f["cache_mem_k"].reshape(2, B, MEMT, 256), "cmv": f["cache_mem_v"].reshape(2, B, MEMT, 256),
        "pages": f["page_table"].reshape(1, -1),
    }


def kernel(**inputs):
    import concourse.bacc as _bacc
    from concourse.bass_utils import run_bass_kernel_spmd as _run

    nc = _bacc.Bacc("TRN2", target_bir_lowering=False, num_devices=1)
    arrays, ins = {}, {}
    for name, a in _layout(inputs).items():
        a = np.ascontiguousarray(a)
        arrays[f"in_{name}"] = a
        ins[name] = nc.dram_tensor(f"in_{name}", a.shape, mybir.dt.from_np(a.dtype), kind="ExternalInput").ap()
    outs = [nc.dram_tensor(f"out_{n}", shape, F32, kind="ExternalOutput").ap() for n, shape in enumerate(_OUTS)]
    build(nc, ins, outs)
    r = _run(nc, [arrays], core_ids=[0])
    return tuple(np.asarray(r.results[0][f"out_{n}"]).reshape(shape) for n, shape in enumerate(_SHAPES))
```
